# Optimizing a Trainium2 kernel written in Bass

```python
import jax
import jax.numpy as jnp
from jax import lax
import numpy as np
import math
import jax, jax.numpy as jnp

D_MODEL = 1024
BATCH = 1
SEQ = 1024
DEPTH = 1

HEAD_DIM = 64
MIX_WIDTH = D_MODEL
A_WIDTH = D_MODEL // 4
A_HEADS = A_WIDTH // HEAD_DIM
A_DK = HEAD_DIM
A_DV = HEAD_DIM
B_WIDTH = D_MODEL // 2
B_BLOCKS = B_WIDTH // HEAD_DIM
B_CONV = 4
LRU_C = 8.0
C_WIDTH = MIX_WIDTH - A_WIDTH - B_WIDTH
C_HEADS = C_WIDTH // HEAD_DIM
C_DV = HEAD_DIM
C_DK = C_DV // 2
C_GATE_RANK = 16
C_GATE_NORM = 16.0
CHUNK = 64
D_FF = 2688
FFN_CONV = 3
EPS = 1e-6
F_FLOOR = 1e-20

IN_SIZES = (A_HEADS * A_DK, A_HEADS * A_DK, A_HEADS * A_DV, A_HEADS * A_DV,
            B_WIDTH, B_WIDTH,
            C_HEADS * C_DK, C_HEADS * C_DK, C_WIDTH, C_WIDTH, C_GATE_RANK)
IN_SPLITS = tuple(int(s) for s in np.cumsum(IN_SIZES)[:-1])
IN_COLS = int(sum(IN_SIZES))


def rmsnorm(x, w):
    xf = x.astype(jnp.float32)
    y = xf * lax.rsqrt(jnp.mean(xf * xf, axis=-1, keepdims=True) + EPS)
    return (y * w.astype(jnp.float32)).astype(x.dtype)

def head_rmsnorm(o, w):
    b, t, h, d = o.shape
    return rmsnorm(o, w.reshape(h, d)).reshape(b, t, h * d)

def causal_dwconv(x, w, bias):
    k_w = w.shape[0]
    t = x.shape[1]
    xp = jnp.pad(x, ((0, 0), (k_w - 1, 0), (0, 0)))
    y = bias + xp[:, k_w - 1:k_w - 1 + t] * w[k_w - 1]
    for k in range(k_w - 1):
        y = y + xp[:, k:k + t] * w[k]
    return y

def chunked_gated_linear_attention(q, k, v, log_f):
    b_sz, t, h, dk = q.shape
    dv = v.shape[-1]
    n = t // CHUNK

    def to_chunks(a):
        return a.astype(jnp.float32).reshape(b_sz, n, CHUNK, h, a.shape[-1]).transpose(1, 0, 3, 2, 4)

    qc, kc, vc, gc = to_chunks(q), to_chunks(k), to_chunks(v), to_chunks(log_f)
    causal = jnp.tril(jnp.ones((CHUNK, CHUNK), dtype=bool))[:, :, None]

    def step(state, inp):
        qi, ki, vi, gi = inp
        cum = jnp.cumsum(gi, axis=2)
        diff = cum[:, :, :, None, :] - cum[:, :, None, :, :]
        decay = jnp.where(causal, jnp.exp(jnp.where(causal, diff, 0.0)), 0.0)
        scores = jnp.einsum('bhid,bhijd,bhjd->bhij', qi, decay, ki)
        last = cum[:, :, -1:, :]
        out = (jnp.einsum('bhij,bhjv->bhiv', scores, vi)
               + jnp.einsum('bhid,bhdv->bhiv', qi * jnp.exp(cum), state))
        state = (jnp.exp(last[:, :, 0, :, None]) * state
                 + jnp.einsum('bhjd,bhjv->bhdv', ki * jnp.exp(last - cum), vi))
        return state, out

    s0 = jnp.zeros((b_sz, h, dk, dv), jnp.float32)
    _, o = lax.scan(step, s0, (qc, kc, vc, gc))
    return o.transpose(1, 0, 3, 2, 4).reshape(b_sz, t, h, dv).astype(q.dtype)

def hgrn2_mixer(q, f_logit, i, g, lower_bound, norm_w):
    b_sz, t, _ = q.shape
    lb = lower_bound.astype(jnp.float32)
    z = f_logit.astype(jnp.float32)
    f = lb + (1.0 - lb) * jax.nn.sigmoid(z)
    log_f = jnp.log(jnp.maximum(f, F_FLOOR))
    key = (1.0 - lb) * jax.nn.sigmoid(-z)
    heads = lambda a, d: a.reshape(b_sz, t, A_HEADS, d)
    o = chunked_gated_linear_attention(heads(q, A_DK), heads(key, A_DK), heads(i, A_DV), heads(log_f, A_DK))
    return head_rmsnorm(o, norm_w) * jax.nn.silu(g)

def rglru_mixer(xb, gb, conv_w, conv_b, w_a, b_a, w_x, b_x, lam):
    b_sz, t, _ = xb.shape
    xc = causal_dwconv(xb, conv_w, conv_b)
    xh = xc.reshape(b_sz, t, B_BLOCKS, HEAD_DIM)
    r = jax.nn.sigmoid(jnp.einsum('bthi,hij->bthj', xh, w_a).reshape(b_sz, t, B_WIDTH) + b_a)
    gi = jax.nn.sigmoid(jnp.einsum('bthi,hij->bthj', xh, w_x).reshape(b_sz, t, B_WIDTH) + b_x)
    log_a = (-LRU_C * r.astype(jnp.float32)) * jax.nn.softplus(-lam.astype(jnp.float32))
    a = jnp.exp(log_a)
    u = jnp.sqrt(jnp.maximum(-jnp.expm1(2.0 * log_a), 0.0)) * (gi * xc).astype(jnp.float32)

    def combine(left, right):
        a1, u1 = left
        a2, u2 = right
        return a1 * a2, a2 * u1 + u2

    _, hs = lax.associative_scan(combine, (a, u), axis=1)
    return hs.astype(xb.dtype) * jax.nn.gelu(gb)

def gla_mixer(q, k, v, g, g_lr, w_g_up, b_g, norm_w):
    b_sz, t, _ = q.shape
    log_f = jax.nn.log_sigmoid((g_lr @ w_g_up + b_g).astype(jnp.float32)) / C_GATE_NORM
    qh = q.reshape(b_sz, t, C_HEADS, C_DK) * (C_DK ** -0.5)
    kh = k.reshape(b_sz, t, C_HEADS, C_DK)
    vh = v.reshape(b_sz, t, C_HEADS, C_DV)
    o = chunked_gated_linear_attention(qh, kh, vh, log_f.reshape(b_sz, t, C_HEADS, C_DK))
    return head_rmsnorm(o, norm_w) * jax.nn.silu(g)

def first_inputs(seed: int = 0) -> dict:
    key = jax.random.key(seed)
    ks = jax.random.split(key, 24)
    f32 = jnp.float32

    def nrm(k, shape, scale):
        return scale * jax.random.normal(k, shape, f32)

    def gain(k, shape):
        return 1.0 + 0.05 * jax.random.normal(k, shape, f32)

    a0 = jax.random.uniform(ks[11], (DEPTH, B_WIDTH), f32, 0.9, 0.999)
    sig = a0 ** (1.0 / LRU_C)
    lam = jnp.log(sig) - jnp.log1p(-sig)
    return {
        'x': jax.random.normal(ks[0], (BATCH, SEQ, D_MODEL), f32),
        'norm_mix': gain(ks[1], (DEPTH, D_MODEL)),
        'w_in': nrm(ks[2], (DEPTH, D_MODEL, IN_COLS), D_MODEL ** -0.5),
        'hgrn_lower_bounds': nrm(ks[3], (DEPTH, A_HEADS * A_DK), 0.5),
        'hgrn_norm': gain(ks[4], (DEPTH, A_HEADS * A_DV)),
        'rg_conv_w': nrm(ks[5], (DEPTH, B_CONV, B_WIDTH), B_CONV ** -0.5),
        'rg_conv_b': nrm(ks[6], (DEPTH, B_WIDTH), 0.05),
        'rg_w_a': nrm(ks[7], (DEPTH, B_BLOCKS, HEAD_DIM, HEAD_DIM), HEAD_DIM ** -0.5),
        'rg_b_a': nrm(ks[8], (DEPTH, B_WIDTH), 0.1),
        'rg_w_x': nrm(ks[9], (DEPTH, B_BLOCKS, HEAD_DIM, HEAD_DIM), HEAD_DIM ** -0.5),
        'rg_b_x': nrm(ks[10], (DEPTH, B_WIDTH), 0.1),
        'rg_lambda': lam,
        'gla_w_gate_up': nrm(ks[12], (DEPTH, C_GATE_RANK, C_HEADS * C_DK), C_GATE_RANK ** -0.5),
        'gla_b_gate': nrm(ks[13], (DEPTH, C_HEADS * C_DK), 0.1),
        'gla_norm': gain(ks[14], (DEPTH, C_WIDTH)),
        'w_out': nrm(ks[15], (DEPTH, MIX_WIDTH, D_MODEL), MIX_WIDTH ** -0.5),
        'norm_ffn': gain(ks[16], (DEPTH, D_MODEL)),
        'ffn_w_gate': nrm(ks[17], (DEPTH, D_MODEL, D_FF), D_MODEL ** -0.5),
        'ffn_w_val': nrm(ks[18], (DEPTH, D_MODEL, D_FF), D_MODEL ** -0.5),
        'ffn_conv_w': nrm(ks[19], (DEPTH, FFN_CONV, D_FF), FFN_CONV ** -0.5),
        'ffn_conv_b': nrm(ks[20], (DEPTH, D_FF), 0.05),
        'ffn_w_down': nrm(ks[21], (DEPTH, D_FF, D_MODEL), D_FF ** -0.5),
        'norm_final': gain(ks[22], (D_MODEL,)),
    }

def first_block(x, norm_mix, w_in, hgrn_lower_bounds, hgrn_norm, rg_conv_w, rg_conv_b, rg_w_a, rg_b_a,
              rg_w_x, rg_b_x, rg_lambda, gla_w_gate_up, gla_b_gate, gla_norm, w_out, norm_ffn,
              ffn_w_gate, ffn_w_val, ffn_conv_w, ffn_conv_b, ffn_w_down, norm_final):
    lb = jax.nn.softmax(hgrn_lower_bounds.astype(jnp.float32), axis=0)
    lb = jnp.cumsum(lb, axis=0) - lb[0]
    for l in range(DEPTH):
        h = rmsnorm(x, norm_mix[l])
        proj = h @ w_in[l]
        a_q, a_f, a_i, a_g, b_x, b_g, c_q, c_k, c_v, c_g, c_lr = jnp.split(proj, IN_SPLITS, axis=-1)
        o_a = hgrn2_mixer(a_q, a_f, a_i, a_g, lb[l], hgrn_norm[l])
        o_b = rglru_mixer(b_x, b_g, rg_conv_w[l], rg_conv_b[l], rg_w_a[l], rg_b_a[l],
                          rg_w_x[l], rg_b_x[l], rg_lambda[l])
        o_c = gla_mixer(c_q, c_k, c_v, c_g, c_lr, gla_w_gate_up[l], gla_b_gate[l], gla_norm[l])
        x = x + jnp.concatenate([o_a, o_b, o_c], axis=-1) @ w_out[l]
        h = rmsnorm(x, norm_ffn[l])
        gate = causal_dwconv(h @ ffn_w_gate[l], ffn_conv_w[l], ffn_conv_b[l])
        x = x + (jax.nn.gelu(gate) * (h @ ffn_w_val[l])) @ ffn_w_down[l]
    return rmsnorm(x, norm_final)


DEPTH_2 = 2

D_MIX = D_MODEL
DIFF_HEADS = D_MIX // 256
DIFF_QK_DIM = HEAD_DIM
DIFF_V_DIM = 2 * HEAD_DIM
DSA_HEADS = D_MIX // 256
DSA_DIM = HEAD_DIM
IDX_HEADS = D_MIX // 128
IDX_DIM = HEAD_DIM
FOX_HEADS = D_MIX // 256
FOX_DIM = HEAD_DIM
DIFF_WIDTH = DIFF_HEADS * DIFF_V_DIM
DSA_WIDTH = DSA_HEADS * DSA_DIM
FOX_WIDTH = FOX_HEADS * FOX_DIM
DSA_TOPK_MAX = 256
Q_BLOCK = 128
ROPE_THETA = 10000.0
LN_EPS = 1e-5
SUBLN_EPS = 1e-5
NEG_INF = -1e30
DEEPNORM_ALPHA = (2 * DEPTH_2) ** 0.25
DEEPNORM_BETA = (8 * DEPTH_2) ** -0.25
IDX_WEIGHT_SCALE = (IDX_HEADS * IDX_DIM) ** -0.5

IN_SPLITS_2 = (
    ('diff_q', DIFF_HEADS * 2 * DIFF_QK_DIM),
    ('diff_k', DIFF_HEADS * 2 * DIFF_QK_DIM),
    ('diff_v', DIFF_HEADS * DIFF_V_DIM),
    ('dsa_q', DSA_HEADS * DSA_DIM),
    ('dsa_k', DSA_DIM),
    ('dsa_v', DSA_DIM),
    ('idx_q', IDX_HEADS * IDX_DIM),
    ('idx_k', IDX_DIM),
    ('idx_w', IDX_HEADS),
    ('fox_q', FOX_HEADS * FOX_DIM),
    ('fox_k', FOX_HEADS * FOX_DIM),
    ('fox_v', FOX_HEADS * FOX_DIM),
    ('fox_f', FOX_HEADS),
    ('gate', D_MIX),
)
VALUE_COLS = ('diff_v', 'dsa_v', 'fox_v')
IN_WIDTH = sum(n for _, n in IN_SPLITS_2)


def split_columns(h):
    out, off = [], 0
    for _, n in IN_SPLITS_2:
        out.append(h[..., off:off + n])
        off += n
    return out

def rope(x, pos):
    d = x.shape[-1]
    inv = ROPE_THETA ** (-jnp.arange(0, d, 2, dtype=jnp.float32) / d)
    ang = pos.astype(jnp.float32)[:, None] * inv[None, :]
    shp = (x.shape[1],) + (1,) * (x.ndim - 3) + (d // 2,)
    cos = jnp.cos(ang).reshape(shp).astype(x.dtype)
    sin = jnp.sin(ang).reshape(shp).astype(x.dtype)
    x1, x2 = x[..., : d // 2], x[..., d // 2:]
    return jnp.concatenate([x1 * cos - x2 * sin, x2 * cos + x1 * sin], axis=-1)

def to_blocks(a):
    B, S = a.shape[:2]
    return jnp.moveaxis(a.reshape((B, S // Q_BLOCK, Q_BLOCK) + a.shape[2:]), 1, 0)

def from_blocks(a):
    nb, B, qb = a.shape[:3]
    return jnp.moveaxis(a, 0, 1).reshape((B, nb * qb) + a.shape[3:])

def layer_norm(x, g, b):
    xf = x.astype(jnp.float32)
    mu = jnp.mean(xf, axis=-1, keepdims=True)
    var = jnp.mean(jnp.square(xf - mu), axis=-1, keepdims=True)
    y = (xf - mu) * lax.rsqrt(var + LN_EPS) * g.astype(jnp.float32) + b.astype(jnp.float32)
    return y.astype(x.dtype)

def diff_attention(q, k, v, lam, pos):
    scale = DIFF_QK_DIM ** -0.5
    S = q.shape[1]

    def block(args):
        qb, t = args
        s = jnp.einsum('bqhmd,bkhmd->bhmqk', qb, k).astype(jnp.float32) * scale
        causal = t[:, None] >= pos[None, :]
        p = jax.nn.softmax(jnp.where(causal, s, NEG_INF), axis=-1)
        p = p[:, :, 0] - lam * p[:, :, 1]
        return jnp.einsum('bhqk,bkhe->bqhe', p, v)

    out = lax.map(block, (to_blocks(q), pos.reshape(S // Q_BLOCK, Q_BLOCK)))
    return from_blocks(out)

def dsa_attention(q, k, v, qi, ki, wi, pos, topk):
    scale = DSA_DIM ** -0.5
    S = q.shape[1]

    def block(args):
        qb, qib, wib, t = args
        sc = jnp.einsum('bqhd,bsd->bqhs', qib, ki).astype(jnp.float32)
        idx_score = jnp.einsum('bqhs,bqh->bqs', jax.nn.relu(sc), wib.astype(jnp.float32))
        causal = t[:, None] >= pos[None, :]
        idx_score = jnp.where(causal[None], idx_score, -jnp.inf)
        _, idx = lax.top_k(idx_score, topk)
        kg = jax.vmap(lambda kk, ii: kk[ii])(k, idx)
        vg = jax.vmap(lambda vv, ii: vv[ii])(v, idx)
        s = jnp.einsum('bqhd,bqkd->bhqk', qb, kg).astype(jnp.float32) * scale
        valid = idx <= t[None, :, None]
        p = jax.nn.softmax(jnp.where(valid[:, None], s, NEG_INF), axis=-1)
        return jnp.einsum('bhqk,bqkd->bqhd', p, vg)

    out = lax.map(block, (to_blocks(q), to_blocks(qi), to_blocks(wi),
                          pos.reshape(S // Q_BLOCK, Q_BLOCK)))
    return from_blocks(out)

def forgetting_attention(q, k, v, logf, pos):
    scale = FOX_DIM ** -0.5
    S = q.shape[1]
    c = jnp.cumsum(logf, axis=1)
    c_keys = jnp.transpose(c, (0, 2, 1))

    def block(args):
        qb, cb, t = args
        s = jnp.einsum('bqhd,bkhd->bhqk', qb, k).astype(jnp.float32) * scale
        s = s + jnp.transpose(cb, (0, 2, 1))[..., None] - c_keys[:, :, None, :]
        causal = t[:, None] >= pos[None, :]
        p = jax.nn.softmax(jnp.where(causal, s, NEG_INF), axis=-1)
        return jnp.einsum('bhqk,bkhd->bqhd', p, v)

    out = lax.map(block, (to_blocks(q), to_blocks(c), pos.reshape(S // Q_BLOCK, Q_BLOCK)))
    return from_blocks(out)

def hybrid_layer(x, w_in, b_f, lam_q1, lam_k1, lam_q2, lam_k2, g_subln, w_out, ln_g, ln_b, layer_idx):
    B, S, _ = x.shape
    pos = jnp.arange(S, dtype=jnp.int32)
    h = jnp.einsum('bsd,de->bse', x, w_in)
    (dq, dk, dv, sq, sk, sv, iq, ik, iw, fq, fk, fv, ff, gate) = split_columns(h)

    dq = rope(dq.reshape(B, S, DIFF_HEADS * 2, DIFF_QK_DIM), pos).reshape(B, S, DIFF_HEADS, 2, DIFF_QK_DIM)
    dk = rope(dk.reshape(B, S, DIFF_HEADS * 2, DIFF_QK_DIM), pos).reshape(B, S, DIFF_HEADS, 2, DIFF_QK_DIM)
    dv = dv.reshape(B, S, DIFF_HEADS, DIFF_V_DIM)
    lambda_init = 0.8 - 0.6 * math.exp(-0.3 * layer_idx)
    lam = (jnp.exp(jnp.sum(lam_q1.astype(jnp.float32) * lam_k1.astype(jnp.float32)))
           - jnp.exp(jnp.sum(lam_q2.astype(jnp.float32) * lam_k2.astype(jnp.float32))) + lambda_init)
    a = diff_attention(dq, dk, dv, lam, pos)
    a = a * lax.rsqrt(jnp.mean(a * a, axis=-1, keepdims=True) + SUBLN_EPS) * g_subln.astype(jnp.float32) * (1.0 - lambda_init)
    a = a.reshape(B, S, DIFF_WIDTH)

    sq = rope(sq.reshape(B, S, DSA_HEADS, DSA_DIM), pos)
    sk = rope(sk, pos)
    iq = rope(iq.reshape(B, S, IDX_HEADS, IDX_DIM), pos)
    ik = rope(ik, pos)
    topk = min(DSA_TOPK_MAX, S // 4)
    bo = dsa_attention(sq, sk, sv, iq, ik, iw * IDX_WEIGHT_SCALE, pos, topk).reshape(B, S, DSA_WIDTH)

    logf = jax.nn.log_sigmoid(ff.astype(jnp.float32) + b_f.astype(jnp.float32))
    co = forgetting_attention(fq.reshape(B, S, FOX_HEADS, FOX_DIM), fk.reshape(B, S, FOX_HEADS, FOX_DIM),
                              fv.reshape(B, S, FOX_HEADS, FOX_DIM), logf, pos).reshape(B, S, FOX_WIDTH)

    mixed = jnp.concatenate([a, bo, co], axis=-1) * jax.nn.silu(gate.astype(jnp.float32))
    out = jnp.einsum('bse,ed->bsd', mixed.astype(x.dtype), w_out)
    return layer_norm(DEEPNORM_ALPHA * x + out, ln_g, ln_b)

def second_inputs(seed: int = 0) -> dict:
    key = jax.random.key(seed)
    ks = jax.random.split(key, 12)
    x = jax.random.normal(ks[0], (BATCH, SEQ, D_MODEL), jnp.float32)
    col_scale = np.concatenate([
        np.full((n,), DEEPNORM_BETA if name in VALUE_COLS else 1.0, np.float32) for name, n in IN_SPLITS_2
    ]) * np.float32(D_MODEL ** -0.5)
    w_in = jax.random.normal(ks[1], (DEPTH_2, D_MODEL, IN_WIDTH), jnp.float32) * jnp.asarray(col_scale)
    b_f = 1.0 + 0.1 * jax.random.normal(ks[2], (DEPTH_2, FOX_HEADS), jnp.float32)
    lam_q1 = 0.1 * jax.random.normal(ks[3], (DEPTH_2, DIFF_QK_DIM), jnp.float32)
    lam_k1 = 0.1 * jax.random.normal(ks[4], (DEPTH_2, DIFF_QK_DIM), jnp.float32)
    lam_q2 = 0.1 * jax.random.normal(ks[5], (DEPTH_2, DIFF_QK_DIM), jnp.float32)
    lam_k2 = 0.1 * jax.random.normal(ks[6], (DEPTH_2, DIFF_QK_DIM), jnp.float32)
    g_subln = 1.0 + 0.02 * jax.random.normal(ks[7], (DEPTH_2, DIFF_V_DIM), jnp.float32)
    w_out = jax.random.normal(ks[8], (DEPTH_2, D_MIX, D_MODEL), jnp.float32) * (D_MIX ** -0.5) * DEEPNORM_BETA
    ln_g = 1.0 + 0.02 * jax.random.normal(ks[9], (DEPTH_2, D_MODEL), jnp.float32)
    ln_b = 0.02 * jax.random.normal(ks[10], (DEPTH_2, D_MODEL), jnp.float32)
    return {'x': x, 'w_in': w_in, 'b_f': b_f, 'lam_q1': lam_q1, 'lam_k1': lam_k1,
            'lam_q2': lam_q2, 'lam_k2': lam_k2, 'g_subln': g_subln, 'w_out': w_out,
            'ln_g': ln_g, 'ln_b': ln_b}

def second_block(x, w_in, b_f, lam_q1, lam_k1, lam_q2, lam_k2, g_subln, w_out, ln_g, ln_b):
    for l in range(DEPTH_2):
        x = hybrid_layer(x, w_in[l], b_f[l], lam_q1[l], lam_k1[l], lam_q2[l], lam_k2[l],
                         g_subln[l], w_out[l], ln_g[l], ln_b[l], l)
    return x


def setup_inputs(seed=0):
    out = dict(first_inputs(seed))
    for name, value in second_inputs(seed + 1).items():
        if name != "x":
            out[name + "_2"] = value
    return out


def reference(
    x, norm_mix, w_in, hgrn_lower_bounds, hgrn_norm, rg_conv_w, rg_conv_b, rg_w_a, rg_b_a,
    rg_w_x, rg_b_x, rg_lambda, gla_w_gate_up, gla_b_gate, gla_norm, w_out, norm_ffn, ffn_w_gate,
    ffn_w_val, ffn_conv_w, ffn_conv_b, ffn_w_down, norm_final, w_in_2, b_f_2, lam_q1_2,
    lam_k1_2, lam_q2_2, lam_k2_2, g_subln_2, w_out_2, ln_g_2, ln_b_2,
):
    x = first_block(
        x, norm_mix, w_in, hgrn_lower_bounds, hgrn_norm, rg_conv_w, rg_conv_b, rg_w_a, rg_b_a,
        rg_w_x, rg_b_x, rg_lambda, gla_w_gate_up, gla_b_gate, gla_norm, w_out, norm_ffn,
        ffn_w_gate, ffn_w_val, ffn_conv_w, ffn_conv_b, ffn_w_down, norm_final,
    )
    return second_block(
        x, w_in_2, b_f_2, lam_q1_2, lam_k1_2, lam_q2_2, lam_k2_2, g_subln_2, w_out_2, ln_g_2,
        ln_b_2,
    )


_drawn_inputs = setup_inputs


def setup_inputs(seed=0):
    import zlib

    import numpy as np

    out = dict(_drawn_inputs(seed))
    spreads = {}
    factors = {'hgrn_norm': 3.836,
     'rg_b_a': 6.26,
     'rg_b_x': 4.231,
     'gla_b_gate': 4.09,
     'gla_norm': 3.833,
     'b_f_2': 64.0,
     'lam_q1_2': 4.803,
     'lam_k1_2': 7.592,
     'lam_q2_2': 3.426,
     'lam_k2_2': 3.443,
     'g_subln_2': 22.646}
    for name, (base, spread) in spreads.items():
        noise = np.random.default_rng([zlib.crc32(name.encode()), seed]).standard_normal(out[name].shape)
        drawn = base * np.exp(spread * noise) if base else spread * noise
        out[name] = jnp.asarray(drawn.astype(out[name].dtype))
    for name, factor in factors.items():
        out[name] = (out[name] * factor).astype(out[name].dtype)
    return out
```

```python
import math
from contextlib import ExitStack

import numpy as np

import concourse.bass as bass
from concourse import mybir

FP32 = mybir.dt.float32
BF16 = mybir.dt.bfloat16
INT32 = mybir.dt.int32
ACT = mybir.ActivationFunctionType
ALU = mybir.AluOpType
AX = mybir.AxisListType

P = 128
S = 1024
D = 1024
NT = S // P
KT = D // P
HALF = 512
EPS = 1e-6
LN_EPS = 1e-5
SUBLN_EPS = 1e-5
F_FLOOR = 1e-20
LRU_C = 8.0
NEG = -1e30
D_FF = 2688
FT = D_FF // P
DEPTH_2 = 2
ALPHA = (2 * DEPTH_2) ** 0.25
IDX_SCALE = 512 ** -0.5
TOPK = 256
BISECTIONS = 32
QK_SCALE = 64 ** -0.5

LEVELS = [64, 32, 16, 8, 4, 2, 1]

CONST_AT = {}


def _const_columns():
    at = 0
    for name, width in (("ident", P), ("swap", P), ("causal", P), ("pick", 4 * P),
                        ("level", 7 * 64), ("keep", S), ("cos", S), ("sin", S)):
        CONST_AT[name] = (at, width)
        at += width
    return at


CONST_WIDTH = _const_columns()
FIRST_AT = CONST_AT["level"][0]
ROPE_AT = CONST_AT["cos"][0]


def constants():
    c = np.zeros((P, CONST_WIDTH), np.float32)

    def put(name, value):
        at, width = CONST_AT[name]
        c[:, at:at + width] = value

    put("ident", np.eye(P))
    j = np.arange(P)
    swap = np.zeros((P, P))
    swap[j, (j // 64) * 64 + (j + 32) % 64] = 1.0
    put("swap", swap)
    put("causal", np.where(j[None, :] > j[:, None], NEG, 0.0))
    level = np.zeros((P, 7, 64))
    for n, b in enumerate(LEVELS):
        i = np.arange(64)
        block = i // b
        level[:, n, :] = (j[:, None] // (2 * b) == block[None, :]) & (j[:, None] % (2 * b) < b)
    put("level", level.reshape(P, -1))
    keep = np.ones(S)
    keep[::P] = 0.0
    put("keep", keep[None, :])
    pick = np.zeros((P, 4, P))
    for h in range(4):
        pick[h, h, :] = 1.0
    put("pick", pick.reshape(P, -1))
    inv = (np.float32(10000.0) ** (-np.arange(0, 64, 2, dtype=np.float32) / np.float32(64))).astype(np.float32)
    angle = (np.arange(S, dtype=np.float32)[:, None] * inv[None, :]).astype(np.float32)
    cos, sin = np.cos(angle).T, np.sin(angle).T
    put("cos", np.concatenate([cos] * 4))
    put("sin", np.concatenate([sin, -sin] * 2))
    return c


class Kit:

    def __init__(self, nc, ctx):
        self.nc, self.ctx = nc, ctx
        self.psum = ctx.enter_context(nc.psum_tensor("psum", [P, 8, HALF], FP32))
        self.sems, self.sem_ctx = [], ctx.enter_context(ExitStack())

    def sem(self, name):
        s = self.sem_ctx.enter_context(self.nc.semaphore(name))
        self.sems.append(s)
        return s

    def clear_semaphores(self):
        with self.nc.Block() as block:
            @block.sync
            def _(sp):
                for sem in self.sems:
                    sp.sem_clear(sem)
        self.sem_ctx.close()
        self.sems = []

    def pair(self, n):
        return self.psum[:, 2 * n:2 * n + 2, :].rearrange("p b n -> p (b n)")


class Own:

    def __init__(self, eng, sem):
        self.eng, self.sem, self.n = eng, sem, 0

    def __call__(self, instruction):
        instruction.then_inc(self.sem, 1)
        self.n += 1
        return self.n

    def wait(self, n=None):
        self.eng.wait_ge(self.sem, self.n if n is None else n)

    def then(self, instruction):
        self(instruction)
        self.wait()


def sbuf(nc, stack, name, shape, dtype=FP32):
    return stack.enter_context(nc.sbuf_tensor(name, shape, dtype))[(slice(None),) * len(shape)]


def bcast(row_ap):
    return row_ap.partition_broadcast(P)


def norm_stage(kit, tag, X, XT, ident, gain, bias=None, eps=EPS, keep=False):
    nc = kit.nc
    layer = bias is not None
    gain_in, squares, stats, root, rows, turned, copied, dve_own = (
        kit.sem(f"{tag}_{n}") for n in ("gain_in", "squares", "stats", "root", "rows", "turned", "copied",
                                        "dve_own"))
    with ExitStack() as mem:
        G = sbuf(nc, mem, f"{tag}_G", [P, D])
        B = sbuf(nc, mem, f"{tag}_B", [P, D]) if layer else None
        H = None if keep else sbuf(nc, mem, f"{tag}_H", [P, 2, D])
        junk = sbuf(nc, mem, f"{tag}_junk", [P, D])
        sums = sbuf(nc, mem, f"{tag}_sums", [P, NT])
        bn = sbuf(nc, mem, f"{tag}_bn", [P, NT, 2, 6])
        mv = sbuf(nc, mem, f"{tag}_mv", [P, NT, 2])
        eps_col = sbuf(nc, mem, f"{tag}_eps", [P, 1])
        dev = sbuf(nc, mem, f"{tag}_dev", [P, NT])
        inv = sbuf(nc, mem, f"{tag}_inv", [P, NT])
        with nc.Block() as block:
            @block.sync
            def _(sp):
                sp.dma_start(G[:, :], bcast(gain)).then_inc(gain_in, 16)
                if layer:
                    sp.dma_start(B[:, :], bcast(bias)).then_inc(gain_in, 16)

            @block.scalar
            def _(act):
                if not layer:
                    for t in range(NT):
                        act.activation(junk[:, :], X[:, t, :], ACT.Square,
                                       accum_out=sums[:, t:t + 1]).then_inc(squares, 1)
                        act.wait_ge(squares, t + 1)
                act.wait_ge(stats, NT + 1 if layer else 1)
                src = mv[:, :, 1] if layer else sums[:, :]
                act.activation(dev[:, :], src, ACT.Sqrt, scale=1.0 if layer else 1.0 / D,
                               bias=eps_col[:, :]).then_inc(root, 1)
                for t in range(NT):
                    act.wait_ge(turned, t + 1)
                    act.activation(XT[:, :, t * P:(t + 1) * P],
                                   kit.pair(t % 2).rearrange("p (k n) -> p k n", k=KT),
                                   ACT.Copy).then_inc(copied, 1)

            @block.vector
            def _(dve):
                own = Own(dve, dve_own)
                if layer:
                    for t in range(NT):
                        for n in range(2):
                            own(dve.bn_stats(bn[:, t, n, :], X[:, t, n * HALF:(n + 1) * HALF]))
                        own.wait()
                        dve.bn_aggr(mv[:, t, :], bn[:, t, :, :]).then_inc(stats, 1)
                dve.memset(eps_col[:, :], eps).then_inc(stats, 1)
                dve.wait_ge(root, 1)
                own.then(dve.reciprocal(inv[:, :], dev[:, :]))
                dve.wait_ge(gain_in, 32 if layer else 16)
                for t in range(NT):
                    out = X[:, t, :] if keep else H[:, t % 2, :]
                    if not keep and t >= 2:
                        dve.wait_ge(turned, t - 1)
                    if layer:
                        own.then(dve.tensor_scalar(out, X[:, t, :], mv[:, t, 0:1], inv[:, t:t + 1],
                                                   ALU.subtract, ALU.mult))
                        own.then(dve.tensor_tensor(out, out, G[:, :], ALU.mult))
                        dve.tensor_tensor(out, out, B[:, :], ALU.add).then_inc(rows, 1)
                    else:
                        dve.scalar_tensor_tensor(out, X[:, t, :], inv[:, t:t + 1], G[:, :],
                                                 ALU.mult, ALU.mult).then_inc(rows, 1)

            @block.tensor
            def _(pe):
                for t in range(NT):
                    src = X[:, t, :] if keep else H[:, t % 2, :]
                    pe.wait_ge(rows, t + 1)
                    if t >= 2:
                        pe.wait_ge(copied, t - 1)
                    for k in range(KT):
                        last = pe.transpose(kit.pair(t % 2)[:, k * P:(k + 1) * P],
                                            src[:, k * P:(k + 1) * P], ident)
                    last.then_inc(turned, 1)


class Unit:

    def __init__(self, kind, items, width, by, take, t=0, store=None):
        self.kind, self.items, self.width, self.by, self.take, self.t = kind, items, width, by, take, t
        self.store = store


def product_stage(kit, tag, XT, items, units, slots=8, rope=None, place=None, rot_place=None, beside=None):
    nc = kit.nc
    n_pairs = 3 if rope else 4
    w_in = [kit.sem(f"{tag}_w_in{s}") for s in range(slots)]
    products, taken_act, taken_dve, act_own, dve_own, scaled, swapped = (
        kit.sem(f"{tag}_{n}") for n in ("products", "taken_act", "taken_dve", "act_own", "dve_own",
                                        "scaled", "swapped"))
    last_use = {}
    for u, unit in enumerate(units):
        for i in unit.items:
            last_use[i] = u
    stores = [u for u, unit in enumerate(units) if unit.store]
    stored = [kit.sem(f"{tag}_stored{s}") for s in range(2)] if stores else []
    by_act = [u for u, unit in enumerate(units) if unit.by == "act"]
    by_dve = [u for u, unit in enumerate(units) if unit.by != "act"]
    ropes = [u for u, unit in enumerate(units) if unit.by == "rope"]
    with ExitStack() as mem:
        W = sbuf(nc, mem, f"{tag}_W", [P, slots, 1024]) if place is None else place
        if rope:
            cos, sin, swap = rope
            rot = sbuf(nc, mem, f"{tag}_rot", [P, 2, S]) if rot_place is None else rot_place
            straight = sbuf(nc, mem, f"{tag}_straight", [P, 2, S])
        with nc.Block() as block:
            def wait_taken(eng, u):
                if units[u].by == "act":
                    eng.wait_ge(taken_act, by_act.index(u) + 1)
                elif units[u].by == "rope":
                    eng.wait_ge(scaled, ropes.index(u) + 1)
                else:
                    eng.wait_ge(taken_dve, [v for v in by_dve if units[v].by == "dve"].index(u) + 1)

            @block.sync
            def _(sp):
                for i, (src, width) in enumerate(items):
                    if i >= slots:
                        sp.wait_ge(products, last_use[i - slots] + 1)
                    dst = W[:, i % slots, 0:width]
                    if len(src.shape) == 3:
                        dst = dst.rearrange("p (a n) -> p a n", a=src.shape[1])
                    sp.dma_start(dst, src).then_inc(w_in[i % slots], 16)

            @block.tensor
            def _(pe):
                def swap_halves(n):
                    pe.wait_ge(scaled, n + 1)
                    if n >= 1:
                        pe.wait_ge(taken_dve, n)
                    for c in range(2):
                        last = pe.matmul(kit.pair(3)[:, c * HALF:(c + 1) * HALF], swap,
                                         rot[:, n % 2, c * HALF:(c + 1) * HALF], start=True, stop=True)
                    last.then_inc(swapped, 1)

                for u, unit in enumerate(units):
                    for i in unit.items:
                        pe.wait_ge(w_in[i % slots], 16 * (i // slots + 1))
                    if u >= n_pairs:
                        wait_taken(pe, u - n_pairs)
                    out = kit.pair(u % n_pairs)
                    if unit.kind == "feature":
                        m = unit.width
                        w = W[:, unit.items[0] % slots, 0:KT * m].rearrange("p (k m) -> p k m", k=KT)
                        for c in range(2):
                            for k in range(KT):
                                last = pe.matmul(out[0:m, c * HALF:(c + 1) * HALF], w[:, k, :],
                                                 XT[:, k, c * HALF:(c + 1) * HALF],
                                                 start=k == 0, stop=k == KT - 1)
                    else:
                        pack = KT // len(unit.items)
                        for c in range(0, unit.width, HALF):
                            e = min(unit.width, c + HALF)
                            for k in range(KT):
                                at = (k % pack) * unit.width
                                last = pe.matmul(out[:, c:e], XT[:, k, unit.t * P:(unit.t + 1) * P],
                                                 W[:, unit.items[k // pack] % slots, at + c:at + e],
                                                 start=k == 0, stop=k == KT - 1)
                    last.then_inc(products, 1)
                    if u - 1 in ropes:
                        swap_halves(ropes.index(u - 1))
                if len(units) - 1 in ropes:
                    swap_halves(len(ropes) - 1)

            @block.scalar
            def _(act):
                own = Own(act, act_own)
                for u in by_act:
                    act.wait_ge(products, u + 1)
                    if u in stores and stores.index(u) >= 2:
                        n = stores.index(u)
                        act.wait_ge(stored[n % 2], 16 * (n // 2))
                    units[u].take(act, kit.pair(u % n_pairs), own).then_inc(taken_act, 1)
                    if u in stores:
                        act.wait_ge(taken_act, by_act.index(u) + 1)
                        act.dma_start(*units[u].store).then_inc(stored[stores.index(u) % 2], 16)
                for n, sem in enumerate(stored):
                    act.wait_ge(sem, 16 * len(stores[n::2]))

            @block.vector
            def _(dve):
                own = Own(dve, dve_own)
                pending = []
                if beside:
                    beside(dve)

                def add_partner(n, dst, split):
                    dve.wait_ge(swapped, n + 1)
                    if split is None:
                        dve.tensor_tensor(dst, dst, kit.pair(3), ALU.add).then_inc(taken_dve, 1)
                        return
                    for i, tile in enumerate(split):
                        half = slice(64 * i, 64 * i + 64)
                        last = dve.tensor_tensor(tile[half, :], dst[half, :], kit.pair(3)[half, :], ALU.add)
                    last.then_inc(taken_dve, 1)

                for u in by_dve:
                    dve.wait_ge(products, u + 1)
                    out = kit.pair(u % n_pairs)
                    if units[u].by == "rope":
                        n = ropes.index(u)
                        dst, scale, split = units[u].take
                        if split is not None:
                            dst = straight[:, n % 2, :]
                            if n >= 2:
                                dve.wait_ge(taken_dve, n - 1)
                        own(dve.scalar_tensor_tensor(dst, out, scale, cos, ALU.mult, ALU.mult))
                        if n >= 2:
                            dve.wait_ge(swapped, n - 1)
                        dve.scalar_tensor_tensor(rot[:, n % 2, :], out, scale, sin, ALU.mult,
                                                 ALU.mult).then_inc(scaled, 1)
                        own.wait()
                        if pending:
                            add_partner(*pending.pop())
                        pending.append((n, dst, split))
                    else:
                        if pending:
                            add_partner(*pending.pop())
                        units[u].take(dve, out, own).then_inc(taken_dve, 1)
                if pending:
                    add_partner(*pending.pop())


def copy_into(dst, rows=P, scale=1.0):
    width = dst.free_size()
    return lambda act, psum, own: act.activation(dst, psum[0:rows, 0:width], ACT.Copy, scale=scale)


def copy_into_dve(dst):
    width = dst.free_size()
    return lambda dve, psum, own: dve.tensor_copy(dst, psum[:, 0:width])


def rglru_stage(kit, BX, BG, XT, spare, d):
    nc = kit.nc
    NB = 4
    params, blocks, zeroed, ready, conv, gates, sig, decay, root, gelu, own_d, own_a, done = (
        kit.sem(f"lru_{n}") for n in ("params", "blocks", "zeroed", "ready", "conv", "gates", "sig", "decay",
                                      "root", "gelu", "own_d", "own_a", "done"))
    with ExitStack() as mem:
        XC, R = XT[:, 0:NB, :], XT[:, NB:2 * NB, :]
        GI = sbuf(nc, mem, "lru_GI", [P, NB, S])
        TH = sbuf(nc, mem, "lru_TH", [P, NB, S])
        A = BX[:, :, 3:3 + S]
        W = spare.rearrange("p (n j m) -> p n j m", n=2, j=NB)
        par = sbuf(nc, mem, "lru_par", [P, 8, NB])
        tmp = sbuf(nc, mem, "lru_tmp", [P, 6, NB])
        with nc.Block() as block:
            @block.sync
            def _(sp):
                with nc.allow_non_contiguous_dma(reason="a few hundred per-channel parameters"):
                    for n, src in enumerate([d["rg_conv_w"][k] for k in range(4)]
                                            + [d["rg_conv_b"], d["rg_b_a"], d["rg_b_x"], d["rg_lambda"]]):
                        sp.dma_start(par[:, n, :], src.rearrange("(j p) -> p j", p=P)).then_inc(params, 16)
                sp.wait_ge(zeroed, 1)
                for n, src in enumerate((d["rg_w_a"], d["rg_w_x"])):
                    for half in range(2):
                        sp.dma_start(W[half * 64:half * 64 + 64, n, :, half * 64:half * 64 + 64],
                                     src.rearrange("(j two) i o -> two i j o", two=2)[half]
                                     ).then_inc(blocks, 16)

            @block.gpsimd
            def _(pool):
                pool.memset(W[:, :, :, :], 0.0).then_inc(zeroed, 1)

            @block.vector
            def _(dve):
                own = Own(dve, own_d)
                dve.wait_ge(params, 16 * 8)
                lam = par[:, 7, :]
                mag, e, w = tmp[:, 0, :], tmp[:, 1, :], tmp[:, 2, :]
                own.then(dve.tensor_scalar(tmp[:, 3, :], lam, -1.0, None, ALU.mult))
                dve.tensor_tensor(mag, tmp[:, 3, :], lam, ALU.min).then_inc(ready, 1)
                for j in range(NB):
                    x = BX[:, j, :]
                    own.then(dve.tensor_scalar(XC[:, j, :], x[:, 3:3 + S], par[:, 3, j:j + 1],
                                               par[:, 4, j:j + 1], ALU.mult, ALU.add))
                    for k in range(3):
                        ins = dve.scalar_tensor_tensor(XC[:, j, :], x[:, k:k + S], par[:, k, j:j + 1],
                                                       XC[:, j, :], ALU.mult, ALU.add)
                        if k < 2:
                            own.then(ins)
                        else:
                            ins.then_inc(conv, 1)
                dve.wait_ge(own_a, 1)
                own.then(dve.tensor_scalar(w, e, 1.0, None, ALU.add))
                own(dve.tensor_scalar(tmp[:, 4, :], w, 1.0, None, ALU.is_equal))
                dve.tensor_scalar(tmp[:, 5, :], w, -1.0, None, ALU.add).then_inc(ready, 1)
                own.wait()
                dve.wait_ge(ready, 2)
                own.then(dve.tensor_tensor(tmp[:, 5, :], tmp[:, 5, :], tmp[:, 4, :], ALU.add))
                own.then(dve.reciprocal(tmp[:, 5, :], tmp[:, 5, :]))
                dve.wait_ge(own_a, 2)
                own.then(dve.tensor_tensor(w, w, tmp[:, 4, :], ALU.add))
                own.then(dve.tensor_tensor(w, w, tmp[:, 5, :], ALU.mult))
                own.then(dve.tensor_tensor(w, w, e, ALU.mult))
                own.then(dve.tensor_scalar(tmp[:, 3, :], tmp[:, 3, :], 0.0, None, ALU.max))
                own.then(dve.tensor_tensor(w, w, tmp[:, 3, :], ALU.add))
                own(dve.tensor_scalar(tmp[:, 3, :], w, LRU_C, None, ALU.mult))
                own(dve.tensor_scalar(tmp[:, 4, :], w, -LRU_C, None, ALU.mult))
                dve.tensor_scalar(tmp[:, 5, :], w, -2 * LRU_C, None, ALU.mult).then_inc(ready, 1)
                for j in range(NB):
                    dve.wait_ge(decay, j + 1)
                    own.then(dve.scalar_tensor_tensor(TH[:, j, :], R[:, j, :], 1.0, TH[:, j, :],
                                                      ALU.add, ALU.mult))
                    dve.tensor_scalar(TH[:, j, :], TH[:, j, :], 0.0, None, ALU.max).then_inc(ready, 1)
                    own.then(dve.tensor_tensor(GI[:, j, :], GI[:, j, :], XC[:, j, :], ALU.mult))
                for j in range(NB):
                    dve.wait_ge(root, j + 1)
                    own.then(dve.tensor_tensor(GI[:, j, :], GI[:, j, :], TH[:, j, :], ALU.mult))
                    own.then(dve.tensor_tensor_scan(XC[:, j, :], A[:, j, :], GI[:, j, :], 0.0,
                                                    ALU.mult, ALU.add))
                    dve.wait_ge(gelu, j + 1)
                    dve.tensor_tensor(BG[:, j, :], BG[:, j, :], XC[:, j, :], ALU.mult).then_inc(done, 1)

            @block.tensor
            def _(pe):
                pe.wait_ge(blocks, 16 * 4)
                for j in range(NB):
                    pe.wait_ge(conv, j + 1)
                    for n in range(2):
                        if j >= 2:
                            pe.wait_ge(sig, 2 * (j - 2) + n + 1)
                        for c in range(2):
                            last = pe.matmul(kit.pair(2 * n + j % 2)[:, c * HALF:(c + 1) * HALF],
                                             W[:, n, j, :], XC[:, j, c * HALF:(c + 1) * HALF],
                                             start=True, stop=True)
                        last.then_inc(gates, 1)

            @block.scalar
            def _(act):
                act.wait_ge(ready, 1)
                act.activation(tmp[:, 1, :], tmp[:, 0, :], ACT.Exp).then_inc(own_a, 1)
                act.wait_ge(ready, 2)
                act.activation(tmp[:, 2, :], tmp[:, 2, :], ACT.Ln).then_inc(own_a, 1)
                for j in range(NB):
                    for n, dst in enumerate((R, GI)):
                        act.wait_ge(gates, 2 * j + n + 1)
                        act.activation(dst[:, j, :], kit.pair(2 * n + j % 2), ACT.Sigmoid,
                                       bias=par[:, 5 + n, j:j + 1]).then_inc(sig, 1)
                act.wait_ge(sig, 2 * NB)
                act.wait_ge(ready, 3)
                for j in range(NB):
                    act.activation(TH[:, j, :], R[:, j, :], ACT.Tanh,
                                   scale=tmp[:, 3, j:j + 1]).then_inc(own_a, 1)
                for j in range(NB):
                    act.activation(A[:, j, :], R[:, j, :], ACT.Exp, scale=tmp[:, 4, j:j + 1]).then_inc(own_a, 1)
                    act.wait_ge(own_a, 2 + NB + j + 1)
                    act.activation(R[:, j, :], R[:, j, :], ACT.Exp, scale=tmp[:, 5, j:j + 1]).then_inc(decay, 1)
                for j in range(NB):
                    act.activation(BG[:, j, :], BG[:, j, :], ACT.Gelu_apprx_tanh).then_inc(gelu, 1)
                for j in range(NB):
                    act.wait_ge(ready, 4 + j)
                    act.activation(TH[:, j, :], TH[:, j, :], ACT.Sqrt).then_inc(root, 1)


def gate_prep_stage(kit, AF, AK, CLR, LF, spare, d):
    nc = kit.nc
    params, low, made, sg, lns, own_d, own_a, gate = (
        kit.sem(f"gp_{n}") for n in ("params", "low", "made", "sg", "lns", "own_d", "own_a", "gate"))
    with ExitStack() as mem:
        par = sbuf(nc, mem, "gp_par", [P, 3])
        lb = sbuf(nc, mem, "gp_lb", [P, 4])
        UP = sbuf(nc, mem, "gp_UP", [16, P])
        F, F2, Y, E = spare[:, 0:2, :], spare[:, 2:4, :], spare[:, 4, :], spare[:, 5, :]
        with nc.Block() as block:
            @block.sync
            def _(sp):
                with nc.allow_non_contiguous_dma(reason="a few hundred per-channel parameters"):
                    sp.dma_start(par[:, 0:2], d["hgrn_lower_bounds"].rearrange("(j p) -> p j", p=P)
                                 ).then_inc(params, 16)
                    sp.dma_start(par[:, 2:3], d["gla_b_gate"].rearrange("(j p) -> p j", p=P)
                                 ).then_inc(params, 16)
                sp.dma_start(UP[:, :], d["gla_w_gate_up"]).then_inc(params, 16)

            @block.tensor
            def _(pe):
                pe.wait_ge(params, 48)
                for c in range(2):
                    last = pe.matmul(kit.pair(0)[:, c * HALF:(c + 1) * HALF], UP[:, :],
                                     CLR[:, c * HALF:(c + 1) * HALF], start=True, stop=True)
                last.then_inc(low, 1)

            @block.scalar
            def _(act):
                act.activation(F, AF[:, :, :], ACT.Sigmoid).then_inc(sg, 1)
                act.activation(AK[:, :, :], AF, ACT.Sigmoid, scale=-1.0).then_inc(sg, 1)
                act.wait_ge(low, 1)
                act.wait_ge(params, 48)
                act.activation(E, kit.pair(0), ACT.Abs, bias=par[:, 2:3]).then_inc(own_a, 1)
                act.wait_ge(own_a, 1)
                act.activation(E, E, ACT.Exp, scale=-1.0).then_inc(own_a, 1)
                act.wait_ge(own_a, 2)
                act.activation(E, E, ACT.Ln, bias=1.0).then_inc(lns, 1)
                act.wait_ge(made, 1)
                act.activation(LF[:, 0:2, :], F2, ACT.Ln).then_inc(lns, 1)
                act.wait_ge(made, 2)
                act.activation(AF[:, :, :], F, ACT.Ln).then_inc(lns, 1)

            @block.vector
            def _(dve):
                own = Own(dve, own_d)
                dve.wait_ge(params, 48)
                own.then(dve.tensor_tensor(lb[:, 0:2], par[:, 0:2], par[:, 0:2], ALU.subtract))
                own.then(dve.tensor_scalar(lb[:, 2:4], lb[:, 0:2], -1.0, 1.0, ALU.mult, ALU.add))
                dve.wait_ge(sg, 2)
                for j in range(2):
                    own(dve.tensor_scalar(F[:, j, :], F[:, j, :], lb[:, 2 + j:3 + j], lb[:, j:j + 1],
                                          ALU.mult, ALU.add))
                    own(dve.tensor_scalar(AK[:, j, :], AK[:, j, :], lb[:, 2 + j:3 + j], None, ALU.mult))
                own.wait()
                own.then(dve.tensor_scalar(F2, F, F_FLOOR, 2.0 ** 60, ALU.max, ALU.mult))
                dve.tensor_scalar(F2, F2, 1.0, None, ALU.min).then_inc(made, 1)
                dve.tensor_scalar(F, F, 2.0 ** -60, None, ALU.max).then_inc(made, 1)
                dve.wait_ge(low, 1)
                dve.wait_ge(own_a, 1)
                own.then(dve.tensor_scalar(Y, kit.pair(0), par[:, 2:3], 0.0, ALU.add, ALU.min))
                dve.wait_ge(lns, 1)
                own.then(dve.tensor_tensor(Y, Y, E, ALU.subtract))
                own(dve.tensor_scalar(LF[:, 2, :], Y, 1.0 / 16.0, None, ALU.mult))
                dve.wait_ge(lns, 3)
                own(dve.tensor_tensor(LF[:, 0:2, :], LF[:, 0:2, :], AF, ALU.add))
                own.wait()


def gla_stage(kit, Q, K, LF, VA, VC, O, XT, spare, ident, level, keep):
    nc = kit.nc
    NL = len(LEVELS)
    VOUT = 256
    cums, refs, weights, mixed, state_w, kt_done, kt_taken, scored, placed, out_done, out_taken, \
        upd_done, upd_taken, own_d, own_a, sc0, masks = (
            kit.sem(f"gla_{n}") for n in ("cums", "refs", "weights", "mixed", "state_w", "kt_done", "kt_taken",
                                          "scored", "placed", "out_done", "out_taken", "upd_done", "upd_taken",
                                          "own_d", "own_a", "sc0", "masks"))
    tiles = [(0, 64, 0), (1, 64, 0), (2, 32, 0)]
    units = []
    for g, dk, _ in tiles:
        for u in range(P // dk // 2):
            units.append((g, dk, u))
    with ExitStack() as mem:
        QK = XT[:, 0:NL, :]
        C = XT[:, NL, :]
        Z = spare
        QE = sbuf(nc, mem, "gla_QE", [P, S])
        KL = sbuf(nc, mem, "gla_KL", [P, S])
        EL = sbuf(nc, mem, "gla_EL", [P, NT])
        KLT = sbuf(nc, mem, "gla_KLT", [P, S])
        SC = sbuf(nc, mem, "gla_SC", [P, 2, 2, P])
        ST = sbuf(nc, mem, "gla_ST", [P, 2, VOUT])
        LM = sbuf(nc, mem, "gla_LM", [P, NL * 64], INT32)
        DM = sbuf(nc, mem, "gla_DM", [P, P], INT32)
        with nc.Block() as block:
            def vals(g):
                return VA if g < 2 else VC

            @block.vector
            def _(dve):
                own = Own(dve, own_d)
                own(dve.tensor_copy(LM[:, :], level))
                own(dve.tensor_copy(DM[:, :], ident))
                own(dve.memset(SC[:, :, :, :], 0.0))
                own.wait()
                step = 0
                upd = 0
                uc = 0
                for g, dk, _ in tiles:
                    if g >= 1:
                        dve.wait_ge(out_done, 8 * uc)
                    own(dve.tensor_tensor_scan(C, keep, LF[:, g, :], 0.0, ALU.mult, ALU.add))
                    own.wait()
                    dve.sem_inc(cums, 1)
                    for n, b in enumerate(LEVELS):
                        z = Z[:, n % 2, :].rearrange("p (m w) -> p m w", w=2 * b)
                        c3 = C.rearrange("p (m w) -> p m w", w=2 * b)
                        ref = c3[:, :, b - 1:b].to_broadcast([P, S // (2 * b), 2 * b])
                        if n >= 2 or g >= 1:
                            dve.wait_ge(weights, NL * g + n - 1 if n >= 2 else NL * g)
                        own(dve.tensor_tensor(z, c3, ref, ALU.subtract))
                        own.wait()
                        dve.sem_inc(refs, 1)
                        dve.wait_ge(weights, NL * g + n + 1)
                        w = QK[:, n, :].rearrange("p (m w) -> p m w", w=2 * b)
                        q3 = Q[:, g, :].rearrange("p (m w) -> p m w", w=2 * b)
                        k3 = K[:, g, :].rearrange("p (m w) -> p m w", w=2 * b)
                        own(dve.tensor_tensor(w[:, :, b:2 * b], w[:, :, b:2 * b], q3[:, :, b:2 * b], ALU.mult))
                        own(dve.tensor_tensor(w[:, :, 0:b], w[:, :, 0:b], k3[:, :, 0:b], ALU.mult))
                    z = Z[:, 0, :].rearrange("p (m w) -> p m w", w=P)
                    c3 = C.rearrange("p (m w) -> p m w", w=P)
                    ref = c3[:, :, P - 1:P].to_broadcast([P, NT, P])
                    own(dve.tensor_tensor(z, ref, c3, ALU.subtract))
                    own.wait()
                    dve.sem_inc(state_w, 1)
                    dve.wait_ge(own_a, 3 * (g + 1))
                    own(dve.tensor_tensor(QE, QE, Q[:, g, :], ALU.mult))
                    own(dve.tensor_tensor(KL[:, :], KL[:, :], K[:, g, :], ALU.mult))
                    own(dve.memset(ST, 0.0))
                    own.wait()
                    dve.sem_inc(mixed, 1)
                    nu = P // dk // 2
                    for c in range(NT):
                        for u in range(nu):
                            dve.wait_ge(scored, step + 1)
                            if step >= 2:
                                dve.wait_ge(out_done, step - 1)
                            slot = SC[:, step % 2, :, :]
                            banks = kit.psum[:, 2 * (step % 2):2 * (step % 2) + 2, :]
                            own.then(dve.tensor_copy(slot[0:64, :, 64:P], banks[0:64, :, 0:64]))
                            own.then(dve.copy_predicated(slot[64:P, :, 64:P],
                                                    DM[64:P, 64:P].unsqueeze(1).to_broadcast([64, 2, 64]),
                                                    banks[64:P, :, 0:64]))
                            own.then(dve.copy_predicated(slot[0:64, :, 0:64],
                                                    DM[0:64, 0:64].unsqueeze(1).to_broadcast([64, 2, 64]),
                                                    banks[0:64, :, 448:512]))
                            for n, b in enumerate(LEVELS[1:], 1):
                                m = 64 // b
                                own.then(dve.copy_predicated(
                                    slot.rearrange("p h (m w) -> p h m w", w=2 * b)[:, :, :, b:2 * b],
                                    LM[:, n * 64:(n + 1) * 64].rearrange("p (m w) -> p m w", w=b)
                                    .unsqueeze(1).to_broadcast([P, 2, m, b]),
                                    banks[:, 0:2, n * 64:(n + 1) * 64]
                                    .rearrange("p h (m w) -> p h m w", w=b)))
                            dve.sem_inc(placed, 1)
                            step += 1
                        dve.wait_ge(upd_done, upd + 1)
                        if c < NT - 1:
                            if c >= 1:
                                dve.wait_ge(out_done, nu * c + 8 * uc)
                            for h in range(P // dk):
                                r, v = slice(h * dk, (h + 1) * dk), slice(h * 64, (h + 1) * 64)
                                last = dve.scalar_tensor_tensor(
                                    ST[r, (c + 1) % 2, v], ST[r, c % 2, v], EL[r, c:c + 1],
                                    kit.psum[r, 7, v], ALU.mult, ALU.add)
                            last.then_inc(upd_taken, 1)
                            dve.wait_ge(upd_taken, (NT - 1) * g + c + 1)
                        upd += 1
                    uc += nu

            @block.scalar
            def _(act):
                own = Own(act, own_a)
                for g, dk, _ in tiles:
                    act.wait_ge(cums, g + 1)
                    for n, b in enumerate(LEVELS):
                        act.wait_ge(refs, NL * g + n + 1)
                        z = Z[:, n % 2, :].rearrange("p (m w) -> p m w", w=2 * b)
                        w = QK[:, n, :].rearrange("p (m w) -> p m w", w=2 * b)
                        act.activation(w[:, :, b:2 * b], z[:, :, b:2 * b], ACT.Exp)
                        act.activation(w[:, :, 0:b], z[:, :, 0:b], ACT.Exp, scale=-1.0).then_inc(weights, 1)
                    act.wait_ge(state_w, g + 1)
                    own(act.activation(QE, C, ACT.Exp))
                    own(act.activation(KL[:, :], Z[:, 0, :], ACT.Exp))
                    own(act.activation(EL[:, :].unsqueeze(2),
                                       C.rearrange("p (m w) -> p m w", w=P)[:, :, P - 1:P], ACT.Exp))
                    for c in range(2):
                        act.wait_ge(kt_done, 2 * g + c + 1)
                        act.activation(KLT[:, c * HALF:(c + 1) * HALF], kit.psum[:, 6, :], ACT.Copy
                                       ).then_inc(kt_taken, 1)
                    nu = P // dk // 2
                    done = [0, 8, 16][g]
                    vw = 64 * (P // dk)
                    at = 128 * g
                    for c in range(NT):
                        act.wait_ge(out_done, done + nu * (c + 1))
                        act.activation(O[:, c, at:at + vw], kit.psum[:, 6, 0:vw], ACT.Copy
                                       ).then_inc(out_taken, 1)

            @block.tensor
            def _(pe):
                step = 0
                for g, dk, _ in tiles:
                    nu = P // dk // 2
                    vw = 64 * (P // dk)
                    V = vals(g)
                    v_at = 128 * g if g < 2 else 0
                    pe.wait_ge(mixed, g + 1)
                    for c in range(2):
                        if c or g:
                            pe.wait_ge(kt_taken, 2 * g + c)
                            pe.wait_ge(out_taken, NT * g) if g else None
                        for n in range(4):
                            m = 4 * c + n
                            last = pe.transpose(kit.psum[:, 6, n * P:(n + 1) * P], KL[:, m * P:(m + 1) * P], ident)
                        last.then_inc(kt_done, 1)
                    pe.wait_ge(kt_taken, 2 * g + 2)

                    def scores(c, u, step):
                        if step >= 2:
                            pe.wait_ge(placed, step - 1)
                        banks = kit.psum[:, 2 * (step % 2):2 * (step % 2) + 2, :]
                        for h in range(2):
                            rows = slice((2 * u + h) * dk, (2 * u + h + 1) * dk)
                            k = K[rows, g, c * P:(c + 1) * P]
                            q = Q[rows, g, c * P:(c + 1) * P]
                            w = QK[rows, 0, c * P:(c + 1) * P]
                            pe.matmul(banks[0:64, h, 0:64], w[:, 0:64], w[:, 64:P], start=True, stop=True)
                            pe.matmul(banks[64:P, h, 0:64], k[:, 64:P], q[:, 64:P], start=True, stop=True)
                            pe.matmul(banks[0:64, h, 448:512], k[:, 0:64], q[:, 0:64], start=True, stop=True)
                            for n, b in enumerate(LEVELS[1:], 1):
                                w = QK[rows, n, c * P:(c + 1) * P]
                                last = pe.matmul(
                                    banks[:, h, n * 64:(n + 1) * 64].rearrange("p (m w) -> p m w", w=b),
                                    w, w.rearrange("p (m w) -> p m w", w=2 * b)[:, :, b:2 * b],
                                    start=True, stop=True)
                        last.then_inc(scored, 1)

                    order = [(c, u) for c in range(NT) for u in range(nu)]
                    scores(*order[0], step)
                    for i, (c, u) in enumerate(order):
                        if i + 1 < len(order):
                            scores(*order[i + 1], step + 1)
                        if u == 0:
                            n_upd = (NT - 1) * g + c
                            if n_upd:
                                pe.wait_ge(upd_taken, n_upd)
                            pe.matmul(kit.psum[:, 7, 0:vw], KLT[:, c * P:(c + 1) * P],
                                      V[:, c, v_at:v_at + vw], start=True, stop=True).then_inc(upd_done, 1)
                            if c >= 1 or g:
                                pe.wait_ge(out_taken, NT * g + c)
                        pe.wait_ge(placed, step + 1)
                        if u == 0:
                            pe.matmul(kit.psum[:, 6, 0:vw], QE[:, c * P:(c + 1) * P], ST[:, c % 2, 0:vw],
                                      start=True, stop=False)
                        for h in range(2):
                            head = 2 * u + h
                            last = pe.matmul(kit.psum[:, 6, head * 64:(head + 1) * 64], SC[:, step % 2, h, :],
                                             V[:, c, v_at + head * 64:v_at + (head + 1) * 64], start=False,
                                             stop=head == 2 * nu - 1)
                        last.then_inc(out_done, 1)
                        step += 1


def head_norm_stage(kit, tag, O, parts, heads, width, gains, eps, copies, ident, scale=None, silu=True):
    nc = kit.nc
    gain_in, sq, root, gated, sums, rows, turned, copied, own_d = (
        kit.sem(f"{tag}_{n}") for n in ("gain_in", "sq", "root", "gated", "sums", "rows", "turned", "copied",
                                        "own_d"))
    W = heads * width
    with ExitStack() as mem:
        G = sbuf(nc, mem, f"{tag}_G", [P, W])
        SQ = sbuf(nc, mem, f"{tag}_SQ", [P, 2, W])
        ss = sbuf(nc, mem, f"{tag}_ss", [P, NT, heads])
        eps_col = sbuf(nc, mem, f"{tag}_eps", [P, 1])
        with nc.Block() as block:
            @block.sync
            def _(sp):
                at = 0
                for g, n in gains:
                    sp.dma_start(G[:, at:at + n], bcast(g)).then_inc(gain_in, 16)
                    at += n

            @block.scalar
            def _(act):
                for t in range(NT):
                    if t >= 2:
                        act.wait_ge(sums, t - 1)
                    act.activation(SQ[:, t % 2, :], O[:, t, 0:W], ACT.Square).then_inc(sq, 1)
                act.wait_ge(sums, NT)
                act.activation(ss, ss, ACT.Sqrt, scale=1.0 / width, bias=eps_col).then_inc(root, 1)
                if silu:
                    for at, n, gate in parts:
                        act.activation(gate, gate, ACT.Silu).then_inc(gated, 1)
                for t in range(NT):
                    act.wait_ge(turned, t + 1)
                    for n, (_, dst) in enumerate(copies):
                        ins = act.activation(dst[:, t * P:(t + 1) * P],
                                             kit.pair(t % 2)[:, n * P:(n + 1) * P], ACT.Copy)
                    ins.then_inc(copied, 1)

            @block.vector
            def _(dve):
                own = Own(dve, own_d)
                own(dve.memset(eps_col, eps))
                own.wait()
                dve.wait_ge(gain_in, 16 * len(gains))
                if scale is not None:
                    own.then(dve.tensor_scalar(G, G, scale, None, ALU.mult))
                for t in range(NT):
                    dve.wait_ge(sq, t + 1)
                    dve.tensor_reduce(ss[:, t, :], SQ[:, t % 2, :].rearrange("p (h w) -> p h w", h=heads),
                                      AX.X, ALU.add).then_inc(sums, 1)
                dve.wait_ge(root, 1)
                own.then(dve.reciprocal(ss, ss))
                if silu:
                    dve.wait_ge(gated, len(parts))
                for t in range(NT):
                    o = O[:, t, 0:W].rearrange("p (h w) -> p h w", h=heads)
                    own.then(dve.tensor_tensor(o, o, ss[:, t, :].unsqueeze(2).to_broadcast([P, heads, width]),
                                               ALU.mult))
                    own.then(dve.tensor_tensor(O[:, t, 0:W], O[:, t, 0:W], G, ALU.mult))
                    for n, (at, w, gate) in enumerate(parts):
                        ins = dve.tensor_tensor(O[:, t, at:at + w], O[:, t, at:at + w], gate[:, t, :], ALU.mult)
                    ins.then_inc(rows, 1)

            @block.tensor
            def _(pe):
                for t in range(NT):
                    pe.wait_ge(rows, t + 1)
                    if t >= 2:
                        pe.wait_ge(copied, t - 1)
                    for n, (c, _) in enumerate(copies):
                        last = pe.transpose(kit.pair(t % 2)[:, n * P:(n + 1) * P],
                                            O[:, t, c * P:(c + 1) * P], ident)
                    last.then_inc(turned, 1)


def residual_stage(kit, tag, tiles, w_view, X, alpha, chunk):
    nc = kit.nc
    K = len(tiles)
    n_chunks = D // chunk
    w_in = [kit.sem(f"{tag}_w_in{s}") for s in range(2)]
    products, added = kit.sem(f"{tag}_products"), kit.sem(f"{tag}_added")
    with ExitStack() as mem:
        W = sbuf(nc, mem, f"{tag}_W", [P, 2, K, chunk])
        with nc.Block() as block:
            @block.sync
            def _(sp):
                for c in range(n_chunks):
                    if c >= 2:
                        sp.wait_ge(products, NT * (c - 1))
                    sp.dma_start(W[:, c % 2, :, :], w_view[:, :, c * chunk:(c + 1) * chunk]
                                 ).then_inc(w_in[c % 2], 16)

            @block.tensor
            def _(pe):
                for c in range(n_chunks):
                    pe.wait_ge(w_in[c % 2], 16 * (c // 2 + 1))
                    for t in range(NT):
                        n = c * NT + t
                        if n >= 8:
                            pe.wait_ge(added, n - 7)
                        for k in range(K):
                            last = pe.matmul(kit.psum[:, n % 8, 0:chunk], tiles[k][:, t * P:(t + 1) * P],
                                             W[:, c % 2, k, :], start=k == 0, stop=k == K - 1)
                        last.then_inc(products, 1)

            @block.vector
            def _(dve):
                for n in range(n_chunks * NT):
                    c, t = divmod(n, NT)
                    dve.wait_ge(products, n + 1)
                    x = X[:, t, c * chunk:(c + 1) * chunk]
                    dve.scalar_tensor_tensor(x, x, alpha, kit.psum[:, n % 8, 0:chunk], ALU.mult, ALU.add
                                             ).then_inc(added, 1)


def ffn_stage(kit, XT, PROD, d):
    nc = kit.nc
    SLOTS = 3
    w_in = [kit.sem(f"ffn_w_in{s}") for s in range(2 * SLOTS)]
    params, padded, products, gate_out, conv, gelu, prod, own_d = (
        kit.sem(f"ffn_{n}") for n in ("params", "padded", "products", "gate_out", "conv", "gelu", "prod", "own_d"))
    with ExitStack() as mem:
        W = sbuf(nc, mem, "ffn_W", [P, SLOTS, 2, KT * P])
        par = sbuf(nc, mem, "ffn_par", [P, 4, FT])
        G = sbuf(nc, mem, "ffn_G", [P, SLOTS, 2 + S])
        Y = sbuf(nc, mem, "ffn_Y", [P, SLOTS, S])
        with nc.Block() as block:
            @block.sync
            def _(sp):
                with nc.allow_non_contiguous_dma(reason="per-channel parameters"):
                    for n in range(4):
                        src = d["ffn_conv_w"][n] if n < 3 else d["ffn_conv_b"]
                        sp.dma_start(par[:, n, :], src.rearrange("(f p) -> p f", p=P)).then_inc(params, 16)
                for s in range(SLOTS):
                    for n, w in enumerate(("ffn_w_gate", "ffn_w_val")):
                        sp.dma_start(W[:, s, n, :], d[w][s]).then_inc(w_in[2 * s + n], 16)
                with sp.Fori(1, FT // SLOTS) as i:
                    for s in range(SLOTS):
                        for n, w in enumerate(("ffn_w_gate", "ffn_w_val")):
                            sp.wait_ge(products, 2 * (SLOTS * i + s - SLOTS) + n + 1)
                            sp.dma_start(W[:, s, n, :], d[w][SLOTS * i + s]).then_inc(w_in[2 * s + n], 16)

            def product(pe, s, n, pair):
                w = W[:, s, n, :].rearrange("p (k m) -> p k m", k=KT)
                for c in range(2):
                    for k in range(KT):
                        last = pe.matmul(kit.pair(pair)[:, c * HALF:(c + 1) * HALF], w[:, k, :],
                                         XT[:, k, c * HALF:(c + 1) * HALF], start=k == 0, stop=k == KT - 1)
                last.then_inc(products, 1)

            @block.tensor
            def _(pe):
                for f in range(2):
                    for n in range(2):
                        pe.wait_ge(w_in[2 * f + n], 16)
                        product(pe, f, n, 2 * n + f)
                n_loop = (FT - 3) // 6
                with pe.Fori(0, n_loop) as i:
                    for j in range(6):
                        s = (j + 2) % SLOTS
                        pe.wait_ge(w_in[2 * s], 16 * (2 * i + (j + 2) // SLOTS + 1))
                        pe.wait_ge(gate_out, 6 * i + j + 1)
                        product(pe, s, 0, j % 2)
                        pe.wait_ge(w_in[2 * s + 1], 16 * (2 * i + (j + 2) // SLOTS + 1))
                        pe.wait_ge(prod, 6 * i + j + 1)
                        product(pe, s, 1, 2 + j % 2)
                for f in range(6 * n_loop + 2, FT):
                    s = f % SLOTS
                    pe.wait_ge(w_in[2 * s], 16 * (f // SLOTS + 1))
                    pe.wait_ge(gate_out, f - 1)
                    product(pe, s, 0, f % 2)
                    pe.wait_ge(w_in[2 * s + 1], 16 * (f // SLOTS + 1))
                    pe.wait_ge(prod, f - 1)
                    product(pe, s, 1, 2 + f % 2)

            @block.scalar
            def _(act):
                act.wait_ge(padded, 1)

                def take_gate(f, s, pair, guard):
                    act.wait_ge(products, 2 * f + 1)
                    if guard:
                        act.wait_ge(conv, f - SLOTS + 1)
                    act.activation(G[:, s, 2:2 + S], kit.pair(pair), ACT.Copy).then_inc(gate_out, 1)

                def bend(f, s):
                    act.wait_ge(conv, f + 1)
                    act.activation(Y[:, s, :], Y[:, s, :], ACT.Gelu_apprx_tanh).then_inc(gelu, 1)

                for f in range(SLOTS):
                    take_gate(f, f, f % 2, False)
                    if f >= 1:
                        bend(f - 1, f - 1)
                n_loop = (FT - SLOTS) // 6
                with act.Fori(0, n_loop) as i:
                    for j in range(6):
                        take_gate(6 * i + (j + SLOTS), j % SLOTS, (j + SLOTS) % 2, True)
                        bend(6 * i + (j + SLOTS - 1), (j + SLOTS - 1) % SLOTS)
                for f in range(SLOTS + 6 * n_loop, FT):
                    take_gate(f, f % SLOTS, f % 2, True)
                    bend(f - 1, (f - 1) % SLOTS)
                bend(FT - 1, (FT - 1) % SLOTS)

            def finish(dve, f):
                dve.wait_ge(gelu, f + 1)
                dve.wait_ge(products, 2 * f + 2)
                dve.tensor_tensor(PROD[:, f, :], Y[:, f % SLOTS, :], kit.pair(2 + f % 2), ALU.mult
                                  ).then_inc(prod, 1)

            @block.vector
            def _(dve):
                own = Own(dve, own_d)
                dve.memset(G[:, :, 0:2], 0.0).then_inc(padded, 1)
                dve.wait_ge(params, 64)
                for f in range(FT):
                    s = f % SLOTS
                    dve.wait_ge(gate_out, f + 1)
                    if f >= SLOTS:
                        dve.wait_ge(prod, f - SLOTS + 1)
                    g = G[:, s, :]
                    own.then(dve.tensor_scalar(Y[:, s, :], g[:, 2:2 + S], par[:, 2, f:f + 1],
                                               par[:, 3, f:f + 1], ALU.mult, ALU.add))
                    own.then(dve.scalar_tensor_tensor(Y[:, s, :], g[:, 0:S], par[:, 0, f:f + 1], Y[:, s, :],
                                                      ALU.mult, ALU.add))
                    dve.scalar_tensor_tensor(Y[:, s, :], g[:, 1:1 + S], par[:, 1, f:f + 1], Y[:, s, :],
                                             ALU.mult, ALU.add).then_inc(conv, 1)
                    if f >= 1:
                        finish(dve, f - 1)
                finish(dve, FT - 1)


def first_block(kit, X, XT, C, d):
    nc = kit.nc
    ident = C("ident")
    tables = ExitStack()
    FIRST = sbuf(nc, tables, "FIRST", [P, ROPE_AT - FIRST_AT])
    level, keep = FIRST[:, 0:7 * 64], FIRST[:, 7 * 64:]
    first_in = kit.sem("first_in")
    with nc.Block() as block:
        @block.sync
        def _(sp):
            sp.dma_start(FIRST, d["constants"][:, FIRST_AT:ROPE_AT]).then_inc(first_in, 16)
            sp.wait_ge(first_in, 16)
    norm_stage(kit, "mixnorm", X, XT, ident, d["norm_mix"])
    mix = ExitStack()
    with mix:
        BG = sbuf(nc, mix, "BG", [P, 4, S])
        gla = ExitStack()
        VA = sbuf(nc, gla, "VA", [P, NT, 512])
        VC = sbuf(nc, gla, "VC", [P, NT, 512])
        Q = sbuf(nc, gla, "Q", [P, 3, S])
        K = sbuf(nc, gla, "K", [P, 3, S])
        AF = sbuf(nc, gla, "AF", [P, 2, S])
        CLR = sbuf(nc, gla, "CLR", [16, S])
        lru = ExitStack()
        BX = sbuf(nc, lru, "BX", [P, 4, 3 + S])
        dst = ([Q[:, 0, :], Q[:, 1, :], AF[:, 0, :], AF[:, 1, :]] + [BX[:, j, 3:3 + S] for j in range(4)]
               + [BG[:, j, :] for j in range(4)] + [Q[:, 2, :], K[:, 2, :]])
        items = [(d["w_in_feat"][m], S) for m in range(14)] + [(d["w_in_lr"], KT * 16)]
        items += [(d["w_in_tok"][k * P:(k + 1) * P, :], 1024) for k in range(KT)]
        units = []
        for m in range(14):
            scale = 32 ** -0.5 if m == 12 else 1.0
            take = copy_into(dst[m], scale=scale) if m % 2 == 0 else copy_into_dve(dst[m])
            units.append(Unit("feature", [m], P, "act" if m % 2 == 0 else "dve", take))
        units.append(Unit("feature", [14], 16, "act", copy_into(CLR[:, :], rows=16)))
        for t in range(NT):
            def take(eng, psum, own, t=t):
                if t % 2:
                    own(eng.tensor_copy(VA[:, t, :], psum[:, 0:512]))
                    return eng.tensor_copy(VC[:, t, :], psum[:, 512:1024])
                eng.activation(VA[:, t, :], psum[:, 0:512], ACT.Copy)
                return eng.activation(VC[:, t, :], psum[:, 512:1024], ACT.Copy)
            units.append(Unit("token", list(range(15, 23)), 1024, "dve" if t % 2 else "act", take, t))
        product_stage(kit, "win", XT, items, units)
        pad = kit.sem("pad")
        with nc.Block() as block:
            @block.gpsimd
            def _(pool):
                pool.memset(BX[:, :, 0:3], 0.0).then_inc(pad, 1)
        rglru_stage(kit, BX, BG, XT, K[:, 0, :], d)
        lru.close()
        OM = sbuf(nc, gla, "OM", [P, NT, 512])
        LF = sbuf(nc, gla, "LF", [P, 3, S])
        gate_prep_stage(kit, AF, K[:, 0:2, :], CLR, LF, XT, d)
        gla_stage(kit, Q, K, LF, VA, VC, OM, XT, AF, ident, level, keep)
        OT = XT
        head_norm_stage(kit, "hn", OM, [(0, 256, VA[:, :, 256:512]), (256, 256, VC[:, :, 256:512])], 8, 64,
                        [(d["hgrn_norm"], 256), (d["gla_norm"], 256)], EPS,
                        [(n, OT[:, n, :]) for n in range(4)], ident)
        gla.close()
        tiles = [OT[:, 0, :], OT[:, 1, :]] + [BG[:, j, :] for j in range(4)] + [OT[:, 2, :], OT[:, 3, :]]
        residual_stage(kit, "wout", tiles, d["w_out"].rearrange("(k p) n -> p k n", p=P), X, 1.0, 512)
    tables.close()
    norm_stage(kit, "ffnnorm", X, XT, ident, d["norm_ffn"])
    with ExitStack() as mem:
        PROD = sbuf(nc, mem, "PROD", [P, FT, S])
        ffn_stage(kit, XT, PROD, d)
        residual_stage(kit, "down", [PROD[:, f, :] for f in range(FT)],
                       d["ffn_w_down"].rearrange("(k p) n -> p k n", p=P), X, 1.0, 256)
    norm_stage(kit, "finalnorm", X, XT, ident, d["norm_final"], keep=True)
    kit.clear_semaphores()


def keys_at(t):
    return P * t * (t + 1) // 2


KEYS = keys_at(NT)


def index_stage(kit, IQ, IW, IS, AM, causal):
    nc = kit.nc
    scored, bent, added, done, own_d = (kit.sem(f"ix_{n}") for n in ("scored", "bent", "added", "done", "own_d"))
    H = 8
    with ExitStack() as mem:
        R = sbuf(nc, mem, "ix_R", [P, 2, S])
        with nc.Block() as block:
            @block.tensor
            def _(pe):
                for t in range(NT):
                    n = P * (t + 1)
                    for h in range(H):
                        j = t * H + h
                        if j >= 2:
                            pe.wait_ge(bent, j - 1)
                        for c in range(0, n, HALF):
                            e = min(n, c + HALF)
                            last = pe.matmul(kit.pair(j % 2)[:, c:e], IQ[:, h // 2, t * P:(t + 1) * P],
                                             IQ[:, 4 + h % 2, c:e], start=True, stop=True)
                        last.then_inc(scored, 1)

            @block.scalar
            def _(act):
                for j in range(NT * H):
                    n = P * (j // H + 1)
                    act.wait_ge(scored, j + 1)
                    if j >= 2:
                        act.wait_ge(added, j - 1)
                    act.activation(R[:, j % 2, 0:n], kit.pair(j % 2)[:, 0:n], ACT.Relu).then_inc(bent, 1)

            @block.vector
            def _(dve):
                own = Own(dve, own_d)
                for t in range(NT):
                    n = P * (t + 1)
                    acc = kit.pair(2 + t % 2)[:, 0:n]
                    out = IS[:, keys_at(t):keys_at(t) + n]
                    for h in range(H):
                        j = t * H + h
                        dve.wait_ge(bent, j + 1)
                        if h:
                            dve.wait_ge(added, j)
                            ins = dve.scalar_tensor_tensor(out if h == H - 1 else acc, R[:, j % 2, 0:n],
                                                           IW[:, t, h:h + 1], acc, ALU.mult, ALU.add)
                        else:
                            ins = dve.tensor_scalar(acc, R[:, j % 2, 0:n], IW[:, t, h:h + 1], None, ALU.mult)
                        ins.then_inc(added, 1)
                    dve.wait_ge(added, (t + 1) * H)
                    own.then(dve.tensor_reduce(AM[:, t:t + 1], out, AX.X, ALU.max, apply_absolute_value=True))
                    dve.tensor_tensor(out[:, t * P:n], out[:, t * P:n], causal, ALU.add).then_inc(done, 1)
                dve.wait_ge(done, NT)


def topk_program(kit, mem, IS, AM, MB, A, B, R, causal):
    nc = kit.nc
    T0 = TOPK // P
    N = NT - T0
    own_d = kit.sem("tk_own_d")
    lo, hi, mid, cnt, left = (sbuf(nc, mem, f"tk_{n}", [P, N]) for n in ("lo", "hi", "mid", "cnt", "left"))
    ge = sbuf(nc, mem, "tk_ge", [P, 2, N], INT32)
    one = sbuf(nc, mem, "tk_one", [P, 1], BF16)

    def program(dve):
        own = Own(dve, own_d)
        own(dve.memset(one, 1.0))
        own(dve.memset(MB[:, 0:keys_at(T0)], 0.0))
        own.wait()
        for t in range(T0):
            own(dve.tensor_copy(MB[:, keys_at(t) + t * P:keys_at(t) + (t + 1) * P], causal))
        own(dve.tensor_scalar(lo, AM[:, T0:NT], -1.0, None, ALU.mult))
        own(dve.tensor_scalar(hi, AM[:, T0:NT], 1.0 + 2.0 ** -20, 1e-37, ALU.mult, ALU.add))
        own.wait()
        for i in range(BISECTIONS):
            own.then(dve.tensor_tensor(mid, lo, hi, ALU.add))
            own.then(dve.tensor_scalar(mid, mid, 0.5, None, ALU.mult))
            for t in range(T0, NT):
                n = P * (t + 1)
                own(dve.tensor_scalar(A[:, 0:n] if t % 2 else B[:, 0:n], IS[:, keys_at(t):keys_at(t) + n],
                                      mid[:, t - T0:t - T0 + 1], 0.0, ALU.is_ge, ALU.add,
                                      accum_out=cnt[:, t - T0:t - T0 + 1]))
                if t % 2:
                    own.wait()
            own.wait()
            own(dve.tensor_scalar(ge[:, 0, :], cnt, float(TOPK), None, ALU.is_ge))
            own(dve.tensor_scalar(ge[:, 1, :], cnt, float(TOPK), None, ALU.is_lt))
            own.wait()
            own(dve.copy_predicated(lo, ge[:, 0, :], mid))
            own(dve.copy_predicated(hi, ge[:, 1, :], mid))
            own.wait()
        for t in range(T0, NT):
            n = P * (t + 1)
            m = t - T0
            s = IS[:, keys_at(t):keys_at(t) + n]
            own(dve.tensor_scalar(A[:, 0:n], s, hi[:, m:m + 1], 0.0, ALU.is_ge, ALU.add,
                                  accum_out=cnt[:, m:m + 1]))
            own(dve.tensor_scalar(B[:, 0:n], s, lo[:, m:m + 1], None, ALU.is_ge))
            own.wait()
            own(dve.tensor_scalar(left[:, m:m + 1], cnt[:, m:m + 1], -1.0, float(TOPK), ALU.mult, ALU.add))
            own.then(dve.tensor_tensor(B[:, 0:n], B[:, 0:n], A[:, 0:n], ALU.subtract))
            own.then(dve.tensor_tensor_scan(R[:, 0:n], one.to_broadcast([P, n]), B[:, 0:n], 0.0, ALU.mult, ALU.add))
            own.then(dve.scalar_tensor_tensor(B[:, 0:n], R[:, 0:n], left[:, m:m + 1], B[:, 0:n],
                                              ALU.is_le, ALU.mult))
            own.then(dve.tensor_tensor(A[:, 0:n], A[:, 0:n], B[:, 0:n], ALU.add))
            own.then(dve.tensor_scalar(MB[:, keys_at(t):keys_at(t) + n], A[:, 0:n], 1.0, -NEG,
                                       ALU.subtract, ALU.mult))
    return program


def clear_stage(kit, tag, tiles):
    done = kit.sem(f"{tag}_done")
    with kit.nc.Block() as block:
        @block.gpsimd
        def _(pool):
            for t in tiles:
                pool.memset(t, 0.0).then_inc(done, 1)


def attend_stage(kit, tag, heads, q, k, v, dv, O, out_at, ident, identb, mask, masked_all, decay=None,
                 minus_lam=None, v_at=lambda h: 0):
    nc = kit.nc
    maps = 2 if minus_lam is not None else 1
    jobs = [(t, h) for t in range(NT) for h in range(heads)]
    J = len(jobs)
    RING = 3
    LAG = 2 if maps == 2 else 1
    groups = []
    for j, (t, h) in enumerate(jobs):
        for b in range(0, t + 1, 4):
            groups.append((j, b, min(t + 1, b + 4)))
    scored, greatest, exped, ready, turned, taken_a, taken_v, summed, out, own_d = (
        kit.sem(f"{tag}_{n}") for n in ("scored", "greatest", "exped", "ready", "turned", "taken_a", "taken_v",
                                        "summed", "out", "own_d"))

    def groups_of(j):
        return [g for g, (jj, _, _) in enumerate(groups) if jj == j]

    with ExitStack() as mem:
        PR = sbuf(nc, mem, f"{tag}_PR", [P, RING, maps, S])
        PT = sbuf(nc, mem, f"{tag}_PT", [P, 2, NT, P])
        nmax = sbuf(nc, mem, f"{tag}_nmax", [P, J, maps])
        sums = sbuf(nc, mem, f"{tag}_sums", [P, J, maps])
        inv = sbuf(nc, mem, f"{tag}_inv", [P, J, 2 * maps - 1])
        with nc.Block() as block:
            @block.tensor
            def _(pe):
                def scores(j):
                    t, h = jobs[j]
                    n = P * (t + 1)
                    for m in range(maps):
                        i = j * maps + m
                        if i >= 2:
                            pe.wait_ge(exped, i - 1)
                        for c in range(0, n, HALF):
                            e = min(n, c + HALF)
                            dst = kit.pair(i % 2)
                            more = masked_all or e == n
                            pe.matmul(dst[:, c:e], q(h, m, t), k(h, m, c, e), start=True,
                                      stop=not (more or decay))
                            if decay:
                                lhs, rhs = decay(h, c, e)
                                last = pe.matmul(dst[:, c:e], lhs, rhs, start=False, stop=not more)
                            if more:
                                a = c if masked_all else t * P
                                last = pe.matmul(dst[:, a:e], identb, mask(t, a, e), start=False, stop=True)
                        last.then_inc(scored, 1)

                def turn(j):
                    if maps == 2:
                        pe.wait_ge(ready, j + 1)
                    else:
                        pe.wait_ge(exped, j + 1)
                    for g in groups_of(j):
                        _, b0, b1 = groups[g]
                        if g >= 2:
                            pe.wait_ge(taken_v if g % 2 else taken_a, g // 2)
                        for b in range(b0, b1):
                            last = pe.transpose(kit.psum[:, 4 + g % 2, (b - b0) * P:(b - b0 + 1) * P],
                                                PR[:, j % RING, 0, b * P:(b + 1) * P], ident)
                        last.then_inc(turned, 1)

                def weigh(j):
                    t, h = jobs[j]
                    g = groups_of(j)[-1]
                    pe.wait_ge(taken_a, g // 2 + 1)
                    if g:
                        pe.wait_ge(taken_v, (g + 1) // 2)
                    if j >= 2:
                        pe.wait_ge(out, j - 1)
                    for b in range(t + 1):
                        last = pe.matmul(kit.psum[:, 6 + j % 2, 0:P], PT[:, j % 2, b, :], v(h, b),
                                         start=b == 0, stop=b == t)
                    last.then_inc(summed, 1)

                for j in range(J + LAG + 1):
                    if j < J:
                        scores(j)
                    if 0 <= j - LAG < J:
                        turn(j - LAG)
                    if 0 <= j - LAG - 1 < J:
                        weigh(j - LAG - 1)

            def take_group(eng, g, sem, copy):
                j, b0, b1 = groups[g]
                eng.wait_ge(turned, g + 1)
                if j >= 2:
                    eng.wait_ge(summed, j - 1)
                copy(PT[:, j % 2, b0:b1, :].rearrange("p b n -> p (b n)"),
                     kit.psum[:, 4 + g % 2, 0:(b1 - b0) * P]).then_inc(sem, 1)

            @block.scalar
            def _(act):
                for j in range(J + LAG):
                    if j < J:
                        n = P * (jobs[j][0] + 1)
                        if j >= RING:
                            act.wait_ge(turned, groups_of(j - RING)[-1] + 1)
                        for m in range(maps):
                            i = j * maps + m
                            act.wait_ge(greatest, i + 1)
                            act.activation(PR[:, j % RING, m, 0:n], kit.pair(i % 2)[:, 0:n], ACT.Exp,
                                           bias=nmax[:, j, m:m + 1], accum_out=sums[:, j, m:m + 1]
                                           ).then_inc(exped, 1)
                    if j >= LAG:
                        for g in groups_of(j - LAG):
                            if g % 2 == 0:
                                take_group(act, g, taken_a, lambda o, i: act.activation(o, i, ACT.Copy))

            @block.vector
            def _(dve):
                own = Own(dve, own_d)

                def maxima(j):
                    n = P * (jobs[j][0] + 1)
                    for m in range(maps):
                        i = j * maps + m
                        dve.wait_ge(scored, i + 1)
                        dve.tensor_reduce(nmax[:, j, m:m + 1], kit.pair(i % 2)[:, 0:n], AX.X, ALU.max,
                                          negate=True).then_inc(greatest, 1)

                def norms(j):
                    dve.wait_ge(exped, (j + 1) * maps)
                    own(dve.reciprocal(inv[:, j, 0:maps], sums[:, j, :]))
                    if maps == 2:
                        n = P * (jobs[j][0] + 1)
                        own.wait()
                        own.then(dve.scalar_tensor_tensor(inv[:, j, 2:3], sums[:, j, 0:1], inv[:, j, 1:2],
                                                          minus_lam, ALU.mult, ALU.mult))
                        dve.scalar_tensor_tensor(PR[:, j % RING, 0, 0:n], PR[:, j % RING, 1, 0:n],
                                                 inv[:, j, 2:3], PR[:, j % RING, 0, 0:n],
                                                 ALU.mult, ALU.add).then_inc(ready, 1)

                def result(j):
                    t, h = jobs[j]
                    at = out_at + h * dv
                    dve.wait_ge(summed, j + 1)
                    a = v_at(h)
                    dve.tensor_scalar(O[:, t, at:at + dv], kit.psum[:, 6 + j % 2, a:a + dv], inv[:, j, 0:1], None,
                                      ALU.mult).then_inc(out, 1)

                for j in range(J + LAG + 1):
                    if j < J:
                        maxima(j)
                    if 0 <= j - 1 < J:
                        norms(j - 1)
                    if 0 <= j - LAG < J:
                        for g in groups_of(j - LAG):
                            if g % 2:
                                take_group(dve, g, taken_v, lambda o, i: dve.tensor_copy(o, i))
                    if 0 <= j - LAG - 1 < J:
                        own.wait()
                        result(j - LAG - 1)


def prepare_stage(kit, l, LAM, IW, VS, FF, identb, causalb, ident, causal, d):
    nc = kit.nc
    params, ff, exps, own_d, own_a = (kit.sem(f"pr_{n}") for n in ("params", "ff", "exps", "own_d", "own_a"))
    with ExitStack() as mem:
        LV = sbuf(nc, mem, "pr_LV", [P, 4, 64])
        dots = sbuf(nc, mem, "pr_dots", [P, 2])
        init = sbuf(nc, mem, "pr_init", [P, 2])
        bf = sbuf(nc, mem, "pr_bf", [4, 1])
        E = sbuf(nc, mem, "pr_E", [4, S])
        ones = sbuf(nc, mem, "pr_ones", [4, S])
        with nc.Block() as block:
            @block.sync
            def _(sp):
                for n, name in enumerate(("lam_q1_2", "lam_q2_2", "lam_k1_2", "lam_k2_2")):
                    sp.dma_start(LV[:, n, :], bcast(d[name][l])).then_inc(params, 16)
                sp.dma_start(init, bcast(d["lam_init"][l])).then_inc(params, 16)
                with nc.allow_non_contiguous_dma(reason="four gate biases"):
                    sp.dma_start(bf, d["b_f_2"][l].rearrange("(p o) -> p o", o=1)).then_inc(params, 16)

            @block.scalar
            def _(act):
                act.wait_ge(params, 96)
                act.activation(E, FF, ACT.Abs, bias=bf).then_inc(own_a, 1)
                act.wait_ge(own_a, 1)
                act.activation(E, E, ACT.Exp, scale=-1.0).then_inc(own_a, 1)
                act.wait_ge(own_a, 2)
                act.activation(E, E, ACT.Ln, bias=1.0).then_inc(exps, 1)
                act.wait_ge(ff, 1)
                act.activation(dots, dots, ACT.Exp).then_inc(exps, 1)

            @block.vector
            def _(dve):
                own = Own(dve, own_d)
                own(dve.memset(ones, 1.0))
                own(dve.tensor_copy(identb, ident))
                own(dve.tensor_copy(causalb, causal))
                own(dve.tensor_scalar(IW, VS[:, :, 64:72], IDX_SCALE, None, ALU.mult))
                dve.wait_ge(params, 96)
                own.then(dve.tensor_tensor(LV[:, 0:2, :], LV[:, 0:2, :], LV[:, 2:4, :], ALU.mult))
                dve.tensor_reduce(dots, LV[:, 0:2, :], AX.X, ALU.add).then_inc(ff, 1)
                dve.wait_ge(exps, 1)
                own.then(dve.tensor_scalar(FF, FF, bf, 0.0, ALU.add, ALU.min))
                own.then(dve.tensor_tensor(FF, FF, E, ALU.subtract))
                own(dve.tensor_tensor_scan(FF, ones, FF, 0.0, ALU.mult, ALU.subtract))
                dve.wait_ge(exps, 2)
                own.then(dve.tensor_tensor(LAM[:, 0:1], dots[:, 1:2], dots[:, 0:1], ALU.subtract))
                own(dve.tensor_tensor(LAM[:, 0:1], LAM[:, 0:1], init[:, 0:1], ALU.subtract))
                own(dve.tensor_copy(LAM[:, 1:2], init[:, 1:2]))
                own.wait()


def finish_stage(kit, tag, O, GATE, w_out, X, XT, g_subln, keep_scale, ln_g, ln_b, ident):
    nc = kit.nc
    H = 4
    gate_in = [kit.sem(f"{tag}_gate_in{s}") for s in range(2)]
    (w_in, gains, sq, summed, root, inverse, scaled, turned, mixed, products, stats, ln_root, rows, ln_turned,
     copied, own_d) = (kit.sem(f"{tag}_{n}") for n in (
         "w_in", "gains", "sq", "summed", "root", "inverse", "scaled", "turned", "mixed", "products", "stats",
         "ln_root", "rows", "ln_turned", "copied", "own_d"))
    w_in = [w_in, kit.sem(f"{tag}_w_in_second")]
    with ExitStack() as mem:
        W = sbuf(nc, mem, f"{tag}_W", [P, KT, D])
        GT = sbuf(nc, mem, f"{tag}_GT", [P, 2, KT, P])
        SQ = sbuf(nc, mem, f"{tag}_SQ", [P, 2, H * P])
        ss = sbuf(nc, mem, f"{tag}_ss", [P, NT, H])
        G = sbuf(nc, mem, f"{tag}_G", [P, D])
        B = sbuf(nc, mem, f"{tag}_B", [P, D])
        gain = sbuf(nc, mem, f"{tag}_gain", [P, 1])
        eps = sbuf(nc, mem, f"{tag}_eps", [P, 2])
        bn = sbuf(nc, mem, f"{tag}_bn", [P, 2, 6])
        mv = sbuf(nc, mem, f"{tag}_mv", [P, NT, 2])
        dev = sbuf(nc, mem, f"{tag}_dev", [P, NT])
        inv = sbuf(nc, mem, f"{tag}_inv", [P, NT])
        with nc.Block() as block:
            @block.sync
            def _(sp):
                def gates(t):
                    sp.dma_start(GT[:, t % 2], GATE[:, :, t * P:(t + 1) * P]).then_inc(gate_in[t % 2], 16)

                with nc.allow_non_contiguous_dma(reason="one gain per partition"):
                    sp.dma_start(gain, g_subln.rearrange("(p o) -> p o", o=1)).then_inc(gains, 16)
                gates(0)
                for c in range(2):
                    sp.dma_start(W[:, :, c * HALF:(c + 1) * HALF], w_out[:, :, c * HALF:(c + 1) * HALF]
                                 ).then_inc(w_in[c], 16)
                sp.dma_start(G, bcast(ln_g)).then_inc(gains, 16)
                sp.dma_start(B, bcast(ln_b)).then_inc(gains, 16)
                gates(1)
                for t in range(2, NT):
                    sp.wait_ge(mixed, t - 1)
                    gates(t)

            @block.scalar
            def _(act):
                for t in range(NT):
                    if t >= 2:
                        act.wait_ge(summed, t - 1)
                    act.activation(SQ[:, t % 2, :], O[:, t, 0:H * P], ACT.Square).then_inc(sq, 1)
                act.wait_ge(summed, NT + 1)
                act.activation(ss, ss, ACT.Sqrt, scale=1.0 / P, bias=eps[:, 0:1]).then_inc(root, 1)
                act.wait_ge(inverse, 1)
                for t in range(NT):
                    for h in range(H):
                        o = O[:, t, h * P:(h + 1) * P]
                        ins = act.activation(o, o, ACT.Copy, scale=ss[:, t, h:h + 1])
                    ins.then_inc(scaled, 1)
                for t in range(NT):
                    act.wait_ge(stats, t + 1)
                    act.activation(dev[:, t:t + 1], mv[:, t, 1:2], ACT.Sqrt, bias=eps[:, 1:2]).then_inc(ln_root, 1)
                    act.wait_ge(ln_turned, t + 1)
                    act.activation(XT[:, :, t * P:(t + 1) * P],
                                   kit.pair(1).rearrange("p (k n) -> p k n", k=KT), ACT.Copy).then_inc(copied, 1)

            @block.vector
            def _(dve):
                own = Own(dve, own_d)
                own(dve.memset(eps[:, 0:1], SUBLN_EPS))
                own.then(dve.memset(eps[:, 1:2], LN_EPS))
                for t in range(NT):
                    dve.wait_ge(sq, t + 1)
                    dve.tensor_reduce(ss[:, t, :], SQ[:, t % 2, :].rearrange("p (h w) -> p h w", h=H),
                                      AX.X, ALU.add).then_inc(summed, 1)
                dve.sem_inc(summed, 1)
                dve.wait_ge(gains, 48)
                own.then(dve.tensor_scalar(gain, gain, keep_scale, None, ALU.mult))
                dve.wait_ge(root, 1)
                dve.reciprocal(ss, ss).then_inc(inverse, 1)

                def gate(t):
                    dve.wait_ge(gate_in[t % 2], 16 * (t // 2 + 1))
                    dve.wait_ge(turned, t + 1)
                    psum = kit.pair(0).rearrange("p (k n) -> p k n", k=KT)
                    at = slice(t * P, (t + 1) * P)
                    dve.scalar_tensor_tensor(XT[:, 0:H, at], psum[:, 0:H, :], gain, GT[:, t % 2, 0:H, :],
                                             ALU.mult, ALU.mult)
                    dve.tensor_tensor(XT[:, H:, at], psum[:, H:, :], GT[:, t % 2, H:, :], ALU.mult
                                      ).then_inc(mixed, 1)

                gate(0)
                for t in range(NT):
                    if t + 1 < NT:
                        gate(t + 1)
                    x = X[:, t, :]
                    dve.wait_ge(products, t + 1)
                    own.then(dve.scalar_tensor_tensor(x, x, ALPHA, kit.pair(2 + t % 2), ALU.mult, ALU.add))
                    for n in range(2):
                        own(dve.bn_stats(bn[:, n, :], x[:, n * HALF:(n + 1) * HALF]))
                    own.wait()
                    dve.bn_aggr(mv[:, t, :], bn).then_inc(stats, 1)
                    dve.wait_ge(ln_root, t + 1)
                    own.then(dve.reciprocal(inv[:, t:t + 1], dev[:, t:t + 1]))
                    own.then(dve.tensor_scalar(x, x, mv[:, t, 0:1], inv[:, t:t + 1], ALU.subtract, ALU.mult))
                    own.then(dve.tensor_tensor(x, x, G, ALU.mult))
                    dve.tensor_tensor(x, x, B, ALU.add).then_inc(rows, 1)

            @block.tensor
            def _(pe):
                def turn(t):
                    pe.wait_ge(scaled, t + 1)
                    if t:
                        pe.wait_ge(mixed, t)
                    for k in range(KT):
                        last = pe.transpose(kit.pair(0)[:, k * P:(k + 1) * P], O[:, t, k * P:(k + 1) * P], ident)
                    last.then_inc(turned, 1)

                def turn_norm(t):
                    pe.wait_ge(rows, t + 1)
                    if t:
                        pe.wait_ge(copied, t)
                    for k in range(KT):
                        last = pe.transpose(kit.pair(1)[:, k * P:(k + 1) * P], X[:, t, k * P:(k + 1) * P], ident)
                    last.then_inc(ln_turned, 1)

                turn(0)
                for t in range(NT):
                    if t + 1 < NT:
                        turn(t + 1)
                    else:
                        pe.wait_ge(mixed, NT)
                    if t >= 2:
                        pe.wait_ge(rows, t - 1)
                    for c in range(2):
                        if t == 0:
                            pe.wait_ge(w_in[c], 16)
                        for k in range(KT):
                            last = pe.matmul(kit.pair(2 + t % 2)[:, c * HALF:(c + 1) * HALF],
                                             XT[:, k, t * P:(t + 1) * P], W[:, k, c * HALF:(c + 1) * HALF],
                                             start=k == 0, stop=k == KT - 1)
                    last.then_inc(products, 1)
                    if t:
                        turn_norm(t - 1)
                turn_norm(NT - 1)


def packed(w, c, e):
    return [(w[2 * k * P:(2 * k + 2) * P, c:e].rearrange("(a p) n -> p a n", a=2), 2 * (e - c))
            for k in range(KT // 2)]


def layer(kit, l, X, XT, C, cos, sin, LAM, OM, GATE, d):
    nc = kit.nc
    ident, causal, swap = C("ident"), C("causal"), C("swap")
    pick = C("pick").rearrange("p (h n) -> p h n", h=4)
    w_feat, w_tok = d["w2_feat"][l], d["w2_tok"][l]
    attn = ExitStack()
    with attn:
        identb = sbuf(nc, attn, "identb", [P, P], BF16)
        causalb = sbuf(nc, attn, "causalb", [P, P], BF16)
        early = ExitStack()
        SQ = sbuf(nc, early, "SQ", [P, 4, S])
        FQ = sbuf(nc, early, "FQ", [P, 6, S])
        VS = sbuf(nc, early, "VS", [P, NT, 328])
        FF = sbuf(nc, early, "FF", [4, S])
        AM = sbuf(nc, early, "AM", [P, NT])
        MB = sbuf(nc, early, "MB", [P, KEYS], BF16)
        index = ExitStack()
        IW = sbuf(nc, index, "IW", [P, NT, 8])
        IQ = sbuf(nc, index, "IQ", [P, 6, S])
        items = [(w_feat[m], S) for m in range(8)] + [(d["w2_ff"][l], KT * 4)]
        items += packed(w_tok, 0, 328)
        dst = [SQ[:, 0, :], SQ[:, 1, :], None] + [IQ[:, j, :] for j in range(4)] + [None]
        split = {2: (SQ[:, 2, :], SQ[:, 3, :]), 7: (IQ[:, 4, :], IQ[:, 5, :])}
        units = []

        def take_keys(pair):
            def take(act, psum, own):
                act.activation(FQ[0:64, 2 + 2 * pair, :], psum[0:64, :], ACT.Copy)
                return act.activation(FQ[64:P, 3 + 2 * pair, :], psum[64:P, :], ACT.Copy)
            return take

        for m in range(8):
            units.append(Unit("feature", [m], P, "rope", (dst[m], QK_SCALE if m < 2 else 1.0, split.get(m))))
        units.append(Unit("feature", [8], 4, "act", copy_into(FF, rows=4)))
        for t in range(NT):
            units.append(Unit("token", list(range(9, 13)), 328, "act", copy_into(VS[:, t, :]), t))
        clear_stage(kit, "za", [t[64 * (1 - i % 2):64 * (2 - i % 2), :] for i, t in enumerate(
            [SQ[:, 2, :], SQ[:, 3, :], IQ[:, 4, :], IQ[:, 5, :]] + [FQ[:, 2 + j, :] for j in range(4)])])
        product_stage(kit, "pa", XT, items, units, rope=(cos, sin, swap), place=OM,
                      rot_place=MB[:, 0:4 * S].bitcast(FP32).rearrange("p (a n) -> p a n", a=2))
        prepare_stage(kit, l, LAM, IW, VS, FF, identb, causalb, ident, causal, d)
        IS = OM.rearrange("p t n -> p (t n)")[:, 0:KEYS]
        index_stage(kit, IQ, IW, IS, AM, causal)
        index.close()
        late = ExitStack()
        DV = late.enter_context(nc.sbuf_tensor("DV", [P, NT, 512], FP32, side="right"))[:, :, :]
        with ExitStack() as mem:
            room = OM.rearrange("p t n -> p (t n)")[:, KEYS:]
            staged = [room[:, n * S:(n + 1) * S] for n in range(2)]
            flags = sbuf(nc, mem, "flags", [P, S], BF16)
            topk = topk_program(kit, mem, IS, AM, MB, flags, room[:, 3 * S:3 * S + S // 2].bitcast(BF16),
                                room[:, 2 * S:3 * S], causal)
            items = [(w_feat[8 + m], S) for m in range(12)] + packed(w_tok, 328, 840)
            units = [Unit("feature", [m], P, "act", copy_into(FQ[:, m, :], scale=QK_SCALE)) for m in range(2)]
            units += [Unit("feature", [2 + m], P, "act", take_keys(m)) for m in range(2)]
            units += [Unit("feature", [4 + m], P, "act",
                           lambda act, psum, own, m=m: act.activation(staged[m % 2], psum, ACT.Silu),
                           store=(GATE[:, m, :], staged[m % 2])) for m in range(KT)]
            units += [Unit("token", list(range(12, 16)), 512, "act", copy_into(DV[:, t, :]), t)
                      for t in range(NT)]
            product_stage(kit, "tk", XT, items, units, slots=4, beside=topk)

        attend_stage(kit, "sp", 4, lambda h, m, t: SQ[:, h // 2, t * P:(t + 1) * P],
                     lambda h, m, c, e: SQ[:, 2 + h % 2, c:e], lambda h, b: VS[:, b, 0:P], 64, OM, 512,
                     ident, identb, lambda t, c, e: MB[:, keys_at(t) + c:keys_at(t) + e], True)
        attend_stage(kit, "fg", 4, lambda h, m, t: FQ[:, h // 2, t * P:(t + 1) * P],
                     lambda h, m, c, e: FQ[:, 2 + h, c:e],
                     lambda h, b: VS[:, b, 72 + P * (h // 2):200 + P * (h // 2)], 64, OM, 768, ident, identb,
                     lambda t, c, e: causalb, False,
                     v_at=lambda h: 64 * (h % 2),
                     decay=lambda h, c, e: (pick[0:4, h, :], FF[:, c:e]))
        early.close()
        DQ = sbuf(nc, late, "DQ", [P, 12, S])
        items = [(w_feat[20 + m], S) for m in range(8)]
        units = [Unit("feature", [m], P, "rope", (DQ[:, m, :], QK_SCALE, None)) for m in range(4)]
        units += [Unit("feature", [m], P, "rope", (None, 1.0, (DQ[:, 2 * m - 4, :], DQ[:, 2 * m - 3, :])))
                  for m in range(4, 8)]
        clear_stage(kit, "zd", [DQ[64 * (1 - m % 2):64 * (2 - m % 2), 4 + m, :] for m in range(8)])
        product_stage(kit, "pd", XT, items, units, slots=4, rope=(cos, sin, swap))
        attend_stage(kit, "df", 4, lambda h, m, t: DQ[:, h, t * P:(t + 1) * P],
                     lambda h, m, c, e: DQ[:, 4 + 2 * h + m, c:e],
                     lambda h, b: DV[:, b, 128 * h:128 * h + 128], 128, OM, 0, ident, identb,
                     lambda t, c, e: causalb, False, minus_lam=LAM[:, 0:1])
        late.close()
    finish_stage(kit, "fin", OM, GATE, d["w_out_2"][l].rearrange("(k p) n -> p k n", p=P), X, XT,
                 d["g_subln_2"][l], LAM[:, 1:2], d["ln_g_2"][l], d["ln_b_2"][l], ident)


def second_block(kit, X, XT, C, d):
    nc = kit.nc
    with ExitStack() as mem:
        ROPE = sbuf(nc, mem, "ROPE", [P, 2 * S])
        LAM = sbuf(nc, mem, "LAM", [P, 2])
        OM = sbuf(nc, mem, "OM2", [P, NT, D])
        GATE = nc.dram_tensor("GATE", (P, KT, S), FP32).ap()
        tables = kit.sem("tables")
        with nc.Block() as block:
            @block.sync
            def _(sp):
                sp.dma_start(ROPE, d["constants"][:, ROPE_AT:ROPE_AT + 2 * S]).then_inc(tables, 16)
                sp.wait_ge(tables, 16)
        kit.clear_semaphores()
        with nc.Fori(0, DEPTH_2) as l:
            layer(kit, l, X, XT, C, ROPE[:, 0:S], ROPE[:, S:2 * S], LAM, OM, GATE, d)
            kit.clear_semaphores()


def build(nc, d, out):
    ctx = ExitStack()
    with ctx:
        kit = Kit(nc, ctx)
        X = sbuf(nc, ctx, "X", [P, NT, D])
        XT = sbuf(nc, ctx, "XT", [P, KT, S])
        CONST = sbuf(nc, ctx, "CONST", [P, FIRST_AT])

        def C(name):
            at, width = CONST_AT[name]
            return CONST[:, at:at + width]

        loaded = kit.sem("loaded")
        with nc.Block() as block:
            @block.sync
            def _(sp):
                sp.dma_start(X[:, :, :], d["x"].rearrange("(t p) n -> p t n", p=P)).then_inc(loaded, 16)
                sp.dma_start(CONST[:, :], d["constants"][:, 0:FIRST_AT]).then_inc(loaded, 16)
                sp.wait_ge(loaded, 32)
        first_block(kit, X, XT, C, d)
        second_block(kit, X, XT, C, d)
        stored = kit.sem("stored")
        with nc.Block() as block:
            @block.sync
            def _(sp):
                sp.dma_start(out.rearrange("(t p) n -> p t n", p=P), X[:, :, :]).then_inc(stored, 16)
                sp.wait_ge(stored, 16)


def _feature_tiles(w):
    k, n = w.shape
    return np.ascontiguousarray(w.reshape(k // P, P, n // P, P).transpose(2, 1, 0, 3)).reshape(n // P, P, k)


def _narrow_tile(w):
    k, m = w.shape
    return np.ascontiguousarray(w.reshape(k // P, P, m).transpose(1, 0, 2)).reshape(P, -1)


def layout(inputs):
    a = {n: np.asarray(v) for n, v in inputs.items()}
    d = {"x": a["x"][0], "constants": constants()}
    for n in ("norm_mix", "hgrn_lower_bounds", "hgrn_norm", "rg_conv_w", "rg_conv_b", "rg_w_a", "rg_b_a",
              "rg_w_x", "rg_b_x", "rg_lambda", "gla_w_gate_up", "gla_b_gate", "gla_norm", "w_out", "norm_ffn",
              "ffn_conv_w", "ffn_conv_b", "ffn_w_down"):
        d[n] = a[n][0]
    d["norm_final"] = a["norm_final"]
    at = np.cumsum([0, 256, 256, 256, 256, 512, 512, 128, 128, 256, 256, 16])
    aq, af, ai, ag, bx, bg, cq, ck, cv, cg, lr = [a["w_in"][0][:, at[n]:at[n + 1]] for n in range(11)]
    d["w_in_feat"] = _feature_tiles(np.concatenate([aq, af, bx, bg, cq, ck], 1))
    d["w_in_lr"] = _narrow_tile(lr)
    d["w_in_tok"] = np.concatenate([ai, ag, cv, cg], 1)
    d["ffn_w_gate"] = _feature_tiles(a["ffn_w_gate"][0])
    d["ffn_w_val"] = _feature_tiles(a["ffn_w_val"][0])
    at = np.cumsum([0, 512, 512, 512, 256, 64, 64, 512, 64, 8, 256, 256, 256, 4, 1024])
    feats, toks, narrow = [], [], []
    for l in range(DEPTH_2):
        dq, dk, dv, sq, sk, sv, iq, ik, iw, fq, fk, fv, ff, gate = [
            a["w_in_2"][l][:, at[n]:at[n + 1]] for n in range(14)]
        feats.append(_feature_tiles(np.concatenate([sq, sk, sk, iq, ik, ik, fq, fk,
                                                      gate, dq, dk], 1)))
        toks.append(np.concatenate([sv, iw, fv, dv], 1))
        narrow.append(_narrow_tile(ff))
    d["w2_feat"], d["w2_tok"], d["w2_ff"] = np.stack(feats), np.stack(toks), np.stack(narrow)
    for n in ("b_f", "lam_q1", "lam_k1", "lam_q2", "lam_k2", "g_subln", "w_out", "ln_g", "ln_b"):
        d[n + "_2"] = a[n + "_2"]
    init = [0.8 - 0.6 * math.exp(-0.3 * l) for l in range(DEPTH_2)]
    d["lam_init"] = np.array([[i, 1.0 - i] for i in init], np.float32)
    return {n: np.ascontiguousarray(v) for n, v in d.items()}


def kernel(**inputs):
    import concourse.bacc as _bacc
    from concourse.bass_utils import run_bass_kernel_spmd as _run

    nc = _bacc.Bacc("TRN2", target_bir_lowering=False, num_devices=1)
    arrays = {f"in_{n}": v for n, v in layout(inputs).items()}
    d = {n[3:]: nc.dram_tensor(n, v.shape, mybir.dt.from_np(v.dtype), kind="ExternalInput").ap()
         for n, v in arrays.items()}
    out = nc.dram_tensor("out_x", (S, D), FP32, kind="ExternalOutput").ap()
    build(nc, d, out)
    r = _run(nc, [arrays], core_ids=[0])
    return r.results[0]["out_x"].reshape(1, S, D)
```

```python
import math
from contextlib import ExitStack

import numpy as np

import concourse.bass as bass
from concourse import mybir

FP32 = mybir.dt.float32
FP32R = mybir.dt.float32r
BF16 = mybir.dt.bfloat16
INT32 = mybir.dt.int32
ACT = mybir.ActivationFunctionType
ALU = mybir.AluOpType
AX = mybir.AxisListType

P = 128
S = 1024
D = 1024
NT = S // P
KT = D // P
HALF = 512
EPS = 1e-6
LN_EPS = 1e-5
SUBLN_EPS = 1e-5
F_FLOOR = 1e-20
LRU_C = 8.0
NEG = -1e30
D_FF = 2688
FT = D_FF // P
DEPTH_2 = 2
ALPHA = (2 * DEPTH_2) ** 0.25
IDX_SCALE = 512 ** -0.5
TOPK = 256
BISECTIONS = 32
QK_SCALE = 64 ** -0.5

LEVELS = [64, 32, 16, 8, 4, 2, 1]
PASS_ROWS = [(0, 64), (0, 64), (0, 32), (64, 32)]

CONST_AT = {}


def _const_columns():
    at = 0
    for name, width in (("ident", P), ("swap", P), ("causal", P), ("pick", 4 * P),
                        ("level", 7 * 64), ("heads", 8), ("keep", S), ("cos", S), ("sin", S)):
        CONST_AT[name] = (at, width)
        at += width
    return at


CONST_WIDTH = _const_columns()
FIRST_AT = CONST_AT["level"][0]
ROPE_AT = CONST_AT["cos"][0]


def constants():
    c = np.zeros((P, CONST_WIDTH), np.float32)

    def put(name, value):
        at, width = CONST_AT[name]
        c[:, at:at + width] = value

    put("ident", np.eye(P))
    j = np.arange(P)
    swap = np.zeros((P, P))
    swap[j, (j // 64) * 64 + (j + 32) % 64] = 1.0
    put("swap", swap)
    put("causal", np.where(j[None, :] > j[:, None], NEG, 0.0))
    level = np.zeros((P, 7, 64))
    for n, b in enumerate(LEVELS):
        i = np.arange(64)
        block = i // b
        level[:, n, :] = (j[:, None] // (2 * b) == block[None, :]) & (j[:, None] % (2 * b) < b)
    put("level", level.reshape(P, -1))
    heads = np.zeros((P, 4, 2))
    for n, (first, dk) in enumerate(PASS_ROWS):
        for h in range(2):
            heads[first + h * dk:first + (h + 1) * dk, n, h] = 1.0
    put("heads", heads.reshape(P, -1))
    keep = np.ones(S)
    keep[::P] = 0.0
    put("keep", keep[None, :])
    pick = np.zeros((P, 4, P))
    for h in range(4):
        pick[[h, 32 + h, 64 + h], h, :] = 1.0
    put("pick", pick.reshape(P, -1))
    inv = (np.float32(10000.0) ** (-np.arange(0, 64, 2, dtype=np.float32) / np.float32(64))).astype(np.float32)
    angle = (np.arange(S, dtype=np.float32)[:, None] * inv[None, :]).astype(np.float32)
    cos, sin = np.cos(angle).T, np.sin(angle).T
    put("cos", np.concatenate([cos] * 4))
    put("sin", np.concatenate([sin, -sin] * 2))
    return c


class Kit:

    def __init__(self, nc, ctx):
        self.nc, self.ctx = nc, ctx
        self.psum = ctx.enter_context(nc.psum_tensor("psum", [P, 8, HALF], FP32))
        self.sems, self.sem_ctx = [], ctx.enter_context(ExitStack())

    def sem(self, name):
        s = self.sem_ctx.enter_context(self.nc.semaphore(name))
        self.sems.append(s)
        return s

    def clear_semaphores(self):
        with self.nc.Block() as block:
            @block.sync
            def _(sp):
                for sem in self.sems:
                    sp.sem_clear(sem)
        self.sem_ctx.close()
        self.sems = []

    def pair(self, n):
        return self.psum[:, 2 * n:2 * n + 2, :].rearrange("p b n -> p (b n)")


class Own:

    def __init__(self, eng, sem, base=0):
        self.eng, self.sem, self.base, self.n = eng, sem, base, 0

    def __call__(self, instruction):
        instruction.then_inc(self.sem, 1)
        self.n += 1
        return self.n

    def wait(self, n=None):
        self.eng.wait_ge(self.sem, self.base + (self.n if n is None else n))

    def then(self, instruction):
        self(instruction)
        self.wait()


def sbuf(nc, stack, name, shape, dtype=FP32):
    return stack.enter_context(nc.sbuf_tensor(name, shape, dtype))[(slice(None),) * len(shape)]


def bcast(row_ap):
    return row_ap.partition_broadcast(P)


def norm_stage(kit, tag, X, XT, ident, gain, bias=None, eps=EPS, keep=False, rest=None):
    nc = kit.nc
    layer = bias is not None
    gain_in, squares, stats, root, rows, turned, copied, parted, dve_own = (
        kit.sem(f"{tag}_{n}") for n in ("gain_in", "squares", "stats", "root", "rows", "turned", "copied",
                                        "parted", "dve_own"))
    with ExitStack() as mem:
        G = sbuf(nc, mem, f"{tag}_G", [P, D])
        B = sbuf(nc, mem, f"{tag}_B", [P, D]) if layer else None
        H = None if keep else sbuf(nc, mem, f"{tag}_H", [P, 2, D])
        junk = sbuf(nc, mem, f"{tag}_junk", [P, D])
        sums = sbuf(nc, mem, f"{tag}_sums", [P, NT])
        bn = sbuf(nc, mem, f"{tag}_bn", [P, NT, 2, 6])
        mv = sbuf(nc, mem, f"{tag}_mv", [P, NT, 2])
        eps_col = sbuf(nc, mem, f"{tag}_eps", [P, 1])
        dev = sbuf(nc, mem, f"{tag}_dev", [P, NT])
        inv = sbuf(nc, mem, f"{tag}_inv", [P, NT])
        with nc.Block() as block:
            @block.sync
            def _(sp):
                sp.dma_start(G[:, :], bcast(gain)).then_inc(gain_in, 16)
                if layer:
                    sp.dma_start(B[:, :], bcast(bias)).then_inc(gain_in, 16)

            @block.scalar
            def _(act):
                if not layer:
                    for t in range(NT):
                        act.activation(junk[:, :], X[:, t, :], ACT.Square,
                                       accum_out=sums[:, t:t + 1]).then_inc(squares, 1)
                        act.wait_ge(squares, t + 1)
                act.wait_ge(stats, NT + 1 if layer else 1)
                src = mv[:, :, 1] if layer else sums[:, :]
                act.activation(dev[:, :], src, ACT.Sqrt, scale=1.0 if layer else 1.0 / D,
                               bias=eps_col[:, :]).then_inc(root, 1)
                for t in range(NT):
                    act.wait_ge(turned, t + 1)
                    act.activation(XT[:, :, t * P:(t + 1) * P],
                                   kit.pair(t % 2).rearrange("p (k n) -> p k n", k=KT),
                                   ACT.Copy).then_inc(copied, 1)

            @block.vector
            def _(dve):
                own = Own(dve, dve_own)
                if layer:
                    for t in range(NT):
                        for n in range(2):
                            own(dve.bn_stats(bn[:, t, n, :], X[:, t, n * HALF:(n + 1) * HALF]))
                        own.wait()
                        dve.bn_aggr(mv[:, t, :], bn[:, t, :, :]).then_inc(stats, 1)
                dve.memset(eps_col[:, :], eps).then_inc(stats, 1)
                dve.wait_ge(root, 1)
                own.then(dve.reciprocal(inv[:, :], dev[:, :]))
                dve.wait_ge(gain_in, 32 if layer else 16)

                def norm(t):
                    out = X[:, t, :] if keep else H[:, t % 2, :]
                    if not keep and t >= 2:
                        dve.wait_ge(turned, t - 1)
                    if layer:
                        own.then(dve.tensor_scalar(out, X[:, t, :], mv[:, t, 0:1], inv[:, t:t + 1],
                                                   ALU.subtract, ALU.mult))
                        own.then(dve.tensor_tensor(out, out, G[:, :], ALU.mult))
                        dve.tensor_tensor(out, out, B[:, :], ALU.add).then_inc(rows, 1)
                    else:
                        dve.scalar_tensor_tensor(out, X[:, t, :], inv[:, t:t + 1], G[:, :],
                                                 ALU.mult, ALU.mult).then_inc(rows, 1)

                for t in range(NT + 1):
                    if t < NT:
                        norm(t)
                    if rest is not None and t:
                        at = slice((t - 1) * P, t * P)
                        dve.wait_ge(copied, t)
                        dve.tensor_tensor(rest[:, :, at], kit.pair((t - 1) % 2).rearrange("p (k n) -> p k n", k=KT),
                                          XT[:, :, at].bitcast(FP32), ALU.subtract).then_inc(parted, 1)

            @block.tensor
            def _(pe):
                for t in range(NT):
                    src = X[:, t, :] if keep else H[:, t % 2, :]
                    pe.wait_ge(rows, t + 1)
                    if t >= 2:
                        pe.wait_ge(copied if rest is None else parted, t - 1)
                    for k in range(KT):
                        last = pe.transpose(kit.pair(t % 2)[:, k * P:(k + 1) * P],
                                            src[:, k * P:(k + 1) * P], ident)
                    last.then_inc(turned, 1)


class Unit:

    def __init__(self, kind, items, width, by, take, t=0, store=None):
        self.kind, self.items, self.width, self.by, self.take, self.t = kind, items, width, by, take, t
        self.store = store


def product_stage(kit, tag, XT, items, units, slots=8, rope=None, place=None, rot_place=None, beside=None):
    nc = kit.nc
    n_pairs = 3 if rope else 4
    w_in = [kit.sem(f"{tag}_w_in{s}") for s in range(slots)]
    products, taken_act, taken_dve, act_own, dve_own, scaled, swapped = (
        kit.sem(f"{tag}_{n}") for n in ("products", "taken_act", "taken_dve", "act_own", "dve_own",
                                        "scaled", "swapped"))
    last_use = {}
    for u, unit in enumerate(units):
        for i in unit.items:
            last_use[i] = u
    stores = [u for u, unit in enumerate(units) if unit.store]
    stored = [kit.sem(f"{tag}_stored{s}") for s in range(2)] if stores else []
    by_act = [u for u, unit in enumerate(units) if unit.by == "act"]
    by_dve = [u for u, unit in enumerate(units) if unit.by != "act"]
    ropes = [u for u, unit in enumerate(units) if unit.by == "rope"]
    with ExitStack() as mem:
        W = sbuf(nc, mem, f"{tag}_W", [P, slots, 1024]) if place is None else place
        if rope:
            cos, sin, swap = rope
            rot = sbuf(nc, mem, f"{tag}_rot", [P, 2, S]) if rot_place is None else rot_place
            straight = sbuf(nc, mem, f"{tag}_straight", [P, 2, S])
        with nc.Block() as block:
            def wait_taken(eng, u):
                if units[u].by == "act":
                    eng.wait_ge(taken_act, by_act.index(u) + 1)
                elif units[u].by == "rope":
                    eng.wait_ge(scaled, ropes.index(u) + 1)
                else:
                    eng.wait_ge(taken_dve, [v for v in by_dve if units[v].by == "dve"].index(u) + 1)

            @block.sync
            def _(sp):
                for i, (src, width) in enumerate(items):
                    if i >= slots:
                        sp.wait_ge(products, last_use[i - slots] + 1)
                    dst = W[:, i % slots, 0:width]
                    if len(src.shape) == 3:
                        dst = dst.rearrange("p (a n) -> p a n", a=src.shape[1])
                    sp.dma_start(dst, src).then_inc(w_in[i % slots], 16)

            @block.tensor
            def _(pe):
                def swap_halves(n):
                    pe.wait_ge(scaled, n + 1)
                    if n >= 1:
                        pe.wait_ge(taken_dve, n)
                    for c in range(2):
                        last = pe.matmul(kit.pair(3)[:, c * HALF:(c + 1) * HALF], swap,
                                         rot[:, n % 2, c * HALF:(c + 1) * HALF], start=True, stop=True)
                    last.then_inc(swapped, 1)

                for u, unit in enumerate(units):
                    for i in unit.items:
                        pe.wait_ge(w_in[i % slots], 16 * (i // slots + 1))
                    if u >= n_pairs:
                        wait_taken(pe, u - n_pairs)
                    out = kit.pair(u % n_pairs)
                    if unit.kind == "feature":
                        m = unit.width
                        w = W[:, unit.items[0] % slots, 0:KT * m].rearrange("p (k m) -> p k m", k=KT)
                        for c in range(2):
                            for k in range(KT):
                                last = pe.matmul(out[0:m, c * HALF:(c + 1) * HALF], w[:, k, :],
                                                 XT[:, k, c * HALF:(c + 1) * HALF],
                                                 start=k == 0, stop=k == KT - 1)
                    else:
                        pack = KT // len(unit.items)
                        for c in range(0, unit.width, HALF):
                            e = min(unit.width, c + HALF)
                            for k in range(KT):
                                at = (k % pack) * unit.width
                                last = pe.matmul(out[:, c:e], XT[:, k, unit.t * P:(unit.t + 1) * P],
                                                 W[:, unit.items[k // pack] % slots, at + c:at + e],
                                                 start=k == 0, stop=k == KT - 1)
                    last.then_inc(products, 1)
                    if u - 1 in ropes:
                        swap_halves(ropes.index(u - 1))
                if len(units) - 1 in ropes:
                    swap_halves(len(ropes) - 1)

            @block.scalar
            def _(act):
                own = Own(act, act_own)
                for u in by_act:
                    act.wait_ge(products, u + 1)
                    if u in stores and stores.index(u) >= 2:
                        n = stores.index(u)
                        act.wait_ge(stored[n % 2], 16 * (n // 2))
                    units[u].take(act, kit.pair(u % n_pairs), own).then_inc(taken_act, 1)
                    if u in stores:
                        act.wait_ge(taken_act, by_act.index(u) + 1)
                        act.dma_start(*units[u].store).then_inc(stored[stores.index(u) % 2], 16)
                for n, sem in enumerate(stored):
                    act.wait_ge(sem, 16 * len(stores[n::2]))

            @block.vector
            def _(dve):
                own = Own(dve, dve_own)
                pending = []
                if beside:
                    beside(dve)

                def add_partner(n, dst, split):
                    dve.wait_ge(swapped, n + 1)
                    if split is None:
                        dve.tensor_tensor(dst, dst, kit.pair(3), ALU.add).then_inc(taken_dve, 1)
                        return
                    for i, tile in enumerate(split):
                        half = slice(64 * i, 64 * i + 64)
                        last = dve.tensor_tensor(tile[half, :], dst[half, :], kit.pair(3)[half, :], ALU.add)
                    last.then_inc(taken_dve, 1)

                for u in by_dve:
                    dve.wait_ge(products, u + 1)
                    out = kit.pair(u % n_pairs)
                    if units[u].by == "rope":
                        n = ropes.index(u)
                        dst, scale, split = units[u].take
                        if split is not None:
                            dst = straight[:, n % 2, :]
                            if n >= 2:
                                dve.wait_ge(taken_dve, n - 1)
                        own(dve.scalar_tensor_tensor(dst, out, scale, cos, ALU.mult, ALU.mult))
                        if n >= 2:
                            dve.wait_ge(swapped, n - 1)
                        dve.scalar_tensor_tensor(rot[:, n % 2, :], out, scale, sin, ALU.mult,
                                                 ALU.mult).then_inc(scaled, 1)
                        own.wait()
                        if pending:
                            add_partner(*pending.pop())
                        pending.append((n, dst, split))
                    else:
                        if pending:
                            add_partner(*pending.pop())
                        units[u].take(dve, out, own).then_inc(taken_dve, 1)
                if pending:
                    add_partner(*pending.pop())


def copy_into(dst, rows=P, scale=1.0):
    width = dst.free_size()
    return lambda act, psum, own: act.activation(dst, psum[0:rows, 0:width], ACT.Copy, scale=scale)


def copy_into_dve(dst):
    width = dst.free_size()
    return lambda dve, psum, own: dve.tensor_copy(dst, psum[:, 0:width])


def rglru_stage(kit, BX, BG, XT, spare, d):
    nc = kit.nc
    NB = 4
    params, blocks, zeroed, ready, conv, gates, sig, decay, root, gelu, own_d, own_a, done = (
        kit.sem(f"lru_{n}") for n in ("params", "blocks", "zeroed", "ready", "conv", "gates", "sig", "decay",
                                      "root", "gelu", "own_d", "own_a", "done"))
    with ExitStack() as mem:
        XC, R = XT[:, 0:NB, :], XT[:, NB:2 * NB, :]
        GI = sbuf(nc, mem, "lru_GI", [P, NB, S])
        TH = sbuf(nc, mem, "lru_TH", [P, NB, S])
        A = BX[:, :, 3:3 + S]
        W = spare.rearrange("p (n j m) -> p n j m", n=2, j=NB)
        par = sbuf(nc, mem, "lru_par", [P, 8, NB])
        tmp = sbuf(nc, mem, "lru_tmp", [P, 6, NB])
        with nc.Block() as block:
            @block.sync
            def _(sp):
                with nc.allow_non_contiguous_dma(reason="a few hundred per-channel parameters"):
                    for n, src in enumerate([d["rg_conv_w"][k] for k in range(4)]
                                            + [d["rg_conv_b"], d["rg_b_a"], d["rg_b_x"], d["rg_lambda"]]):
                        sp.dma_start(par[:, n, :], src.rearrange("(j p) -> p j", p=P)).then_inc(params, 16)
                sp.wait_ge(zeroed, 1)
                for n, src in enumerate((d["rg_w_a"], d["rg_w_x"])):
                    for half in range(2):
                        sp.dma_start(W[half * 64:half * 64 + 64, n, :, half * 64:half * 64 + 64],
                                     src.rearrange("(j two) i o -> two i j o", two=2)[half]
                                     ).then_inc(blocks, 16)

            @block.gpsimd
            def _(pool):
                pool.memset(W[:, :, :, :], 0.0).then_inc(zeroed, 1)

            @block.vector
            def _(dve):
                own = Own(dve, own_d)
                dve.wait_ge(params, 16 * 8)
                lam = par[:, 7, :]
                mag, e, w = tmp[:, 0, :], tmp[:, 1, :], tmp[:, 2, :]
                own.then(dve.tensor_scalar(tmp[:, 3, :], lam, -1.0, None, ALU.mult))
                dve.tensor_tensor(mag, tmp[:, 3, :], lam, ALU.min).then_inc(ready, 1)
                for j in range(NB):
                    x = BX[:, j, :]
                    own.then(dve.tensor_scalar(XC[:, j, :], x[:, 3:3 + S], par[:, 3, j:j + 1],
                                               par[:, 4, j:j + 1], ALU.mult, ALU.add))
                    for k in range(3):
                        ins = dve.scalar_tensor_tensor(XC[:, j, :], x[:, k:k + S], par[:, k, j:j + 1],
                                                       XC[:, j, :], ALU.mult, ALU.add)
                        if k < 2:
                            own.then(ins)
                        else:
                            ins.then_inc(conv, 1)
                dve.wait_ge(own_a, 1)
                own.then(dve.tensor_scalar(w, e, 1.0, None, ALU.add))
                own(dve.tensor_scalar(tmp[:, 4, :], w, 1.0, None, ALU.is_equal))
                dve.tensor_scalar(tmp[:, 5, :], w, -1.0, None, ALU.add).then_inc(ready, 1)
                own.wait()
                dve.wait_ge(ready, 2)
                own.then(dve.tensor_tensor(tmp[:, 5, :], tmp[:, 5, :], tmp[:, 4, :], ALU.add))
                own.then(dve.reciprocal(tmp[:, 5, :], tmp[:, 5, :]))
                dve.wait_ge(own_a, 2)
                own.then(dve.tensor_tensor(w, w, tmp[:, 4, :], ALU.add))
                own.then(dve.tensor_tensor(w, w, tmp[:, 5, :], ALU.mult))
                own.then(dve.tensor_tensor(w, w, e, ALU.mult))
                own.then(dve.tensor_scalar(tmp[:, 3, :], tmp[:, 3, :], 0.0, None, ALU.max))
                own.then(dve.tensor_tensor(w, w, tmp[:, 3, :], ALU.add))
                own(dve.tensor_scalar(tmp[:, 3, :], w, LRU_C, None, ALU.mult))
                own(dve.tensor_scalar(tmp[:, 4, :], w, -LRU_C, None, ALU.mult))
                dve.tensor_scalar(tmp[:, 5, :], w, -2 * LRU_C, None, ALU.mult).then_inc(ready, 1)
                for j in range(NB):
                    dve.wait_ge(decay, j + 1)
                    own.then(dve.scalar_tensor_tensor(TH[:, j, :], R[:, j, :], 1.0, TH[:, j, :],
                                                      ALU.add, ALU.mult))
                    dve.tensor_scalar(TH[:, j, :], TH[:, j, :], 0.0, None, ALU.max).then_inc(ready, 1)
                    own.then(dve.tensor_tensor(GI[:, j, :], GI[:, j, :], XC[:, j, :], ALU.mult))
                for j in range(NB):
                    dve.wait_ge(root, j + 1)
                    own.then(dve.tensor_tensor(GI[:, j, :], GI[:, j, :], TH[:, j, :], ALU.mult))
                    own.then(dve.tensor_tensor_scan(XC[:, j, :], A[:, j, :], GI[:, j, :], 0.0,
                                                    ALU.mult, ALU.add))
                    dve.wait_ge(gelu, j + 1)
                    dve.tensor_tensor(BG[:, j, :], BG[:, j, :], XC[:, j, :], ALU.mult).then_inc(done, 1)

            @block.tensor
            def _(pe):
                pe.wait_ge(blocks, 16 * 4)
                for j in range(NB):
                    pe.wait_ge(conv, j + 1)
                    for n in range(2):
                        if j >= 2:
                            pe.wait_ge(sig, 2 * (j - 2) + n + 1)
                        for c in range(2):
                            last = pe.matmul(kit.pair(2 * n + j % 2)[:, c * HALF:(c + 1) * HALF],
                                             W[:, n, j, :], XC[:, j, c * HALF:(c + 1) * HALF],
                                             start=True, stop=True)
                        last.then_inc(gates, 1)

            @block.scalar
            def _(act):
                act.wait_ge(ready, 1)
                act.activation(tmp[:, 1, :], tmp[:, 0, :], ACT.Exp).then_inc(own_a, 1)
                act.wait_ge(ready, 2)
                act.activation(tmp[:, 2, :], tmp[:, 2, :], ACT.Ln).then_inc(own_a, 1)
                for j in range(NB):
                    for n, dst in enumerate((R, GI)):
                        act.wait_ge(gates, 2 * j + n + 1)
                        act.activation(dst[:, j, :], kit.pair(2 * n + j % 2), ACT.Sigmoid,
                                       bias=par[:, 5 + n, j:j + 1]).then_inc(sig, 1)
                act.wait_ge(sig, 2 * NB)
                act.wait_ge(ready, 3)
                for j in range(NB):
                    act.activation(TH[:, j, :], R[:, j, :], ACT.Tanh,
                                   scale=tmp[:, 3, j:j + 1]).then_inc(own_a, 1)
                for j in range(NB):
                    act.activation(A[:, j, :], R[:, j, :], ACT.Exp, scale=tmp[:, 4, j:j + 1]).then_inc(own_a, 1)
                    act.wait_ge(own_a, 2 + NB + j + 1)
                    act.activation(R[:, j, :], R[:, j, :], ACT.Exp, scale=tmp[:, 5, j:j + 1]).then_inc(decay, 1)
                for j in range(NB):
                    act.activation(BG[:, j, :], BG[:, j, :], ACT.Gelu_apprx_tanh).then_inc(gelu, 1)
                for j in range(NB):
                    act.wait_ge(ready, 4 + j)
                    act.activation(TH[:, j, :], TH[:, j, :], ACT.Sqrt).then_inc(root, 1)


def gate_prep_stage(kit, AF, AK, CLR, LF, spare, d):
    nc = kit.nc
    params, low, made, sg, lns, own_d, own_a, gate = (
        kit.sem(f"gp_{n}") for n in ("params", "low", "made", "sg", "lns", "own_d", "own_a", "gate"))
    with ExitStack() as mem:
        par = sbuf(nc, mem, "gp_par", [P, 3])
        lb = sbuf(nc, mem, "gp_lb", [P, 4])
        UP = sbuf(nc, mem, "gp_UP", [16, P])
        F, F2, Y, E = spare[:, 0:2, :], spare[:, 2:4, :], spare[:, 4, :], spare[:, 5, :]
        with nc.Block() as block:
            @block.sync
            def _(sp):
                with nc.allow_non_contiguous_dma(reason="a few hundred per-channel parameters"):
                    sp.dma_start(par[:, 0:2], d["hgrn_lower_bounds"].rearrange("(j p) -> p j", p=P)
                                 ).then_inc(params, 16)
                    sp.dma_start(par[:, 2:3], d["gla_b_gate"].rearrange("(j p) -> p j", p=P)
                                 ).then_inc(params, 16)
                sp.dma_start(UP[:, :], d["gla_w_gate_up"]).then_inc(params, 16)

            @block.tensor
            def _(pe):
                pe.wait_ge(params, 48)
                for c in range(2):
                    last = pe.matmul(kit.pair(0)[:, c * HALF:(c + 1) * HALF], UP[:, :],
                                     CLR[:, c * HALF:(c + 1) * HALF], start=True, stop=True)
                last.then_inc(low, 1)

            @block.scalar
            def _(act):
                act.activation(F, AF[:, :, :], ACT.Sigmoid).then_inc(sg, 1)
                act.activation(AK[:, :, :], AF, ACT.Sigmoid, scale=-1.0).then_inc(sg, 1)
                act.wait_ge(low, 1)
                act.wait_ge(params, 48)
                act.activation(E, kit.pair(0), ACT.Abs, bias=par[:, 2:3]).then_inc(own_a, 1)
                act.wait_ge(own_a, 1)
                act.activation(E, E, ACT.Exp, scale=-1.0).then_inc(own_a, 1)
                act.wait_ge(own_a, 2)
                act.activation(E, E, ACT.Ln, bias=1.0).then_inc(lns, 1)
                act.wait_ge(made, 1)
                act.activation(LF[:, 0:2, :], F2, ACT.Ln).then_inc(lns, 1)
                act.wait_ge(made, 2)
                act.activation(AF[:, :, :], F, ACT.Ln).then_inc(lns, 1)

            @block.vector
            def _(dve):
                own = Own(dve, own_d)
                dve.wait_ge(params, 48)
                own.then(dve.tensor_tensor(lb[:, 0:2], par[:, 0:2], par[:, 0:2], ALU.subtract))
                own.then(dve.tensor_scalar(lb[:, 2:4], lb[:, 0:2], -1.0, 1.0, ALU.mult, ALU.add))
                dve.wait_ge(sg, 2)
                for j in range(2):
                    own(dve.tensor_scalar(F[:, j, :], F[:, j, :], lb[:, 2 + j:3 + j], lb[:, j:j + 1],
                                          ALU.mult, ALU.add))
                    own(dve.tensor_scalar(AK[:, j, :], AK[:, j, :], lb[:, 2 + j:3 + j], None, ALU.mult))
                own.wait()
                own.then(dve.tensor_scalar(F2, F, F_FLOOR, 2.0 ** 60, ALU.max, ALU.mult))
                dve.tensor_scalar(F2, F2, 1.0, None, ALU.min).then_inc(made, 1)
                dve.tensor_scalar(F, F, 2.0 ** -60, None, ALU.max).then_inc(made, 1)
                dve.wait_ge(low, 1)
                dve.wait_ge(own_a, 1)
                own.then(dve.tensor_scalar(Y, kit.pair(0), par[:, 2:3], 0.0, ALU.add, ALU.min))
                dve.wait_ge(lns, 1)
                own.then(dve.tensor_tensor(Y, Y, E, ALU.subtract))
                own(dve.tensor_scalar(LF[:, 2, :], Y, 1.0 / 16.0, None, ALU.mult))
                dve.wait_ge(lns, 3)
                own(dve.tensor_tensor(LF[:, 0:2, :], LF[:, 0:2, :], AF, ALU.add))
                own.wait()


def gla_stage(kit, Q, K, LF, VA, VC, O, XT, X, spare, ident, level, heads, keep):
    nc = kit.nc
    NL = len(LEVELS)
    NP = len(PASS_ROWS)
    cums, refs, weights, mixed, state_w, cleared, kt_done, kt_taken, scored, placed, out_done, out_taken, \
        upd_done, upd_taken, own_d, own_a, own_m = (
            kit.sem(f"gla_{n}") for n in ("cums", "refs", "weights", "mixed", "state_w", "cleared", "kt_done",
                                          "kt_taken", "scored", "placed", "out_done", "out_taken", "upd_done",
                                          "upd_taken", "own_d", "own_a", "own_m"))
    tile_of = [0, 1, 2, 2]
    flat = X.rearrange("p t n -> p (t n)")
    with ExitStack() as mem:
        KW = XT[:, 0:NL, :]
        C = XT[:, NL, :]
        QW = flat[:, 0:NL * S].rearrange("p (n c h m) -> p n c h m", n=NL, c=NT, h=2)
        QK = flat[:, NL * S:]
        Z = spare
        QE = sbuf(nc, mem, "gla_QE", [P, S])
        KL = sbuf(nc, mem, "gla_KL", [P, S])
        EL = sbuf(nc, mem, "gla_EL", [P, NT])
        KLT = sbuf(nc, mem, "gla_KLT", [P, S])
        SC = sbuf(nc, mem, "gla_SC", [P, 2, 2, P])
        ST = sbuf(nc, mem, "gla_ST", [P, 2, P])
        LM = sbuf(nc, mem, "gla_LM", [P, NL * 64], INT32)
        DM = sbuf(nc, mem, "gla_DM", [P, P], INT32)
        with nc.Block() as block:
            @block.gpsimd
            def _(pool):
                for n, p in enumerate((0, 2, 3)):
                    if p:
                        pool.wait_ge(out_done, NT * p)
                    pool.memset(flat[:, 0:NL * S], 0.0).then_inc(cleared, 1)

            @block.vector
            def _(dve):
                own = Own(dve, own_d)
                own(dve.tensor_copy(LM[:, :], level))
                own(dve.tensor_copy(DM[:, :], ident))
                own(dve.memset(SC, 0.0))
                own.wait()
                for p, (first, dk) in enumerate(PASS_ROWS):
                    g = tile_of[p]
                    rows = [slice(first + h * dk, first + (h + 1) * dk) for h in range(2)]
                    new_tile = p == 0 or tile_of[p - 1] != g
                    if p:
                        dve.wait_ge(out_done, NT * p)
                    if new_tile:
                        own.then(dve.tensor_tensor_scan(C, keep, LF[:, g, :], 0.0, ALU.mult, ALU.add))
                        dve.sem_inc(cums, 1)

                    def refer(n):
                        b = LEVELS[n]
                        z = Z[:, n % 2, :].rearrange("p (m w) -> p m w", w=2 * b)
                        c3 = C.rearrange("p (m w) -> p m w", w=2 * b)
                        ref = c3[:, :, b - 1:b].to_broadcast([P, S // (2 * b), 2 * b])
                        if n >= 2 or g >= 1:
                            dve.wait_ge(weights, NL * g + n - 1 if n >= 2 else NL * g)
                        dve.tensor_tensor(z, c3, ref, ALU.subtract).then_inc(refs, 1)

                    if new_tile:
                        refer(0)
                    for n, b in enumerate(LEVELS):
                        if new_tile:
                            if n + 1 < NL:
                                refer(n + 1)
                            dve.wait_ge(weights, NL * g + n + 1)
                        if n == 0:
                            dve.wait_ge(cleared, max(p, 1))
                        w = KW[:, n, :].rearrange("p (c m w) -> p c m w", c=NT, w=2 * b)
                        q4 = Q[:, g, :].rearrange("p (c m w) -> p c m w", c=NT, w=2 * b)
                        for h, r in enumerate(rows):
                            own(dve.tensor_tensor(QW[r, n, :, h, :].rearrange("p c (m w) -> p c m w", w=b),
                                                  w[r, :, :, b:2 * b], q4[r, :, :, b:2 * b], ALU.mult))
                        if new_tile:
                            w3 = KW[:, n, :].rearrange("p (m w) -> p m w", w=2 * b)[:, :, 0:b]
                            k3 = K[:, g, :].rearrange("p (m w) -> p m w", w=2 * b)[:, :, 0:b]
                            own(dve.tensor_tensor(w3, w3, k3, ALU.mult))
                    if new_tile:
                        own(dve.tensor_tensor(QK, Q[:, g, :], K[:, g, :], ALU.mult))
                        z = Z[:, 0, :].rearrange("p (m w) -> p m w", w=P)
                        c3 = C.rearrange("p (m w) -> p m w", w=P)
                        own.then(dve.tensor_tensor(z, c3[:, :, P - 1:P].to_broadcast([P, NT, P]), c3,
                                                   ALU.subtract))
                        dve.sem_inc(state_w, 1)
                        dve.wait_ge(own_a, 3 * (g + 1))
                        own(dve.tensor_tensor(QE, QE, Q[:, g, :], ALU.mult))
                        own(dve.tensor_tensor(KL[:, :], KL[:, :], K[:, g, :], ALU.mult))
                    own(dve.memset(ST, 0.0))
                    own.wait()
                    dve.sem_inc(mixed, 1)
                    for c in range(NT):
                        step = NT * p + c
                        dve.wait_ge(scored, step + 1)
                        if step >= 2:
                            dve.wait_ge(out_done, step - 1)
                        slot = SC[:, step % 2, :, :]
                        bank = kit.pair(step % 2)
                        own.then(dve.copy_predicated(slot, DM.unsqueeze(1).to_broadcast([P, 2, P]),
                                                     bank[:, NL * P:NL * P + 2].unsqueeze(2)
                                                     .to_broadcast([P, 2, P])))
                        own.then(dve.tensor_copy(slot[0:64, :, 64:P],
                                                 bank[0:64, 0:P].rearrange("p (h m) -> p h m", h=2)))
                        for n, b in enumerate(LEVELS[1:], 1):
                            own.then(dve.copy_predicated(
                                slot.rearrange("p h (m w) -> p h m w", w=2 * b)[:, :, :, b:2 * b],
                                LM[:, n * 64:(n + 1) * 64].rearrange("p (m w) -> p m w", w=b)
                                .unsqueeze(1).to_broadcast([P, 2, 64 // b, b]),
                                bank[:, n * P:(n + 1) * P].rearrange("p (h m w) -> p h m w", h=2, w=b)))
                        dve.sem_inc(placed, 1)
                        dve.wait_ge(upd_done, step + 1)
                        if c < NT - 1:
                            if c >= 1:
                                dve.wait_ge(out_done, step)
                            for h, r in enumerate(rows):
                                v = slice(h * 64, (h + 1) * 64)
                                last = dve.scalar_tensor_tensor(
                                    ST[r, (c + 1) % 2, v], ST[r, c % 2, v], EL[r, c:c + 1],
                                    kit.psum[r, 7, v], ALU.mult, ALU.add)
                            last.then_inc(upd_taken, 1)
                            dve.wait_ge(upd_taken, (NT - 1) * p + c + 1)

            @block.scalar
            def _(act):
                own = Own(act, own_a)
                for p in range(NP):
                    g = tile_of[p]
                    if p == 0 or tile_of[p - 1] != g:
                        act.wait_ge(cums, g + 1)
                        for n, b in enumerate(LEVELS):
                            act.wait_ge(refs, NL * g + n + 1)
                            z = Z[:, n % 2, :].rearrange("p (m w) -> p m w", w=2 * b)
                            w = KW[:, n, :].rearrange("p (m w) -> p m w", w=2 * b)
                            act.activation(w[:, :, b:2 * b], z[:, :, b:2 * b], ACT.Exp)
                            act.activation(w[:, :, 0:b], z[:, :, 0:b], ACT.Exp, scale=-1.0).then_inc(weights, 1)
                        act.wait_ge(state_w, g + 1)
                        own(act.activation(QE, C, ACT.Exp))
                        own(act.activation(KL[:, :], Z[:, 0, :], ACT.Exp))
                        own(act.activation(EL[:, :].unsqueeze(2),
                                           C.rearrange("p (m w) -> p m w", w=P)[:, :, P - 1:P], ACT.Exp))
                        for c in range(2):
                            act.wait_ge(kt_done, 2 * g + c + 1)
                            act.activation(KLT[:, c * HALF:(c + 1) * HALF], kit.psum[:, 4 + c, :], ACT.Copy
                                           ).then_inc(kt_taken, 1)
                    for c in range(NT):
                        act.wait_ge(out_done, NT * p + c + 1)
                        act.activation(O[:, c, P * p:P * (p + 1)], kit.psum[:, 6, 0:P], ACT.Copy
                                       ).then_inc(out_taken, 1)

            @block.tensor
            def _(pe):
                def scores(p, c):
                    step = NT * p + c
                    if step >= 2:
                        pe.wait_ge(placed, step - 1)
                    bank = kit.pair(step % 2)
                    at = slice(c * P, (c + 1) * P)
                    for n in range(NL):
                        pe.matmul(bank[:, n * P:(n + 1) * P], KW[:, n, at],
                                  QW[:, n, c, :, :].rearrange("p h m -> p (h m)"), start=True, stop=True)
                    pe.matmul(bank[:, NL * P:NL * P + 2], QK[:, at], heads[:, 2 * p:2 * p + 2],
                              start=True, stop=True).then_inc(scored, 1)

                for p in range(NP):
                    g = tile_of[p]
                    V, v_at = (VA, P * p) if p < 2 else (VC, P * (p - 2))
                    pe.wait_ge(mixed, p + 1)
                    if p == 0 or tile_of[p - 1] != g:
                        for c in range(2):
                            if g:
                                pe.wait_ge(kt_taken, 2 * g + c - 1)
                            for n in range(4):
                                m = 4 * c + n
                                last = pe.transpose(kit.psum[:, 4 + c, n * P:(n + 1) * P],
                                                    KL[:, m * P:(m + 1) * P], ident)
                            last.then_inc(kt_done, 1)
                    scores(p, 0)
                    pe.wait_ge(kt_taken, 2 * g + 2)
                    for c in range(NT):
                        step = NT * p + c
                        if c + 1 < NT:
                            scores(p, c + 1)
                        if (NT - 1) * p + c:
                            pe.wait_ge(upd_taken, (NT - 1) * p + c)
                        pe.matmul(kit.psum[:, 7, 0:P], KLT[:, c * P:(c + 1) * P], V[:, c, v_at:v_at + P],
                                  start=True, stop=True).then_inc(upd_done, 1)
                        if step:
                            pe.wait_ge(out_taken, step)
                        pe.matmul(kit.psum[:, 6, 0:P], QE[:, c * P:(c + 1) * P], ST[:, c % 2, :],
                                  start=True, stop=False)
                        pe.wait_ge(placed, step + 1)
                        for h in range(2):
                            last = pe.matmul(kit.psum[:, 6, h * 64:(h + 1) * 64], SC[:, step % 2, h, :],
                                             V[:, c, v_at + h * 64:v_at + (h + 1) * 64], start=False,
                                             stop=h == 1)
                        last.then_inc(out_done, 1)


def head_norm_stage(kit, tag, O, parts, heads, width, gains, eps, copies, ident, scale=None, silu=True, also=()):
    nc = kit.nc
    also_in = kit.sem(f"{tag}_also_in")
    gain_in, sq, root, gated, sums, rows, turned, copied, own_d = (
        kit.sem(f"{tag}_{n}") for n in ("gain_in", "sq", "root", "gated", "sums", "rows", "turned", "copied",
                                        "own_d"))
    W = heads * width
    with ExitStack() as mem:
        G = sbuf(nc, mem, f"{tag}_G", [P, W])
        SQ = sbuf(nc, mem, f"{tag}_SQ", [P, 2, W])
        ss = sbuf(nc, mem, f"{tag}_ss", [P, NT, heads])
        eps_col = sbuf(nc, mem, f"{tag}_eps", [P, 1])
        with nc.Block() as block:
            @block.sync
            def _(sp):
                at = 0
                for g, n in gains:
                    sp.dma_start(G[:, at:at + n], bcast(g)).then_inc(gain_in, 16)
                    at += n
                for dst, src in also:
                    sp.dma_start(dst, src).then_inc(also_in, 16)
                if also:
                    sp.wait_ge(also_in, 16 * len(also))

            @block.scalar
            def _(act):
                for t in range(NT):
                    if t >= 2:
                        act.wait_ge(sums, t - 1)
                    act.activation(SQ[:, t % 2, :], O[:, t, 0:W], ACT.Square).then_inc(sq, 1)
                act.wait_ge(sums, NT)
                act.activation(ss, ss, ACT.Sqrt, scale=1.0 / width, bias=eps_col).then_inc(root, 1)
                if silu:
                    for at, n, gate in parts:
                        act.activation(gate, gate, ACT.Silu).then_inc(gated, 1)
                for t in range(NT):
                    act.wait_ge(turned, t + 1)
                    for n, (_, dst) in enumerate(copies):
                        ins = act.activation(dst[:, t * P:(t + 1) * P],
                                             kit.pair(t % 2)[:, n * P:(n + 1) * P], ACT.Copy)
                    ins.then_inc(copied, 1)

            @block.vector
            def _(dve):
                own = Own(dve, own_d)
                own(dve.memset(eps_col, eps))
                own.wait()
                dve.wait_ge(gain_in, 16 * len(gains))
                if scale is not None:
                    own.then(dve.tensor_scalar(G, G, scale, None, ALU.mult))
                for t in range(NT):
                    dve.wait_ge(sq, t + 1)
                    dve.tensor_reduce(ss[:, t, :], SQ[:, t % 2, :].rearrange("p (h w) -> p h w", h=heads),
                                      AX.X, ALU.add).then_inc(sums, 1)
                dve.wait_ge(root, 1)
                own.then(dve.reciprocal(ss, ss))
                if silu:
                    dve.wait_ge(gated, len(parts))
                for t in range(NT):
                    o = O[:, t, 0:W].rearrange("p (h w) -> p h w", h=heads)
                    own.then(dve.tensor_tensor(o, o, ss[:, t, :].unsqueeze(2).to_broadcast([P, heads, width]),
                                               ALU.mult))
                    own.then(dve.tensor_tensor(O[:, t, 0:W], O[:, t, 0:W], G, ALU.mult))
                    for n, (at, w, gate) in enumerate(parts):
                        ins = dve.tensor_tensor(O[:, t, at:at + w], O[:, t, at:at + w], gate[:, t, :], ALU.mult)
                    ins.then_inc(rows, 1)

            @block.tensor
            def _(pe):
                for t in range(NT):
                    pe.wait_ge(rows, t + 1)
                    if t >= 2:
                        pe.wait_ge(copied, t - 1)
                    for n, (c, _) in enumerate(copies):
                        last = pe.transpose(kit.pair(t % 2)[:, n * P:(n + 1) * P],
                                            O[:, t, c * P:(c + 1) * P], ident)
                    last.then_inc(turned, 1)


def residual_stage(kit, tag, tiles, w_view, X, alpha, chunk):
    nc = kit.nc
    K = len(tiles)
    n_chunks = D // chunk
    w_in = [kit.sem(f"{tag}_w_in{s}") for s in range(2)]
    products, added = kit.sem(f"{tag}_products"), kit.sem(f"{tag}_added")
    with ExitStack() as mem:
        W = sbuf(nc, mem, f"{tag}_W", [P, 2, K, chunk])
        with nc.Block() as block:
            @block.sync
            def _(sp):
                for c in range(n_chunks):
                    if c >= 2:
                        sp.wait_ge(products, NT * (c - 1))
                    sp.dma_start(W[:, c % 2, :, :], w_view[:, :, c * chunk:(c + 1) * chunk]
                                 ).then_inc(w_in[c % 2], 16)

            @block.tensor
            def _(pe):
                for c in range(n_chunks):
                    pe.wait_ge(w_in[c % 2], 16 * (c // 2 + 1))
                    for t in range(NT):
                        n = c * NT + t
                        if n >= 8:
                            pe.wait_ge(added, n - 7)
                        for k in range(K):
                            last = pe.matmul(kit.psum[:, n % 8, 0:chunk], tiles[k][:, t * P:(t + 1) * P],
                                             W[:, c % 2, k, :], start=k == 0, stop=k == K - 1)
                        last.then_inc(products, 1)

            @block.vector
            def _(dve):
                for n in range(n_chunks * NT):
                    c, t = divmod(n, NT)
                    dve.wait_ge(products, n + 1)
                    x = X[:, t, c * chunk:(c + 1) * chunk]
                    dve.scalar_tensor_tensor(x, x, alpha, kit.psum[:, n % 8, 0:chunk], ALU.mult, ALU.add
                                             ).then_inc(added, 1)


def ffn_stage(kit, XT, REST, X, d):
    nc = kit.nc
    GROUP = 7
    GROUPS = FT // GROUP
    RAW, SLOTS = 4, 2
    ITEMS = 4 * GROUP
    w_in = [kit.sem(f"ffn_w_in{s}") for s in range(RAW)]
    begun = kit.sem("ffn_begun")
    params, padded, split, rounded, used, banks, gate_out, conv, gelu, val_out, parts, added, own_d = (
        kit.sem(f"ffn_{n}") for n in ("params", "padded", "split", "rounded", "used", "banks", "gate_out", "conv",
                                      "gelu", "val_out", "parts", "added", "own_d"))
    SPLIT_CREDIT, USED_CREDIT, CONV_CREDIT, PARTS_CREDIT, ADDED_CREDIT = RAW, SLOTS, 2, 2, 1
    BANKS = 2 * (NT - 1)

    def width(i):
        return KT * P if i < 2 * GROUP else HALF

    with ExitStack() as mem:
        W = sbuf(nc, mem, "ffn_W", [P, RAW, KT * P])
        W1 = sbuf(nc, mem, "ffn_W1", [P, SLOTS, KT * P], FP32R)
        W2 = sbuf(nc, mem, "ffn_W2", [P, SLOTS, KT * P], FP32R)
        PR1 = sbuf(nc, mem, "ffn_PR1", [P, GROUP, S], FP32R)
        PR2 = sbuf(nc, mem, "ffn_PR2", [P, GROUP, S], FP32R)
        par = sbuf(nc, mem, "ffn_par", [P, 4, GROUP])
        G = sbuf(nc, mem, "ffn_G", [P, 2, 2 + S])
        Y = sbuf(nc, mem, "ffn_Y", [P, 2, S])
        with nc.Block() as block:
            @block.sync
            def _(sp):
                with sp.Fori(0, GROUPS) as g:
                    sp.wait_ge(conv, GROUP * g + CONV_CREDIT)
                    sp.dma_start(par.rearrange("p n f -> p (n f)"), d["ffn_par"][g]).then_inc(params, 16)
                    for i in range(ITEMS):
                        sp.wait_ge(split, ITEMS * g + (i + 1))
                        if i < 2 * GROUP:
                            src = d["ffn_w_val" if i % 2 else "ffn_w_gate"][GROUP * g + i // 2]
                        else:
                            c, j = divmod(i - 2 * GROUP, GROUP)
                            src = d["ffn_w_down"][GROUP * g + j][:, c * HALF:(c + 1) * HALF]
                        sp.dma_start(W[:, i % RAW, 0:width(i)], src).then_inc(w_in[i % RAW], 16)

            @block.gpsimd
            def _(pool):
                pool.sem_inc(split, SPLIT_CREDIT)
                with pool.Fori(0, GROUPS) as g:
                    for i in range(ITEMS):
                        w, w1, w2 = (a[:, i % n, 0:width(i)] for a, n in ((W, RAW), (W1, SLOTS), (W2, SLOTS)))
                        pool.wait_ge(w_in[i % RAW], 16 * (ITEMS // RAW) * g + 16 * (i // RAW + 1))
                        pool.wait_ge(used, ITEMS * g + (i + 1))
                        pool.sem_inc(begun, 1)
                        pool.tensor_copy(w1, w).then_inc(rounded, 1)
                        pool.wait_ge(rounded, ITEMS * g + (i + 1))
                        pool.tensor_tensor(w2, w, w1.bitcast(FP32), ALU.subtract).then_inc(split, 1)

            @block.tensor
            def _(pe):
                def wait_weights(g, i):
                    pe.wait_ge(split, ITEMS * g + (i + 1 + SPLIT_CREDIT))

                def three(out, a1, a2, b1, b2, start, stop):
                    pe.matmul(out, a1, b1, start=start, stop=False)
                    pe.matmul(out, a1, b2, start=False, stop=False)
                    return pe.matmul(out, a2, b1, start=False, stop=stop)

                def product(g, i, pair):
                    wait_weights(g, i)
                    w1, w2 = (a[:, i % SLOTS, :].rearrange("p (k m) -> p k m", k=KT) for a in (W1, W2))
                    for c in range(2):
                        for k in range(KT):
                            at = slice(c * HALF, (c + 1) * HALF)
                            last = three(kit.pair(pair)[:, at], w1[:, k, :], w2[:, k, :], XT[:, k, at],
                                         REST[:, k, at], k == 0, k == KT - 1)
                    last.then_inc(used, 1)

                pe.sem_inc(used, USED_CREDIT)
                with pe.Fori(0, GROUPS) as g:
                    for j in range(GROUP):
                        if j < 2:
                            pe.wait_ge(added, 2 * NT * g + ADDED_CREDIT)
                        else:
                            pe.wait_ge(gate_out, GROUP * g + (j - 1))
                        product(g, 2 * j, j % 2)
                        if j >= 2:
                            pe.wait_ge(val_out, GROUP * g + (j - 1))
                        product(g, 2 * j + 1, 2 + j % 2)
                    pe.wait_ge(gate_out, GROUP * g + GROUP)
                    for c in range(2):
                        for j in range(GROUP):
                            i = 2 * GROUP + c * GROUP + j
                            wait_weights(g, i)
                            if c == 0:
                                pe.wait_ge(parts, GROUP * g + (j + 1 + PARTS_CREDIT))
                            for n, t in enumerate((0, 1, 2, 3, 6, 7, 4, 5)):
                                if j == 0 and c == 0 and t in (6, 4):
                                    pe.wait_ge(val_out, GROUP * g + GROUP - (t == 6))
                                if j == 0 and c == 1:
                                    pe.wait_ge(added, 2 * NT * g + (n + 1 + ADDED_CREDIT))
                                at = slice(t * P, (t + 1) * P)
                                last = three(kit.psum[:, t, :], PR1[:, j, at], PR2[:, j, at],
                                             W1[:, i % SLOTS, 0:HALF], W2[:, i % SLOTS, 0:HALF],
                                             j == 0, j == GROUP - 1)
                                if j == GROUP - 1 and n < NT - 1:
                                    last.then_inc(banks, 1)
                            last.then_inc(used, 1)

            @block.scalar
            def _(act):
                act.wait_ge(padded, 1)

                def bend(g, j):
                    act.wait_ge(conv, GROUP * g + (j + 1 + CONV_CREDIT))
                    act.activation(Y[:, j % 2, :], Y[:, j % 2, :], ACT.Gelu_apprx_tanh).then_inc(gelu, 1)

                with act.Fori(0, GROUPS) as g:
                    for j in range(GROUP):
                        act.wait_ge(used, ITEMS * g + (2 * j + 1 + USED_CREDIT))
                        act.wait_ge(conv, GROUP * g + (j - 1 + CONV_CREDIT + (j == 0)))
                        act.activation(G[:, j % 2, 2:2 + S], kit.pair(j % 2), ACT.Copy).then_inc(gate_out, 1)
                        if j >= 1:
                            bend(g, j - 1)
                    bend(g, GROUP - 1)

            @block.vector
            def _(dve):
                def convolve(g, j, own):
                    x, y = G[:, j % 2, :], Y[:, j % 2, :]
                    dve.wait_ge(gate_out, GROUP * g + (j + 1))
                    dve.wait_ge(parts, GROUP * g + (j - 1 + PARTS_CREDIT + (j == 0)))
                    own.then(dve.tensor_scalar(y, x[:, 2:2 + S], par[:, 2, j:j + 1], par[:, 3, j:j + 1],
                                               ALU.mult, ALU.add))
                    own.then(dve.scalar_tensor_tensor(y, x[:, 0:S], par[:, 0, j:j + 1], y, ALU.mult, ALU.add))
                    dve.scalar_tensor_tensor(y, x[:, 1:1 + S], par[:, 1, j:j + 1], y, ALU.mult, ALU.add
                                             ).then_inc(conv, 1)

                def finish(g, j, own):
                    y = Y[:, j % 2, :]
                    dve.wait_ge(gelu, GROUP * g + (j + 1))
                    dve.wait_ge(used, ITEMS * g + (2 * j + 2 + USED_CREDIT))
                    dve.tensor_tensor(y, y, kit.pair(2 + j % 2), ALU.mult).then_inc(val_out, 1)
                    dve.wait_ge(val_out, GROUP * g + (j + 1))
                    own.then(dve.tensor_copy(PR1[:, j, :], y))
                    dve.tensor_tensor(PR2[:, j, :], y, PR1[:, j, :].bitcast(FP32), ALU.subtract
                                      ).then_inc(parts, 1)

                dve.memset(G[:, :, 0:2], 0.0).then_inc(padded, 1)
                dve.sem_inc(conv, CONV_CREDIT)
                dve.sem_inc(parts, PARTS_CREDIT)
                dve.sem_inc(added, ADDED_CREDIT)
                with dve.Fori(0, GROUPS) as g:
                    own = Own(dve, own_d, 3 * GROUP * g)
                    dve.wait_ge(params, 16 * g + 16)
                    for j in range(GROUP):
                        convolve(g, j, own)
                        if j >= 1:
                            finish(g, j - 1, own)
                    finish(g, GROUP - 1, own)
                    dve.wait_ge(added, 2 * NT * g + ADDED_CREDIT)
                    for c in range(2):
                        for n, t in enumerate((0, 1, 2, 3, 6, 7, 4, 5)):
                            if n < NT - 1:
                                dve.wait_ge(banks, BANKS * g + (c * (NT - 1) + n + 1))
                            else:
                                dve.wait_ge(used, ITEMS * g + ((3 + c) * GROUP + USED_CREDIT))
                            x = X[:, t, c * HALF:(c + 1) * HALF]
                            dve.tensor_tensor(x, x, kit.psum[:, t, :], ALU.add).then_inc(added, 1)


def first_block(kit, X, C, d):
    nc = kit.nc
    ident = C("ident")
    mixer = ExitStack()
    XT = sbuf(nc, mixer, "XT_mixer", [P, KT, S])
    tables = ExitStack()
    FIRST = sbuf(nc, tables, "FIRST", [P, ROPE_AT - FIRST_AT])
    level, heads, keep = FIRST[:, 0:7 * 64], FIRST[:, 7 * 64:7 * 64 + 8], FIRST[:, 7 * 64 + 8:]
    first_in = kit.sem("first_in")
    with nc.Block() as block:
        @block.sync
        def _(sp):
            sp.dma_start(FIRST, d["constants"][:, FIRST_AT:ROPE_AT]).then_inc(first_in, 16)
            sp.wait_ge(first_in, 16)
    norm_stage(kit, "mixnorm", X, XT, ident, d["norm_mix"])
    mix = ExitStack()
    with mix:
        BG = sbuf(nc, mix, "BG", [P, 4, S])
        gla = ExitStack()
        VA = sbuf(nc, gla, "VA", [P, NT, 512])
        VC = sbuf(nc, gla, "VC", [P, NT, 512])
        Q = sbuf(nc, gla, "Q", [P, 3, S])
        K = sbuf(nc, gla, "K", [P, 3, S])
        AF = sbuf(nc, gla, "AF", [P, 2, S])
        CLR = sbuf(nc, gla, "CLR", [16, S])
        lru = ExitStack()
        BX = sbuf(nc, lru, "BX", [P, 4, 3 + S])
        dst = ([Q[:, 0, :], Q[:, 1, :], AF[:, 0, :], AF[:, 1, :]] + [BX[:, j, 3:3 + S] for j in range(4)]
               + [BG[:, j, :] for j in range(4)] + [Q[:, 2, :], K[:, 2, :]])
        items = [(d["w_in_feat"][m], S) for m in range(14)] + [(d["w_in_lr"], KT * 16)]
        items += [(d["w_in_tok"][k * P:(k + 1) * P, :], 1024) for k in range(KT)]
        units = []
        for m in range(14):
            scale = 32 ** -0.5 if m == 12 else 1.0
            take = copy_into(dst[m], scale=scale) if m % 2 == 0 else copy_into_dve(dst[m])
            units.append(Unit("feature", [m], P, "act" if m % 2 == 0 else "dve", take))
        units.append(Unit("feature", [14], 16, "act", copy_into(CLR[:, :], rows=16)))
        for t in range(NT):
            def take(eng, psum, own, t=t):
                if t % 2:
                    own(eng.tensor_copy(VA[:, t, :], psum[:, 0:512]))
                    return eng.tensor_copy(VC[:, t, :], psum[:, 512:1024])
                eng.activation(VA[:, t, :], psum[:, 0:512], ACT.Copy)
                return eng.activation(VC[:, t, :], psum[:, 512:1024], ACT.Copy)
            units.append(Unit("token", list(range(15, 23)), 1024, "dve" if t % 2 else "act", take, t))
        product_stage(kit, "win", XT, items, units)
        pad = kit.sem("pad")
        with nc.Block() as block:
            @block.gpsimd
            def _(pool):
                pool.memset(BX[:, :, 0:3], 0.0).then_inc(pad, 1)
        rglru_stage(kit, BX, BG, XT, K[:, 0, :], d)
        lru.close()
        OM = sbuf(nc, gla, "OM", [P, NT, 512])
        LF = sbuf(nc, gla, "LF", [P, 3, S])
        gate_prep_stage(kit, AF, K[:, 0:2, :], CLR, LF, XT, d)
        gla_stage(kit, Q, K, LF, VA, VC, OM, XT, X, AF, ident, level, heads, keep)
        OT = XT
        head_norm_stage(kit, "hn", OM, [(0, 256, VA[:, :, 256:512]), (256, 256, VC[:, :, 256:512])], 8, 64,
                        [(d["hgrn_norm"], 256), (d["gla_norm"], 256)], EPS,
                        [(n, OT[:, n, :]) for n in range(4)], ident,
                        also=[(X, d["x"].rearrange("(t p) n -> p t n", p=P))])
        gla.close()
        tiles = [OT[:, 0, :], OT[:, 1, :]] + [BG[:, j, :] for j in range(4)] + [OT[:, 2, :], OT[:, 3, :]]
        residual_stage(kit, "wout", tiles, d["w_out"].rearrange("(k p) n -> p k n", p=P), X, 1.0, 512)
    tables.close()
    mixer.close()
    with ExitStack() as mem:
        H1 = sbuf(nc, mem, "H1", [P, KT, S], FP32R)
        H2 = sbuf(nc, mem, "H2", [P, KT, S], FP32R)
        norm_stage(kit, "ffnnorm", X, H1, ident, d["norm_ffn"], rest=H2)
        ffn_stage(kit, H1, H2, X, d)
    kit.clear_semaphores()


def keys_at(t):
    return P * t * (t + 1) // 2


KEYS = keys_at(NT)


def index_stage(kit, IQ, IW, IS, AM, causal):
    nc = kit.nc
    scored, bent, added, done, own_d = (kit.sem(f"ix_{n}") for n in ("scored", "bent", "added", "done", "own_d"))
    H = 8
    with ExitStack() as mem:
        R = sbuf(nc, mem, "ix_R", [P, 2, S])
        with nc.Block() as block:
            @block.tensor
            def _(pe):
                for t in range(NT):
                    n = P * (t + 1)
                    for h in range(H):
                        j = t * H + h
                        if j >= 2:
                            pe.wait_ge(bent, j - 1)
                        for c in range(0, n, HALF):
                            e = min(n, c + HALF)
                            last = pe.matmul(kit.pair(j % 2)[:, c:e], IQ[:, h // 2, t * P:(t + 1) * P],
                                             IQ[:, 4 + h % 2, c:e], start=True, stop=True)
                        last.then_inc(scored, 1)

            @block.scalar
            def _(act):
                for j in range(NT * H):
                    n = P * (j // H + 1)
                    act.wait_ge(scored, j + 1)
                    if j >= 2:
                        act.wait_ge(added, j - 1)
                    act.activation(R[:, j % 2, 0:n], kit.pair(j % 2)[:, 0:n], ACT.Relu).then_inc(bent, 1)

            @block.vector
            def _(dve):
                own = Own(dve, own_d)
                for t in range(NT):
                    n = P * (t + 1)
                    acc = kit.pair(2 + t % 2)[:, 0:n]
                    out = IS[:, keys_at(t):keys_at(t) + n]
                    for h in range(H):
                        j = t * H + h
                        dve.wait_ge(bent, j + 1)
                        if h:
                            dve.wait_ge(added, j)
                            ins = dve.scalar_tensor_tensor(out if h == H - 1 else acc, R[:, j % 2, 0:n],
                                                           IW[:, t, h:h + 1], acc, ALU.mult, ALU.add)
                        else:
                            ins = dve.tensor_scalar(acc, R[:, j % 2, 0:n], IW[:, t, h:h + 1], None, ALU.mult)
                        ins.then_inc(added, 1)
                    dve.wait_ge(added, (t + 1) * H)
                    own.then(dve.tensor_reduce(AM[:, t:t + 1], out, AX.X, ALU.max, apply_absolute_value=True))
                    dve.tensor_tensor(out[:, t * P:n], out[:, t * P:n], causal, ALU.add).then_inc(done, 1)
                dve.wait_ge(done, NT)


def topk_program(kit, mem, IS, AM, MB, A, B, R, causal):
    nc = kit.nc
    T0 = TOPK // P
    N = NT - T0
    own_d = kit.sem("tk_own_d")
    lo, hi, mid, cnt, left = (sbuf(nc, mem, f"tk_{n}", [P, N]) for n in ("lo", "hi", "mid", "cnt", "left"))
    ge = sbuf(nc, mem, "tk_ge", [P, 2, N], INT32)
    one = sbuf(nc, mem, "tk_one", [P, 1], BF16)

    def program(dve):
        own = Own(dve, own_d)
        own(dve.memset(one, 1.0))
        own(dve.memset(MB[:, 0:keys_at(T0)], 0.0))
        own.wait()
        for t in range(T0):
            own(dve.tensor_copy(MB[:, keys_at(t) + t * P:keys_at(t) + (t + 1) * P], causal))
        own(dve.tensor_scalar(lo, AM[:, T0:NT], -1.0, None, ALU.mult))
        own(dve.tensor_scalar(hi, AM[:, T0:NT], 1.0 + 2.0 ** -20, 1e-37, ALU.mult, ALU.add))
        own.wait()
        for i in range(BISECTIONS):
            own.then(dve.tensor_tensor(mid, lo, hi, ALU.add))
            own.then(dve.tensor_scalar(mid, mid, 0.5, None, ALU.mult))
            for t in range(T0, NT):
                n = P * (t + 1)
                own(dve.tensor_scalar(A[:, 0:n] if t % 2 else B[:, 0:n], IS[:, keys_at(t):keys_at(t) + n],
                                      mid[:, t - T0:t - T0 + 1], 0.0, ALU.is_ge, ALU.add,
                                      accum_out=cnt[:, t - T0:t - T0 + 1]))
                if t % 2:
                    own.wait()
            own.wait()
            own(dve.tensor_scalar(ge[:, 0, :], cnt, float(TOPK), None, ALU.is_ge))
            own(dve.tensor_scalar(ge[:, 1, :], cnt, float(TOPK), None, ALU.is_lt))
            own.wait()
            own(dve.copy_predicated(lo, ge[:, 0, :], mid))
            own(dve.copy_predicated(hi, ge[:, 1, :], mid))
            own.wait()
        for t in range(T0, NT):
            n = P * (t + 1)
            m = t - T0
            s = IS[:, keys_at(t):keys_at(t) + n]
            own(dve.tensor_scalar(A[:, 0:n], s, hi[:, m:m + 1], 0.0, ALU.is_ge, ALU.add,
                                  accum_out=cnt[:, m:m + 1]))
            own(dve.tensor_scalar(B[:, 0:n], s, lo[:, m:m + 1], None, ALU.is_ge))
            own.wait()
            own(dve.tensor_scalar(left[:, m:m + 1], cnt[:, m:m + 1], -1.0, float(TOPK), ALU.mult, ALU.add))
            own.then(dve.tensor_tensor(B[:, 0:n], B[:, 0:n], A[:, 0:n], ALU.subtract))
            own.then(dve.tensor_tensor_scan(R[:, 0:n], one.to_broadcast([P, n]), B[:, 0:n], 0.0, ALU.mult, ALU.add))
            own.then(dve.scalar_tensor_tensor(B[:, 0:n], R[:, 0:n], left[:, m:m + 1], B[:, 0:n],
                                              ALU.is_le, ALU.mult))
            own.then(dve.tensor_tensor(A[:, 0:n], A[:, 0:n], B[:, 0:n], ALU.add))
            own.then(dve.tensor_scalar(MB[:, keys_at(t):keys_at(t) + n], A[:, 0:n], 1.0, -NEG,
                                       ALU.subtract, ALU.mult))
    return program


def clear_stage(kit, tag, tiles):
    done = kit.sem(f"{tag}_done")
    with kit.nc.Block() as block:
        @block.gpsimd
        def _(pool):
            for t in tiles:
                pool.memset(t, 0.0).then_inc(done, 1)


def attend_stage(kit, tag, heads, q, k, v, dv, O, out_at, ident, identb, mask, masked_all, decay=None,
                 minus_lam=None, v_at=lambda h: 0, place=None, also=()):
    nc = kit.nc
    maps = 2 if minus_lam is not None else 1
    jobs = [(t, h) for t in range(NT) for h in range(heads)]
    J = len(jobs)
    RING = 3
    LAG = 2 if maps == 2 else 1
    groups = []
    for j, (t, h) in enumerate(jobs):
        for b in range(0, t + 1, 4):
            groups.append((j, b, min(t + 1, b + 4)))
    scored, greatest, exped, ready, turned, taken_a, taken_v, summed, out, own_d = (
        kit.sem(f"{tag}_{n}") for n in ("scored", "greatest", "exped", "ready", "turned", "taken_a", "taken_v",
                                        "summed", "out", "own_d"))

    def groups_of(j):
        return [g for g, (jj, _, _) in enumerate(groups) if jj == j]

    with ExitStack() as mem:
        if place is None:
            PR = sbuf(nc, mem, f"{tag}_PR", [P, RING, maps, S])
            PT = sbuf(nc, mem, f"{tag}_PT", [P, 2, NT, P])
        else:
            PR = place[:, 0:RING * maps * S].rearrange("p (r m n) -> p r m n", r=RING, m=maps)
            PT = place[:, RING * maps * S:(RING * maps + 2) * S].rearrange("p (s b n) -> p s b n", s=2, b=NT)
        nmax = sbuf(nc, mem, f"{tag}_nmax", [P, J, maps])
        sums = sbuf(nc, mem, f"{tag}_sums", [P, J, maps])
        inv = sbuf(nc, mem, f"{tag}_inv", [P, J, 2 * maps - 1])
        with nc.Block() as block:
            @block.sync
            def _(sp):
                for dst, src, sem in also:
                    sp.dma_start(dst, src).then_inc(sem, 16)

            @block.tensor
            def _(pe):
                def scores(j):
                    t, h = jobs[j]
                    n = P * (t + 1)
                    for m in range(maps):
                        i = j * maps + m
                        if i >= 2:
                            pe.wait_ge(exped, i - 1)
                        for c in range(0, n, HALF):
                            e = min(n, c + HALF)
                            dst = kit.pair(i % 2)
                            more = masked_all or e == n
                            pe.matmul(dst[:, c:e], q(h, m, t), k(h, m, c, e), start=True,
                                      stop=not (more or decay))
                            if decay:
                                lhs, rhs = decay(h, c, e)
                                last = pe.matmul(dst[:, c:e], lhs, rhs, start=False, stop=not more)
                            if more:
                                a = c if masked_all else t * P
                                last = pe.matmul(dst[:, a:e], identb, mask(t, a, e), start=False, stop=True)
                        last.then_inc(scored, 1)

                def turn(j):
                    if maps == 2:
                        pe.wait_ge(ready, j + 1)
                    else:
                        pe.wait_ge(exped, j + 1)
                    for g in groups_of(j):
                        _, b0, b1 = groups[g]
                        if g >= 2:
                            pe.wait_ge(taken_v if g % 2 else taken_a, g // 2)
                        for b in range(b0, b1):
                            last = pe.transpose(kit.psum[:, 4 + g % 2, (b - b0) * P:(b - b0 + 1) * P],
                                                PR[:, j % RING, 0, b * P:(b + 1) * P], ident)
                        last.then_inc(turned, 1)

                def weigh(j):
                    t, h = jobs[j]
                    g = groups_of(j)[-1]
                    pe.wait_ge(taken_a, g // 2 + 1)
                    if g:
                        pe.wait_ge(taken_v, (g + 1) // 2)
                    if j >= 2:
                        pe.wait_ge(out, j - 1)
                    for b in range(t + 1):
                        last = pe.matmul(kit.psum[:, 6 + j % 2, 0:P], PT[:, j % 2, b, :], v(h, b),
                                         start=b == 0, stop=b == t)
                    last.then_inc(summed, 1)

                for j in range(J + LAG + 1):
                    if j < J:
                        scores(j)
                    if 0 <= j - LAG < J:
                        turn(j - LAG)
                    if 0 <= j - LAG - 1 < J:
                        weigh(j - LAG - 1)

            def take_group(eng, g, sem, copy):
                j, b0, b1 = groups[g]
                eng.wait_ge(turned, g + 1)
                if j >= 2:
                    eng.wait_ge(summed, j - 1)
                copy(PT[:, j % 2, b0:b1, :].rearrange("p b n -> p (b n)"),
                     kit.psum[:, 4 + g % 2, 0:(b1 - b0) * P]).then_inc(sem, 1)

            @block.scalar
            def _(act):
                for j in range(J + LAG):
                    if j < J:
                        n = P * (jobs[j][0] + 1)
                        if j >= RING:
                            act.wait_ge(turned, groups_of(j - RING)[-1] + 1)
                        for m in range(maps):
                            i = j * maps + m
                            act.wait_ge(greatest, i + 1)
                            act.activation(PR[:, j % RING, m, 0:n], kit.pair(i % 2)[:, 0:n], ACT.Exp,
                                           bias=nmax[:, j, m:m + 1], accum_out=sums[:, j, m:m + 1]
                                           ).then_inc(exped, 1)
                    if j >= LAG:
                        for g in groups_of(j - LAG):
                            if g % 2 == 0:
                                take_group(act, g, taken_a, lambda o, i: act.activation(o, i, ACT.Copy))

            @block.vector
            def _(dve):
                own = Own(dve, own_d)

                def maxima(j):
                    n = P * (jobs[j][0] + 1)
                    for m in range(maps):
                        i = j * maps + m
                        dve.wait_ge(scored, i + 1)
                        dve.tensor_reduce(nmax[:, j, m:m + 1], kit.pair(i % 2)[:, 0:n], AX.X, ALU.max,
                                          negate=True).then_inc(greatest, 1)

                def norms(j):
                    dve.wait_ge(exped, (j + 1) * maps)
                    own(dve.reciprocal(inv[:, j, 0:maps], sums[:, j, :]))
                    if maps == 2:
                        n = P * (jobs[j][0] + 1)
                        own.wait()
                        own.then(dve.scalar_tensor_tensor(inv[:, j, 2:3], sums[:, j, 0:1], inv[:, j, 1:2],
                                                          minus_lam, ALU.mult, ALU.mult))
                        dve.scalar_tensor_tensor(PR[:, j % RING, 0, 0:n], PR[:, j % RING, 1, 0:n],
                                                 inv[:, j, 2:3], PR[:, j % RING, 0, 0:n],
                                                 ALU.mult, ALU.add).then_inc(ready, 1)

                def result(j):
                    t, h = jobs[j]
                    at = out_at + h * dv
                    dve.wait_ge(summed, j + 1)
                    a = v_at(h)
                    dve.tensor_scalar(O[:, t, at:at + dv], kit.psum[:, 6 + j % 2, a:a + dv], inv[:, j, 0:1], None,
                                      ALU.mult).then_inc(out, 1)

                for j in range(J + LAG + 1):
                    if j < J:
                        maxima(j)
                    if 0 <= j - 1 < J:
                        norms(j - 1)
                    if 0 <= j - LAG < J:
                        for g in groups_of(j - LAG):
                            if g % 2:
                                take_group(dve, g, taken_v, lambda o, i: dve.tensor_copy(o, i))
                    if 0 <= j - LAG - 1 < J:
                        own.wait()
                        result(j - LAG - 1)


def prepare_stage(kit, l, LAM, IW, VS, FF, FB, pick, pickb, identb, causalb, ident, causal, d):
    nc = kit.nc
    params, ff, exps, own_d, own_a = (kit.sem(f"pr_{n}") for n in ("params", "ff", "exps", "own_d", "own_a"))
    with ExitStack() as mem:
        LV = sbuf(nc, mem, "pr_LV", [P, 4, 64])
        dots = sbuf(nc, mem, "pr_dots", [P, 2])
        init = sbuf(nc, mem, "pr_init", [P, 2])
        bf = sbuf(nc, mem, "pr_bf", [4, 1])
        E = sbuf(nc, mem, "pr_E", [4, S])
        ones = sbuf(nc, mem, "pr_ones", [4, 1])
        part = sbuf(nc, mem, "pr_part", [4, S], BF16)
        with nc.Block() as block:
            @block.sync
            def _(sp):
                for n, name in enumerate(("lam_q1_2", "lam_q2_2", "lam_k1_2", "lam_k2_2")):
                    sp.dma_start(LV[:, n, :], bcast(d[name][l])).then_inc(params, 16)
                sp.dma_start(init, bcast(d["lam_init"][l])).then_inc(params, 16)
                with nc.allow_non_contiguous_dma(reason="four gate biases"):
                    sp.dma_start(bf, d["b_f_2"][l].rearrange("(p o) -> p o", o=1)).then_inc(params, 16)

            @block.scalar
            def _(act):
                act.wait_ge(params, 96)
                act.activation(E, FF, ACT.Abs, bias=bf).then_inc(own_a, 1)
                act.wait_ge(own_a, 1)
                act.activation(E, E, ACT.Exp, scale=-1.0).then_inc(own_a, 1)
                act.wait_ge(own_a, 2)
                act.activation(E, E, ACT.Ln, bias=1.0).then_inc(exps, 1)
                act.wait_ge(ff, 1)
                act.activation(dots, dots, ACT.Exp).then_inc(exps, 1)

            @block.vector
            def _(dve):
                own = Own(dve, own_d)
                own(dve.memset(ones, 1.0))
                own(dve.memset(FB, 0.0))
                own(dve.tensor_copy(pickb, pick))
                own(dve.tensor_copy(identb, ident))
                own(dve.tensor_copy(causalb, causal))
                own(dve.tensor_scalar(IW, VS[:, :, 64:72], IDX_SCALE, None, ALU.mult))
                dve.wait_ge(params, 96)
                own.then(dve.tensor_tensor(LV[:, 0:2, :], LV[:, 0:2, :], LV[:, 2:4, :], ALU.mult))
                dve.tensor_reduce(dots, LV[:, 0:2, :], AX.X, ALU.add).then_inc(ff, 1)
                dve.wait_ge(exps, 1)
                own.then(dve.tensor_scalar(FF, FF, bf, 0.0, ALU.add, ALU.min))
                own.then(dve.tensor_tensor(FF, FF, E, ALU.subtract))
                own(dve.tensor_tensor_scan(FF, ones.to_broadcast([4, S]), FF, 0.0, ALU.mult, ALU.subtract))
                own.wait()
                for n in range(3):
                    own.then(dve.tensor_copy(part, FF))
                    own(dve.tensor_copy(FB[32 * n:32 * n + 4, :], part))
                    if n < 2:
                        own.then(dve.tensor_tensor(FF, FF, part, ALU.subtract))
                dve.wait_ge(exps, 2)
                own.then(dve.tensor_tensor(LAM[:, 0:1], dots[:, 1:2], dots[:, 0:1], ALU.subtract))
                own(dve.tensor_tensor(LAM[:, 0:1], LAM[:, 0:1], init[:, 0:1], ALU.subtract))
                own(dve.tensor_copy(LAM[:, 1:2], init[:, 1:2]))
                own.wait()


def finish_stage(kit, tag, O, GATE, W, w_in, X, XT, g_subln, keep_scale, ln_g, ln_b, ident):
    nc = kit.nc
    H = 4
    gate_in = [kit.sem(f"{tag}_gate_in{s}") for s in range(2)]
    (gains, sq, summed, root, inverse, scaled, turned, mixed, products, stats, ln_root, rows, ln_turned,
     copied, own_d) = (kit.sem(f"{tag}_{n}") for n in (
         "gains", "sq", "summed", "root", "inverse", "scaled", "turned", "mixed", "products", "stats",
         "ln_root", "rows", "ln_turned", "copied", "own_d"))
    with ExitStack() as mem:
        GT = sbuf(nc, mem, f"{tag}_GT", [P, 2, KT, P])
        SQ = sbuf(nc, mem, f"{tag}_SQ", [P, 2, H * P])
        ss = sbuf(nc, mem, f"{tag}_ss", [P, NT, H])
        G = sbuf(nc, mem, f"{tag}_G", [P, D])
        B = sbuf(nc, mem, f"{tag}_B", [P, D])
        gain = sbuf(nc, mem, f"{tag}_gain", [P, 1])
        eps = sbuf(nc, mem, f"{tag}_eps", [P, 2])
        bn = sbuf(nc, mem, f"{tag}_bn", [P, 2, 6])
        mv = sbuf(nc, mem, f"{tag}_mv", [P, NT, 2])
        dev = sbuf(nc, mem, f"{tag}_dev", [P, NT])
        inv = sbuf(nc, mem, f"{tag}_inv", [P, NT])
        with nc.Block() as block:
            @block.sync
            def _(sp):
                def gates(t):
                    sp.dma_start(GT[:, t % 2], GATE[:, :, t * P:(t + 1) * P]).then_inc(gate_in[t % 2], 16)

                with nc.allow_non_contiguous_dma(reason="one gain per partition"):
                    sp.dma_start(gain, g_subln.rearrange("(p o) -> p o", o=1)).then_inc(gains, 16)
                gates(0)
                sp.dma_start(G, bcast(ln_g)).then_inc(gains, 16)
                sp.dma_start(B, bcast(ln_b)).then_inc(gains, 16)
                gates(1)
                for t in range(2, NT):
                    sp.wait_ge(mixed, t - 1)
                    gates(t)

            @block.scalar
            def _(act):
                for t in range(NT):
                    if t >= 2:
                        act.wait_ge(summed, t - 1)
                    act.activation(SQ[:, t % 2, :], O[:, t, 0:H * P], ACT.Square).then_inc(sq, 1)
                act.wait_ge(summed, NT + 1)
                act.activation(ss, ss, ACT.Sqrt, scale=1.0 / P, bias=eps[:, 0:1]).then_inc(root, 1)
                act.wait_ge(inverse, 1)
                for t in range(NT):
                    for h in range(H):
                        o = O[:, t, h * P:(h + 1) * P]
                        ins = act.activation(o, o, ACT.Copy, scale=ss[:, t, h:h + 1])
                    ins.then_inc(scaled, 1)
                for t in range(NT):
                    act.wait_ge(stats, t + 1)
                    act.activation(dev[:, t:t + 1], mv[:, t, 1:2], ACT.Sqrt, bias=eps[:, 1:2]).then_inc(ln_root, 1)
                    act.wait_ge(ln_turned, t + 1)
                    act.activation(XT[:, :, t * P:(t + 1) * P],
                                   kit.pair(1).rearrange("p (k n) -> p k n", k=KT), ACT.Copy).then_inc(copied, 1)

            @block.vector
            def _(dve):
                own = Own(dve, own_d)
                own(dve.memset(eps[:, 0:1], SUBLN_EPS))
                own.then(dve.memset(eps[:, 1:2], LN_EPS))
                for t in range(NT):
                    dve.wait_ge(sq, t + 1)
                    dve.tensor_reduce(ss[:, t, :], SQ[:, t % 2, :].rearrange("p (h w) -> p h w", h=H),
                                      AX.X, ALU.add).then_inc(summed, 1)
                dve.sem_inc(summed, 1)
                dve.wait_ge(gains, 48)
                own.then(dve.tensor_scalar(gain, gain, keep_scale, None, ALU.mult))
                dve.wait_ge(root, 1)
                dve.reciprocal(ss, ss).then_inc(inverse, 1)

                def gate(t):
                    dve.wait_ge(gate_in[t % 2], 16 * (t // 2 + 1))
                    dve.wait_ge(turned, t + 1)
                    psum = kit.pair(0).rearrange("p (k n) -> p k n", k=KT)
                    at = slice(t * P, (t + 1) * P)
                    dve.scalar_tensor_tensor(XT[:, 0:H, at], psum[:, 0:H, :], gain, GT[:, t % 2, 0:H, :],
                                             ALU.mult, ALU.mult)
                    dve.tensor_tensor(XT[:, H:, at], psum[:, H:, :], GT[:, t % 2, H:, :], ALU.mult
                                      ).then_inc(mixed, 1)

                gate(0)
                for t in range(NT):
                    if t + 1 < NT:
                        gate(t + 1)
                    x = X[:, t, :]
                    dve.wait_ge(products, t + 1)
                    own.then(dve.scalar_tensor_tensor(x, x, ALPHA, kit.pair(2 + t % 2), ALU.mult, ALU.add))
                    for n in range(2):
                        own(dve.bn_stats(bn[:, n, :], x[:, n * HALF:(n + 1) * HALF]))
                    own.wait()
                    dve.bn_aggr(mv[:, t, :], bn).then_inc(stats, 1)
                    dve.wait_ge(ln_root, t + 1)
                    own.then(dve.reciprocal(inv[:, t:t + 1], dev[:, t:t + 1]))
                    own.then(dve.tensor_scalar(x, x, mv[:, t, 0:1], inv[:, t:t + 1], ALU.subtract, ALU.mult))
                    own.then(dve.tensor_tensor(x, x, G, ALU.mult))
                    dve.tensor_tensor(x, x, B, ALU.add).then_inc(rows, 1)

            @block.tensor
            def _(pe):
                def turn(t):
                    pe.wait_ge(scaled, t + 1)
                    if t:
                        pe.wait_ge(mixed, t)
                    for k in range(KT):
                        last = pe.transpose(kit.pair(0)[:, k * P:(k + 1) * P], O[:, t, k * P:(k + 1) * P], ident)
                    last.then_inc(turned, 1)

                def turn_norm(t):
                    pe.wait_ge(rows, t + 1)
                    if t:
                        pe.wait_ge(copied, t)
                    for k in range(KT):
                        last = pe.transpose(kit.pair(1)[:, k * P:(k + 1) * P], X[:, t, k * P:(k + 1) * P], ident)
                    last.then_inc(ln_turned, 1)

                turn(0)
                for t in range(NT):
                    if t + 1 < NT:
                        turn(t + 1)
                    else:
                        pe.wait_ge(mixed, NT)
                    if t >= 2:
                        pe.wait_ge(rows, t - 1)
                    for c in range(2):
                        if t == 0:
                            pe.wait_ge(w_in[c], 16)
                        for k in range(KT):
                            last = pe.matmul(kit.pair(2 + t % 2)[:, c * HALF:(c + 1) * HALF],
                                             XT[:, k, t * P:(t + 1) * P], W[:, k, c * HALF:(c + 1) * HALF],
                                             start=k == 0, stop=k == KT - 1)
                    last.then_inc(products, 1)
                    if t:
                        turn_norm(t - 1)
                turn_norm(NT - 1)


def packed(w, c, e):
    return [(w[2 * k * P:(2 * k + 2) * P, c:e].rearrange("(a p) n -> p a n", a=2), 2 * (e - c))
            for k in range(KT // 2)]


def layer(kit, l, X, XT, C, cos, sin, LAM, OM, GATE, d):
    nc = kit.nc
    ident, causal, swap = C("ident"), C("causal"), C("swap")
    pick = C("pick").rearrange("p (h n) -> p h n", h=4)
    w_feat, w_tok = d["w2_feat"][l], d["w2_tok"][l]
    attn, ends = ExitStack(), ExitStack()
    with attn:
        identb = sbuf(nc, attn, "identb", [P, P], BF16)
        causalb = sbuf(nc, attn, "causalb", [P, P], BF16)
        early = ExitStack()
        SQ = sbuf(nc, early, "SQ", [P, 4, S])
        FQ = sbuf(nc, early, "FQ", [P, 6, S])
        VS = sbuf(nc, early, "VS", [P, NT, 328])
        FB = sbuf(nc, early, "FB", [P, S], BF16)
        pickb = sbuf(nc, early, "pickb", [P, 4, P], BF16)
        AM = sbuf(nc, early, "AM", [P, NT])
        MB = sbuf(nc, early, "MB", [P, KEYS], BF16)
        index = ExitStack()
        IW = sbuf(nc, index, "IW", [P, NT, 8])
        FF = sbuf(nc, index, "FF", [4, S])
        IQ = sbuf(nc, index, "IQ", [P, 6, S])
        items = [(w_feat[m], S) for m in range(8)] + [(d["w2_ff"][l], KT * 4)]
        items += packed(w_tok, 0, 328)
        dst = [SQ[:, 0, :], SQ[:, 1, :], None] + [IQ[:, j, :] for j in range(4)] + [None]
        split = {2: (SQ[:, 2, :], SQ[:, 3, :]), 7: (IQ[:, 4, :], IQ[:, 5, :])}
        units = []

        def take_keys(pair):
            def take(act, psum, own):
                act.activation(FQ[0:64, 2 + 2 * pair, :], psum[0:64, :], ACT.Copy)
                return act.activation(FQ[64:P, 3 + 2 * pair, :], psum[64:P, :], ACT.Copy)
            return take

        for m in range(8):
            units.append(Unit("feature", [m], P, "rope", (dst[m], QK_SCALE if m < 2 else 1.0, split.get(m))))
        units.append(Unit("feature", [8], 4, "act", copy_into(FF, rows=4)))
        for t in range(NT):
            units.append(Unit("token", list(range(9, 13)), 328, "act", copy_into(VS[:, t, :]), t))
        clear_stage(kit, "za", [t[64 * (1 - i % 2):64 * (2 - i % 2), :] for i, t in enumerate(
            [SQ[:, 2, :], SQ[:, 3, :], IQ[:, 4, :], IQ[:, 5, :]] + [FQ[:, 2 + j, :] for j in range(4)])])
        product_stage(kit, "pa", XT, items, units, rope=(cos, sin, swap), place=OM,
                      rot_place=MB[:, 0:4 * S].bitcast(FP32).rearrange("p (a n) -> p a n", a=2))
        prepare_stage(kit, l, LAM, IW, VS, FF, FB, pick, pickb, identb, causalb, ident, causal, d)
        IS = OM.rearrange("p t n -> p (t n)")[:, 0:KEYS]
        index_stage(kit, IQ, IW, IS, AM, causal)
        index.close()
        late = ExitStack()
        DV = ends.enter_context(nc.sbuf_tensor("DV", [P, NT, 512], FP32, side="right"))[:, :, :]
        with ExitStack() as mem:
            room = OM.rearrange("p t n -> p (t n)")[:, KEYS:]
            staged = [room[:, n * S:(n + 1) * S] for n in range(2)]
            flags = sbuf(nc, mem, "flags", [P, S], BF16)
            topk = topk_program(kit, mem, IS, AM, MB, flags, room[:, 3 * S:3 * S + S // 2].bitcast(BF16),
                                room[:, 2 * S:3 * S], causal)
            items = [(w_feat[8 + m], S) for m in range(12)] + packed(w_tok, 328, 840)
            units = [Unit("feature", [m], P, "act", copy_into(FQ[:, m, :], scale=QK_SCALE)) for m in range(2)]
            units += [Unit("feature", [2 + m], P, "act", take_keys(m)) for m in range(2)]
            units += [Unit("feature", [4 + m], P, "act",
                           lambda act, psum, own, m=m: act.activation(staged[m % 2], psum, ACT.Silu),
                           store=(GATE[:, m, :], staged[m % 2])) for m in range(KT)]
            units += [Unit("token", list(range(12, 16)), 512, "act", copy_into(DV[:, t, :]), t)
                      for t in range(NT)]
            product_stage(kit, "tk", XT, items, units, slots=4, beside=topk)

        attend_stage(kit, "sp", 4, lambda h, m, t: SQ[:, h // 2, t * P:(t + 1) * P],
                     lambda h, m, c, e: SQ[:, 2 + h % 2, c:e], lambda h, b: VS[:, b, 0:P], 64, OM, 512,
                     ident, identb, lambda t, c, e: MB[:, keys_at(t) + c:keys_at(t) + e], True)
        attend_stage(kit, "fg", 4, lambda h, m, t: FQ[:, h // 2, t * P:(t + 1) * P],
                     lambda h, m, c, e: FQ[:, 2 + h, c:e],
                     lambda h, b: VS[:, b, 72 + P * (h // 2):200 + P * (h // 2)], 64, OM, 768, ident, identb,
                     lambda t, c, e: causalb, False,
                     v_at=lambda h: 64 * (h % 2),
                     decay=lambda h, c, e: (pickb[:, h, :], FB[:, c:e]))
        early.close()
        DQ = sbuf(nc, late, "DQ", [P, 12, S])
        items = [(w_feat[20 + m], S) for m in range(8)]
        units = [Unit("feature", [m], P, "rope", (DQ[:, m, :], QK_SCALE, None)) for m in range(4)]
        units += [Unit("feature", [m], P, "rope", (None, 1.0, (DQ[:, 2 * m - 4, :], DQ[:, 2 * m - 3, :])))
                  for m in range(4, 8)]
        clear_stage(kit, "zd", [DQ[64 * (1 - m % 2):64 * (2 - m % 2), 4 + m, :] for m in range(8)])
        product_stage(kit, "pd", XT, items, units, slots=4, rope=(cos, sin, swap))
        W = ends.enter_context(nc.sbuf_tensor("W_out", [P, KT, D], FP32, side="right"))[:, :, :]
        w_out = d["w_out_2"][l].rearrange("(k p) n -> p k n", p=P)
        w_out_in = [kit.sem(f"w_out_in{c}") for c in range(2)]
        attend_stage(kit, "df", 4, lambda h, m, t: DQ[:, h, t * P:(t + 1) * P],
                     lambda h, m, c, e: DQ[:, 4 + 2 * h + m, c:e],
                     lambda h, b: DV[:, b, 128 * h:128 * h + 128], 128, OM, 0, ident, identb,
                     lambda t, c, e: causalb, False, minus_lam=LAM[:, 0:1],
                     place=XT.rearrange("p k n -> p (k n)"),
                     also=[(W[:, :, c * HALF:(c + 1) * HALF], w_out[:, :, c * HALF:(c + 1) * HALF], w_out_in[c])
                           for c in range(2)])
        late.close()
    with ends:
        finish_stage(kit, "fin", OM, GATE, W, w_out_in, X, XT, d["g_subln_2"][l], LAM[:, 1:2], d["ln_g_2"][l],
                     d["ln_b_2"][l], ident)


def second_block(kit, X, XT, C, d):
    nc = kit.nc
    with ExitStack() as mem:
        ROPE = sbuf(nc, mem, "ROPE", [P, 2 * S])
        LAM = sbuf(nc, mem, "LAM", [P, 2])
        OM = sbuf(nc, mem, "OM2", [P, NT, D])
        GATE = nc.dram_tensor("GATE", (P, KT, S), FP32).ap()
        tables = kit.sem("tables")
        with nc.Block() as block:
            @block.sync
            def _(sp):
                sp.dma_start(ROPE, d["constants"][:, ROPE_AT:ROPE_AT + 2 * S]).then_inc(tables, 16)
                sp.wait_ge(tables, 16)
        kit.clear_semaphores()
        with nc.Fori(0, DEPTH_2) as l:
            layer(kit, l, X, XT, C, ROPE[:, 0:S], ROPE[:, S:2 * S], LAM, OM, GATE, d)
            kit.clear_semaphores()


def build(nc, d, out):
    ctx = ExitStack()
    with ctx:
        kit = Kit(nc, ctx)
        X = sbuf(nc, ctx, "X", [P, NT, D])
        CONST = sbuf(nc, ctx, "CONST", [P, FIRST_AT])

        def C(name):
            at, width = CONST_AT[name]
            return CONST[:, at:at + width]

        loaded = kit.sem("loaded")
        with nc.Block() as block:
            @block.sync
            def _(sp):
                sp.dma_start(X[:, :, :], d["x"].rearrange("(t p) n -> p t n", p=P)).then_inc(loaded, 16)
                sp.dma_start(CONST[:, :], d["constants"][:, 0:FIRST_AT]).then_inc(loaded, 16)
                sp.wait_ge(loaded, 32)
        first_block(kit, X, C, d)
        XT = sbuf(nc, ctx, "XT", [P, KT, S])
        norm_stage(kit, "finalnorm", X, XT, C("ident"), d["norm_final"], keep=True)
        second_block(kit, X, XT, C, d)
        stored = kit.sem("stored")
        with nc.Block() as block:
            @block.sync
            def _(sp):
                sp.dma_start(out.rearrange("(t p) n -> p t n", p=P), X[:, :, :]).then_inc(stored, 16)
                sp.wait_ge(stored, 16)


def _feature_tiles(w):
    k, n = w.shape
    return np.ascontiguousarray(w.reshape(k // P, P, n // P, P).transpose(2, 1, 0, 3)).reshape(n // P, P, k)


def _narrow_tile(w):
    k, m = w.shape
    return np.ascontiguousarray(w.reshape(k // P, P, m).transpose(1, 0, 2)).reshape(P, -1)


def layout(inputs):
    a = {n: np.asarray(v) for n, v in inputs.items()}
    d = {"x": a["x"][0], "constants": constants()}
    for n in ("norm_mix", "hgrn_lower_bounds", "hgrn_norm", "rg_conv_w", "rg_conv_b", "rg_w_a", "rg_b_a",
              "rg_w_x", "rg_b_x", "rg_lambda", "gla_w_gate_up", "gla_b_gate", "gla_norm", "w_out", "norm_ffn"):
        d[n] = a[n][0]
    d["norm_final"] = a["norm_final"]
    at = np.cumsum([0, 256, 256, 256, 256, 512, 512, 128, 128, 256, 256, 16])
    aq, af, ai, ag, bx, bg, cq, ck, cv, cg, lr = [a["w_in"][0][:, at[n]:at[n + 1]] for n in range(11)]
    d["w_in_feat"] = _feature_tiles(np.concatenate([aq, af, bx, bg, cq, ck], 1))
    d["w_in_lr"] = _narrow_tile(lr)
    d["w_in_tok"] = np.concatenate([ai, ag, cv, cg], 1)
    d["ffn_w_gate"] = _feature_tiles(a["ffn_w_gate"][0])
    d["ffn_w_val"] = _feature_tiles(a["ffn_w_val"][0])
    d["ffn_w_down"] = a["ffn_w_down"][0].reshape(FT, P, D)
    d["ffn_par"] = np.concatenate([a["ffn_conv_w"][0], a["ffn_conv_b"]], 0).reshape(
        4, FT // 7, 7, P).transpose(1, 3, 0, 2).reshape(FT // 7, P, 28)
    at = np.cumsum([0, 512, 512, 512, 256, 64, 64, 512, 64, 8, 256, 256, 256, 4, 1024])
    feats, toks, narrow = [], [], []
    for l in range(DEPTH_2):
        dq, dk, dv, sq, sk, sv, iq, ik, iw, fq, fk, fv, ff, gate = [
            a["w_in_2"][l][:, at[n]:at[n + 1]] for n in range(14)]
        feats.append(_feature_tiles(np.concatenate([sq, sk, sk, iq, ik, ik, fq, fk,
                                                      gate, dq, dk], 1)))
        toks.append(np.concatenate([sv, iw, fv, dv], 1))
        narrow.append(_narrow_tile(ff))
    d["w2_feat"], d["w2_tok"], d["w2_ff"] = np.stack(feats), np.stack(toks), np.stack(narrow)
    for n in ("b_f", "lam_q1", "lam_k1", "lam_q2", "lam_k2", "g_subln", "w_out", "ln_g", "ln_b"):
        d[n + "_2"] = a[n + "_2"]
    init = [0.8 - 0.6 * math.exp(-0.3 * l) for l in range(DEPTH_2)]
    d["lam_init"] = np.array([[i, 1.0 - i] for i in init], np.float32)
    return {n: np.ascontiguousarray(v) for n, v in d.items()}


def kernel(**inputs):
    import concourse.bacc as _bacc
    from concourse.bass_utils import run_bass_kernel_spmd as _run

    nc = _bacc.Bacc("TRN2", target_bir_lowering=False, num_devices=1)
    arrays = {f"in_{n}": v for n, v in layout(inputs).items()}
    d = {n[3:]: nc.dram_tensor(n, v.shape, mybir.dt.from_np(v.dtype), kind="ExternalInput").ap()
         for n, v in arrays.items()}
    out = nc.dram_tensor("out_x", (S, D), FP32, kind="ExternalOutput").ap()
    build(nc, d, out)
    r = _run(nc, [arrays], core_ids=[0])
    return r.results[0]["out_x"].reshape(1, S, D)
```

```python
import math
from contextlib import ExitStack

import numpy as np

import concourse.bass as bass
from concourse import mybir

FP32 = mybir.dt.float32
FP32R = mybir.dt.float32r
BF16 = mybir.dt.bfloat16
INT32 = mybir.dt.int32
ACT = mybir.ActivationFunctionType
ALU = mybir.AluOpType
AX = mybir.AxisListType

P = 128
S = 1024
D = 1024
NT = S // P
KT = D // P
HALF = 512
EPS = 1e-6
LN_EPS = 1e-5
SUBLN_EPS = 1e-5
F_FLOOR = 1e-20
LRU_C = 8.0
NEG = -1e30
D_FF = 2688
FT = D_FF // P
DEPTH_2 = 2
ALPHA = (2 * DEPTH_2) ** 0.25
IDX_SCALE = 512 ** -0.5
TOPK = 256
BISECTIONS = 32
QK_SCALE = 64 ** -0.5

LEVELS = [64, 32, 16, 8, 4, 2, 1]
PASS_ROWS = [(0, 64), (0, 64), (0, 32), (64, 32)]

CONST_AT = {}


def _const_columns():
    at = 0
    for name, width in (("ident", P), ("swap", P), ("causal", P), ("pick", 4 * P),
                        ("level", 7 * 64), ("heads", 8), ("keep", S), ("cos", S), ("sin", S)):
        CONST_AT[name] = (at, width)
        at += width
    return at


CONST_WIDTH = _const_columns()
FIRST_AT = CONST_AT["level"][0]
ROPE_AT = CONST_AT["cos"][0]


def constants():
    c = np.zeros((P, CONST_WIDTH), np.float32)

    def put(name, value):
        at, width = CONST_AT[name]
        c[:, at:at + width] = value

    put("ident", np.eye(P))
    j = np.arange(P)
    swap = np.zeros((P, P))
    swap[j, (j // 64) * 64 + (j + 32) % 64] = 1.0
    put("swap", swap)
    put("causal", np.where(j[None, :] > j[:, None], NEG, 0.0))
    level = np.zeros((P, 7, 64))
    for n, b in enumerate(LEVELS):
        i = np.arange(64)
        block = i // b
        level[:, n, :] = (j[:, None] // (2 * b) == block[None, :]) & (j[:, None] % (2 * b) < b)
    put("level", level.reshape(P, -1))
    heads = np.zeros((P, 4, 2))
    for n, (first, dk) in enumerate(PASS_ROWS):
        for h in range(2):
            heads[first + h * dk:first + (h + 1) * dk, n, h] = 1.0
    put("heads", heads.reshape(P, -1))
    keep = np.ones(S)
    keep[::P] = 0.0
    put("keep", keep[None, :])
    pick = np.zeros((P, 4, P))
    for h in range(4):
        pick[[h, 32 + h, 64 + h], h, :] = 1.0
    put("pick", pick.reshape(P, -1))
    inv = (np.float32(10000.0) ** (-np.arange(0, 64, 2, dtype=np.float32) / np.float32(64))).astype(np.float32)
    angle = (np.arange(S, dtype=np.float32)[:, None] * inv[None, :]).astype(np.float32)
    cos, sin = np.cos(angle).T, np.sin(angle).T
    put("cos", np.concatenate([cos] * 4))
    put("sin", np.concatenate([sin, -sin] * 2))
    return c


class Kit:

    def __init__(self, nc, ctx):
        self.nc, self.ctx = nc, ctx
        self.psum = ctx.enter_context(nc.psum_tensor("psum", [P, 8, HALF], FP32))
        self.sems, self.sem_ctx = [], ctx.enter_context(ExitStack())

    def sem(self, name):
        s = self.sem_ctx.enter_context(self.nc.semaphore(name))
        self.sems.append(s)
        return s

    def clear_semaphores(self):
        with self.nc.Block() as block:
            @block.sync
            def _(sp):
                for sem in self.sems:
                    sp.sem_clear(sem)
        self.sem_ctx.close()
        self.sems = []

    def pair(self, n):
        return self.psum[:, 2 * n:2 * n + 2, :].rearrange("p b n -> p (b n)")


class Own:

    def __init__(self, eng, sem, base=0):
        self.eng, self.sem, self.base, self.n = eng, sem, base, 0

    def __call__(self, instruction):
        instruction.then_inc(self.sem, 1)
        self.n += 1
        return self.n

    def wait(self, n=None):
        self.eng.wait_ge(self.sem, self.base + (self.n if n is None else n))

    def then(self, instruction):
        self(instruction)
        self.wait()


def sbuf(nc, stack, name, shape, dtype=FP32, side="left"):
    return stack.enter_context(nc.sbuf_tensor(name, shape, dtype, side=side))[(slice(None),) * len(shape)]


def bcast(row_ap):
    return row_ap.partition_broadcast(P)


def norm_stage(kit, tag, X, XT, ident, gain, bias=None, eps=EPS, keep=False, rest=None,
               store=None, load=None, also=()):
    nc = kit.nc
    layer = bias is not None
    stored, also_in = kit.sem(f"{tag}_stored"), kit.sem(f"{tag}_also_in")
    x_in = [kit.sem(f"{tag}_x_in{t}") for t in range(NT)] if load is not None else None
    gain_in, squares, stats, root, rows, turned, copied, parted, dve_own = (
        kit.sem(f"{tag}_{n}") for n in ("gain_in", "squares", "stats", "root", "rows", "turned", "copied",
                                        "parted", "dve_own"))
    with ExitStack() as mem:
        G = sbuf(nc, mem, f"{tag}_G", [P, D])
        B = sbuf(nc, mem, f"{tag}_B", [P, D]) if layer else None
        H = None if keep else sbuf(nc, mem, f"{tag}_H", [P, 2, D])
        junk = sbuf(nc, mem, f"{tag}_junk", [P, D])
        sums = sbuf(nc, mem, f"{tag}_sums", [P, NT])
        bn = sbuf(nc, mem, f"{tag}_bn", [P, NT, 2, 6])
        mv = sbuf(nc, mem, f"{tag}_mv", [P, NT, 2])
        eps_col = sbuf(nc, mem, f"{tag}_eps", [P, 1])
        dev = sbuf(nc, mem, f"{tag}_dev", [P, NT])
        inv = sbuf(nc, mem, f"{tag}_inv", [P, NT])
        with nc.Block() as block:
            @block.sync
            def _(sp):
                if load is not None:
                    for t in range(NT):
                        sp.dma_start(X[:, t, :], load[t * P:(t + 1) * P, :]).then_inc(x_in[t], 16)
                sp.dma_start(G[:, :], bcast(gain)).then_inc(gain_in, 16)
                for dst, src in also:
                    sp.dma_start(dst, src).then_inc(also_in, 16)
                if also:
                    sp.wait_ge(also_in, 16 * len(also))
                if layer:
                    sp.dma_start(B[:, :], bcast(bias)).then_inc(gain_in, 16)
                if store is not None:
                    for t in range(NT):
                        sp.wait_ge(rows, t + 1)
                        sp.dma_start(store[t * P:(t + 1) * P, :], X[:, t, :]).then_inc(stored, 16)
                    sp.wait_ge(stored, 16 * NT)

            @block.scalar
            def _(act):
                if not layer:
                    for t in range(NT):
                        if load is not None:
                            act.wait_ge(x_in[t], 16)
                        act.activation(junk[:, :], X[:, t, :], ACT.Square,
                                       accum_out=sums[:, t:t + 1]).then_inc(squares, 1)
                        act.wait_ge(squares, t + 1)
                act.wait_ge(stats, NT + 1 if layer else 1)
                src = mv[:, :, 1] if layer else sums[:, :]
                act.activation(dev[:, :], src, ACT.Sqrt, scale=1.0 if layer else 1.0 / D,
                               bias=eps_col[:, :]).then_inc(root, 1)
                for t in range(NT):
                    act.wait_ge(turned, t + 1)
                    act.activation(XT[:, :, t * P:(t + 1) * P],
                                   kit.pair(t % 2).rearrange("p (k n) -> p k n", k=KT),
                                   ACT.Copy).then_inc(copied, 1)

            @block.vector
            def _(dve):
                own = Own(dve, dve_own)
                if layer:
                    for t in range(NT):
                        for n in range(2):
                            own(dve.bn_stats(bn[:, t, n, :], X[:, t, n * HALF:(n + 1) * HALF]))
                        own.wait()
                        dve.bn_aggr(mv[:, t, :], bn[:, t, :, :]).then_inc(stats, 1)
                dve.memset(eps_col[:, :], eps).then_inc(stats, 1)
                dve.wait_ge(root, 1)
                own.then(dve.reciprocal(inv[:, :], dev[:, :]))
                dve.wait_ge(gain_in, 32 if layer else 16)

                def norm(t):
                    out = X[:, t, :] if keep else H[:, t % 2, :]
                    if not keep and t >= 2:
                        dve.wait_ge(turned, t - 1)
                    if layer:
                        own.then(dve.tensor_scalar(out, X[:, t, :], mv[:, t, 0:1], inv[:, t:t + 1],
                                                   ALU.subtract, ALU.mult))
                        own.then(dve.tensor_tensor(out, out, G[:, :], ALU.mult))
                        dve.tensor_tensor(out, out, B[:, :], ALU.add).then_inc(rows, 1)
                    else:
                        dve.scalar_tensor_tensor(out, X[:, t, :], inv[:, t:t + 1], G[:, :],
                                                 ALU.mult, ALU.mult).then_inc(rows, 1)

                for t in range(NT + 1):
                    if t < NT:
                        norm(t)
                    if rest is not None and t:
                        at = slice((t - 1) * P, t * P)
                        dve.wait_ge(copied, t)
                        dve.tensor_tensor(rest[:, :, at], kit.pair((t - 1) % 2).rearrange("p (k n) -> p k n", k=KT),
                                          XT[:, :, at].bitcast(FP32), ALU.subtract).then_inc(parted, 1)

            @block.tensor
            def _(pe):
                for t in range(NT):
                    src = X[:, t, :] if keep else H[:, t % 2, :]
                    pe.wait_ge(rows, t + 1)
                    if t >= 2:
                        pe.wait_ge(copied if rest is None else parted, t - 1)
                    for k in range(KT):
                        last = pe.transpose(kit.pair(t % 2)[:, k * P:(k + 1) * P],
                                            src[:, k * P:(k + 1) * P], ident)
                    last.then_inc(turned, 1)


def three_products(pe, out, a1, a2, b1, b2, start, stop):
    pe.matmul(out, a1, b1, start=start, stop=False)
    pe.matmul(out, a1, b2, start=False, stop=False)
    return pe.matmul(out, a2, b1, start=False, stop=stop)


class Wide:

    def __init__(self, width, take):
        self.width, self.take = width, take


class Unit:

    def __init__(self, width, by, take, store=None):
        self.width, self.by, self.take, self.store = width, by, take, store


def product_stage(kit, tag, XT, rest, items, units, slots=8, rope=None, place=None, rot_place=None, beside=None,
                  wides=()):
    nc = kit.nc
    n_pairs = 3 if rope else 4
    w_in = [kit.sem(f"{tag}_w_in{s}") for s in range(slots)]
    products, taken_act, taken_dve, act_own, dve_own, scaled, swapped = (
        kit.sem(f"{tag}_{n}") for n in ("products", "taken_act", "taken_dve", "act_own", "dve_own",
                                        "scaled", "swapped"))
    split, rounded, bank_done, wide_taken = (kit.sem(f"{tag}_{n}") for n in ("split", "rounded", "bank_done",
                                                                             "wide_taken"))
    PARTS = 2
    stores = [u for u, unit in enumerate(units) if unit.store]
    stored = [kit.sem(f"{tag}_stored{s}") for s in range(2)] if stores else []
    by_act = [u for u, unit in enumerate(units) if unit.by == "act"]
    by_dve = [u for u, unit in enumerate(units) if unit.by != "act"]
    ropes = [u for u, unit in enumerate(units) if unit.by == "rope"]
    with ExitStack() as mem:
        W = sbuf(nc, mem, f"{tag}_W", [P, slots, 1024]) if place is None else place
        W1 = sbuf(nc, mem, f"{tag}_W1", [P, PARTS, 1024], FP32R)
        W2 = sbuf(nc, mem, f"{tag}_W2", [P, PARTS, 1024], FP32R)
        if rope:
            cos, sin, swap = rope
            rot = sbuf(nc, mem, f"{tag}_rot", [P, 2, S]) if rot_place is None else rot_place
            straight = sbuf(nc, mem, f"{tag}_straight", [P, 2, S])
        with nc.Block() as block:
            def wait_taken(eng, u):
                if units[u].by == "act":
                    eng.wait_ge(taken_act, by_act.index(u) + 1)
                elif units[u].by == "rope":
                    eng.wait_ge(scaled, ropes.index(u) + 1)
                else:
                    eng.wait_ge(taken_dve, [v for v in by_dve if units[v].by == "dve"].index(u) + 1)

            @block.sync
            def _(sp):
                for i, (src, width) in enumerate(items):
                    if i >= slots:
                        sp.wait_ge(split, i - slots + 1)
                    dst = W[:, i % slots, 0:width]
                    if len(src.shape) == 3:
                        dst = dst.rearrange("p (a n) -> p a n", a=src.shape[1])
                    sp.dma_start(dst, src).then_inc(w_in[i % slots], 16)

            @block.tensor
            def _(pe):
                def swap_halves(n):
                    pe.wait_ge(scaled, n + 1)
                    if n >= 1:
                        pe.wait_ge(taken_dve, n)
                    for c in range(2):
                        last = pe.matmul(kit.pair(3)[:, c * HALF:(c + 1) * HALF], swap,
                                         rot[:, n % 2, c * HALF:(c + 1) * HALF], start=True, stop=True)
                    last.then_inc(swapped, 1)

                for u, unit in enumerate(units):
                    pe.wait_ge(split, u + 1)
                    if u >= n_pairs:
                        wait_taken(pe, u - n_pairs)
                    out = kit.pair(u % n_pairs)
                    m = unit.width
                    w1, w2 = (a[:, u % PARTS, 0:KT * m].rearrange("p (k m) -> p k m", k=KT)
                              for a in (W1, W2))
                    for c in range(2):
                        at = slice(c * HALF, (c + 1) * HALF)
                        for k in range(KT):
                            last = three_products(pe, out[0:m, at], w1[:, k, :], w2[:, k, :], XT[:, k, at],
                                                  rest[:, k, at], k == 0, k == KT - 1)
                    last.then_inc(products, 1)
                    if u - 1 in ropes:
                        swap_halves(ropes.index(u - 1))
                if len(units) - 1 in ropes:
                    swap_halves(len(ropes) - 1)
                if wides:
                    for u in range(max(0, len(units) - n_pairs), len(units)):
                        wait_taken(pe, u)
                    if ropes:
                        pe.wait_ge(taken_dve, len(by_dve))
                for n, wide in enumerate(wides):
                    for k in range(KT):
                        i = len(units) + n * KT + k
                        pe.wait_ge(split, i + 1)
                        for t in range(NT):
                            if k == 0 and n:
                                pe.wait_ge(wide_taken, NT * (n - 1) + t + 1)
                            at = slice(t * P, (t + 1) * P)
                            last = three_products(pe, kit.psum[:, t, 0:wide.width], XT[:, k, at], rest[:, k, at],
                                                  W1[:, i % PARTS, 0:wide.width], W2[:, i % PARTS, 0:wide.width],
                                                  k == 0, k == KT - 1)
                            if k == KT - 1 and t < NT - 1:
                                last.then_inc(bank_done, 1)
                        last.then_inc(products, 1)

            @block.scalar
            def _(act):
                own = Own(act, act_own)
                for u in by_act:
                    act.wait_ge(products, u + 1)
                    if u in stores and stores.index(u) >= 2:
                        n = stores.index(u)
                        act.wait_ge(stored[n % 2], 16 * (n // 2))
                    units[u].take(act, kit.pair(u % n_pairs), own).then_inc(taken_act, 1)
                    if u in stores:
                        act.wait_ge(taken_act, by_act.index(u) + 1)
                        act.dma_start(*units[u].store).then_inc(stored[stores.index(u) % 2], 16)
                for n, wide in enumerate(wides):
                    for t in range(NT):
                        if t < NT - 1:
                            act.wait_ge(bank_done, (NT - 1) * n + t + 1)
                        else:
                            act.wait_ge(products, len(units) + KT * (n + 1))
                        wide.take(act, kit.psum[:, t, 0:wide.width], t).then_inc(wide_taken, 1)
                for n, sem in enumerate(stored):
                    act.wait_ge(sem, 16 * len(stores[n::2]))

            @block.gpsimd
            def _(pool):
                for i, (_, width) in enumerate(items):
                    w1, w2 = W1[:, i % PARTS, 0:width], W2[:, i % PARTS, 0:width]
                    pool.wait_ge(w_in[i % slots], 16 * (i // slots + 1))
                    if i >= PARTS:
                        pool.wait_ge(products, i - PARTS + 1)
                    pool.tensor_copy(w1, W[:, i % slots, 0:width]).then_inc(rounded, 1)
                    pool.wait_ge(rounded, i + 1)
                    pool.tensor_tensor(w2, W[:, i % slots, 0:width], w1.bitcast(FP32), ALU.subtract
                                       ).then_inc(split, 1)

            @block.vector
            def _(dve):
                own = Own(dve, dve_own)
                pending = []
                if beside:
                    beside(dve)

                def add_partner(n, dst, split):
                    dve.wait_ge(swapped, n + 1)
                    if split is None:
                        dve.tensor_tensor(dst, dst, kit.pair(3), ALU.add).then_inc(taken_dve, 1)
                        return
                    for i, tile in enumerate(split):
                        half = slice(64 * i, 64 * i + 64)
                        last = dve.tensor_tensor(tile[half, :], dst[half, :], kit.pair(3)[half, :], ALU.add)
                    last.then_inc(taken_dve, 1)

                for u in by_dve:
                    dve.wait_ge(products, u + 1)
                    out = kit.pair(u % n_pairs)
                    if units[u].by == "rope":
                        n = ropes.index(u)
                        dst, scale, split = units[u].take
                        if split is not None:
                            dst = straight[:, n % 2, :]
                            if n >= 2:
                                dve.wait_ge(taken_dve, n - 1)
                        own(dve.scalar_tensor_tensor(dst, out, scale, cos, ALU.mult, ALU.mult))
                        if n >= 2:
                            dve.wait_ge(swapped, n - 1)
                        dve.scalar_tensor_tensor(rot[:, n % 2, :], out, scale, sin, ALU.mult,
                                                 ALU.mult).then_inc(scaled, 1)
                        own.wait()
                        if pending:
                            add_partner(*pending.pop())
                        pending.append((n, dst, split))
                    else:
                        if pending:
                            add_partner(*pending.pop())
                        units[u].take(dve, out, own).then_inc(taken_dve, 1)
                if pending:
                    add_partner(*pending.pop())


def copy_into(dst, rows=P, scale=1.0):
    width = dst.free_size()
    return lambda act, psum, own: act.activation(dst, psum[0:rows, 0:width], ACT.Copy, scale=scale)


def copy_into_dve(dst):
    width = dst.free_size()
    return lambda dve, psum, own: dve.tensor_copy(dst, psum[:, 0:width])


def rglru_stage(kit, BX, BG, XT, spare, d):
    nc = kit.nc
    NB = 4
    params, blocks, zeroed, ready, conv, gates, sig, decay, root, gelu, own_d, own_a, done = (
        kit.sem(f"lru_{n}") for n in ("params", "blocks", "zeroed", "ready", "conv", "gates", "sig", "decay",
                                      "root", "gelu", "own_d", "own_a", "done"))
    with ExitStack() as mem:
        XC, R = XT[:, 0:NB, :], XT[:, NB:2 * NB, :]
        GI = sbuf(nc, mem, "lru_GI", [P, NB, S])
        TH = sbuf(nc, mem, "lru_TH", [P, NB, S])
        A = BX[:, :, 3:3 + S]
        W = spare.rearrange("p (n j m) -> p n j m", n=2, j=NB)
        par = sbuf(nc, mem, "lru_par", [P, 8, NB])
        tmp = sbuf(nc, mem, "lru_tmp", [P, 6, NB])
        with nc.Block() as block:
            @block.sync
            def _(sp):
                with nc.allow_non_contiguous_dma(reason="a few hundred per-channel parameters"):
                    for n, src in enumerate([d["rg_conv_w"][k] for k in range(4)]
                                            + [d["rg_conv_b"], d["rg_b_a"], d["rg_b_x"], d["rg_lambda"]]):
                        sp.dma_start(par[:, n, :], src.rearrange("(j p) -> p j", p=P)).then_inc(params, 16)
                sp.wait_ge(zeroed, 1)
                for n, src in enumerate((d["rg_w_a"], d["rg_w_x"])):
                    for half in range(2):
                        sp.dma_start(W[half * 64:half * 64 + 64, n, :, half * 64:half * 64 + 64],
                                     src.rearrange("(j two) i o -> two i j o", two=2)[half]
                                     ).then_inc(blocks, 16)

            @block.gpsimd
            def _(pool):
                pool.memset(W[:, :, :, :], 0.0).then_inc(zeroed, 1)

            @block.vector
            def _(dve):
                own = Own(dve, own_d)
                dve.wait_ge(params, 16 * 8)
                lam = par[:, 7, :]
                mag, e, w = tmp[:, 0, :], tmp[:, 1, :], tmp[:, 2, :]
                own.then(dve.tensor_scalar(tmp[:, 3, :], lam, -1.0, None, ALU.mult))
                dve.tensor_tensor(mag, tmp[:, 3, :], lam, ALU.min).then_inc(ready, 1)
                for j in range(NB):
                    x = BX[:, j, :]
                    own.then(dve.tensor_scalar(XC[:, j, :], x[:, 3:3 + S], par[:, 3, j:j + 1],
                                               par[:, 4, j:j + 1], ALU.mult, ALU.add))
                    for k in range(3):
                        ins = dve.scalar_tensor_tensor(XC[:, j, :], x[:, k:k + S], par[:, k, j:j + 1],
                                                       XC[:, j, :], ALU.mult, ALU.add)
                        if k < 2:
                            own.then(ins)
                        else:
                            ins.then_inc(conv, 1)
                dve.wait_ge(own_a, 1)
                own.then(dve.tensor_scalar(w, e, 1.0, None, ALU.add))
                own(dve.tensor_scalar(tmp[:, 4, :], w, 1.0, None, ALU.is_equal))
                dve.tensor_scalar(tmp[:, 5, :], w, -1.0, None, ALU.add).then_inc(ready, 1)
                own.wait()
                dve.wait_ge(ready, 2)
                own.then(dve.tensor_tensor(tmp[:, 5, :], tmp[:, 5, :], tmp[:, 4, :], ALU.add))
                own.then(dve.reciprocal(tmp[:, 5, :], tmp[:, 5, :]))
                dve.wait_ge(own_a, 2)
                own.then(dve.tensor_tensor(w, w, tmp[:, 4, :], ALU.add))
                own.then(dve.tensor_tensor(w, w, tmp[:, 5, :], ALU.mult))
                own.then(dve.tensor_tensor(w, w, e, ALU.mult))
                own.then(dve.tensor_scalar(tmp[:, 3, :], tmp[:, 3, :], 0.0, None, ALU.max))
                own.then(dve.tensor_tensor(w, w, tmp[:, 3, :], ALU.add))
                own(dve.tensor_scalar(tmp[:, 3, :], w, LRU_C, None, ALU.mult))
                own(dve.tensor_scalar(tmp[:, 4, :], w, -LRU_C, None, ALU.mult))
                dve.tensor_scalar(tmp[:, 5, :], w, -2 * LRU_C, None, ALU.mult).then_inc(ready, 1)
                for j in range(NB):
                    dve.wait_ge(decay, j + 1)
                    own.then(dve.scalar_tensor_tensor(TH[:, j, :], R[:, j, :], 1.0, TH[:, j, :],
                                                      ALU.add, ALU.mult))
                    dve.tensor_scalar(TH[:, j, :], TH[:, j, :], 0.0, None, ALU.max).then_inc(ready, 1)
                    own.then(dve.tensor_tensor(GI[:, j, :], GI[:, j, :], XC[:, j, :], ALU.mult))
                for j in range(NB):
                    dve.wait_ge(root, j + 1)
                    own.then(dve.tensor_tensor(GI[:, j, :], GI[:, j, :], TH[:, j, :], ALU.mult))
                    own.then(dve.tensor_tensor_scan(XC[:, j, :], A[:, j, :], GI[:, j, :], 0.0,
                                                    ALU.mult, ALU.add))
                    dve.wait_ge(gelu, j + 1)
                    dve.tensor_tensor(BG[:, j, :], BG[:, j, :], XC[:, j, :], ALU.mult).then_inc(done, 1)

            @block.tensor
            def _(pe):
                pe.wait_ge(blocks, 16 * 4)
                for j in range(NB):
                    pe.wait_ge(conv, j + 1)
                    for n in range(2):
                        if j >= 2:
                            pe.wait_ge(sig, 2 * (j - 2) + n + 1)
                        for c in range(2):
                            last = pe.matmul(kit.pair(2 * n + j % 2)[:, c * HALF:(c + 1) * HALF],
                                             W[:, n, j, :], XC[:, j, c * HALF:(c + 1) * HALF],
                                             start=True, stop=True)
                        last.then_inc(gates, 1)

            @block.scalar
            def _(act):
                act.wait_ge(ready, 1)
                act.activation(tmp[:, 1, :], tmp[:, 0, :], ACT.Exp).then_inc(own_a, 1)
                act.wait_ge(ready, 2)
                act.activation(tmp[:, 2, :], tmp[:, 2, :], ACT.Ln).then_inc(own_a, 1)
                for j in range(NB):
                    for n, dst in enumerate((R, GI)):
                        act.wait_ge(gates, 2 * j + n + 1)
                        act.activation(dst[:, j, :], kit.pair(2 * n + j % 2), ACT.Sigmoid,
                                       bias=par[:, 5 + n, j:j + 1]).then_inc(sig, 1)
                act.wait_ge(sig, 2 * NB)
                act.wait_ge(ready, 3)
                for j in range(NB):
                    act.activation(TH[:, j, :], R[:, j, :], ACT.Tanh,
                                   scale=tmp[:, 3, j:j + 1]).then_inc(own_a, 1)
                for j in range(NB):
                    act.activation(A[:, j, :], R[:, j, :], ACT.Exp, scale=tmp[:, 4, j:j + 1]).then_inc(own_a, 1)
                    act.wait_ge(own_a, 2 + NB + j + 1)
                    act.activation(R[:, j, :], R[:, j, :], ACT.Exp, scale=tmp[:, 5, j:j + 1]).then_inc(decay, 1)
                for j in range(NB):
                    act.activation(BG[:, j, :], BG[:, j, :], ACT.Gelu_apprx_tanh).then_inc(gelu, 1)
                for j in range(NB):
                    act.wait_ge(ready, 4 + j)
                    act.activation(TH[:, j, :], TH[:, j, :], ACT.Sqrt).then_inc(root, 1)


def gate_prep_stage(kit, AF, AK, CLR, LF, spare, d):
    nc = kit.nc
    params, low, made, sg, lns, own_d, own_a, gate = (
        kit.sem(f"gp_{n}") for n in ("params", "low", "made", "sg", "lns", "own_d", "own_a", "gate"))
    with ExitStack() as mem:
        par = sbuf(nc, mem, "gp_par", [P, 3])
        lb = sbuf(nc, mem, "gp_lb", [P, 4])
        UP = sbuf(nc, mem, "gp_UP", [16, P])
        F, F2, Y, E = spare[:, 0:2, :], spare[:, 2:4, :], spare[:, 4, :], spare[:, 5, :]
        with nc.Block() as block:
            @block.sync
            def _(sp):
                with nc.allow_non_contiguous_dma(reason="a few hundred per-channel parameters"):
                    sp.dma_start(par[:, 0:2], d["hgrn_lower_bounds"].rearrange("(j p) -> p j", p=P)
                                 ).then_inc(params, 16)
                    sp.dma_start(par[:, 2:3], d["gla_b_gate"].rearrange("(j p) -> p j", p=P)
                                 ).then_inc(params, 16)
                sp.dma_start(UP[:, :], d["gla_w_gate_up"]).then_inc(params, 16)

            @block.tensor
            def _(pe):
                pe.wait_ge(params, 48)
                for c in range(2):
                    last = pe.matmul(kit.pair(0)[:, c * HALF:(c + 1) * HALF], UP[:, :],
                                     CLR[:, c * HALF:(c + 1) * HALF], start=True, stop=True)
                last.then_inc(low, 1)

            @block.scalar
            def _(act):
                act.activation(F, AF[:, :, :], ACT.Sigmoid).then_inc(sg, 1)
                act.activation(AK[:, :, :], AF, ACT.Sigmoid, scale=-1.0).then_inc(sg, 1)
                act.wait_ge(low, 1)
                act.wait_ge(params, 48)
                act.activation(E, kit.pair(0), ACT.Abs, bias=par[:, 2:3]).then_inc(own_a, 1)
                act.wait_ge(own_a, 1)
                act.activation(E, E, ACT.Exp, scale=-1.0).then_inc(own_a, 1)
                act.wait_ge(own_a, 2)
                act.activation(E, E, ACT.Ln, bias=1.0).then_inc(lns, 1)
                act.wait_ge(made, 1)
                act.activation(LF[:, 0:2, :], F2, ACT.Ln).then_inc(lns, 1)
                act.wait_ge(made, 2)
                act.activation(AF[:, :, :], F, ACT.Ln).then_inc(lns, 1)

            @block.vector
            def _(dve):
                own = Own(dve, own_d)
                dve.wait_ge(params, 48)
                own.then(dve.tensor_tensor(lb[:, 0:2], par[:, 0:2], par[:, 0:2], ALU.subtract))
                own.then(dve.tensor_scalar(lb[:, 2:4], lb[:, 0:2], -1.0, 1.0, ALU.mult, ALU.add))
                dve.wait_ge(sg, 2)
                for j in range(2):
                    own(dve.tensor_scalar(F[:, j, :], F[:, j, :], lb[:, 2 + j:3 + j], lb[:, j:j + 1],
                                          ALU.mult, ALU.add))
                    own(dve.tensor_scalar(AK[:, j, :], AK[:, j, :], lb[:, 2 + j:3 + j], None, ALU.mult))
                own.wait()
                own.then(dve.tensor_scalar(F2, F, F_FLOOR, 2.0 ** 60, ALU.max, ALU.mult))
                dve.tensor_scalar(F2, F2, 1.0, None, ALU.min).then_inc(made, 1)
                dve.tensor_scalar(F, F, 2.0 ** -60, None, ALU.max).then_inc(made, 1)
                dve.wait_ge(low, 1)
                dve.wait_ge(own_a, 1)
                own.then(dve.tensor_scalar(Y, kit.pair(0), par[:, 2:3], 0.0, ALU.add, ALU.min))
                dve.wait_ge(lns, 1)
                own.then(dve.tensor_tensor(Y, Y, E, ALU.subtract))
                own(dve.tensor_scalar(LF[:, 2, :], Y, 1.0 / 16.0, None, ALU.mult))
                dve.wait_ge(lns, 3)
                own(dve.tensor_tensor(LF[:, 0:2, :], LF[:, 0:2, :], AF, ALU.add))
                own.wait()


def gla_stage(kit, Q, K, LF, VA, VC, O, XT, X, spare, ident, level, heads, keep):
    nc = kit.nc
    NL = len(LEVELS)
    NP = len(PASS_ROWS)
    cums, refs, weights, mixed, state_w, cleared, kt_done, kt_taken, scored, placed, out_done, out_taken, \
        upd_done, upd_taken, own_d, own_a, own_m = (
            kit.sem(f"gla_{n}") for n in ("cums", "refs", "weights", "mixed", "state_w", "cleared", "kt_done",
                                          "kt_taken", "scored", "placed", "out_done", "out_taken", "upd_done",
                                          "upd_taken", "own_d", "own_a", "own_m"))
    tile_of = [0, 1, 2, 2]
    flat = X.rearrange("p t n -> p (t n)")
    with ExitStack() as mem:
        KW = XT[:, 0:NL, :]
        C = XT[:, NL, :]
        QW = flat[:, 0:NL * S].rearrange("p (n c h m) -> p n c h m", n=NL, c=NT, h=2)
        QK = flat[:, NL * S:]
        Z = spare
        QE = sbuf(nc, mem, "gla_QE", [P, S])
        KL = sbuf(nc, mem, "gla_KL", [P, S])
        EL = sbuf(nc, mem, "gla_EL", [P, NT])
        KLT = sbuf(nc, mem, "gla_KLT", [P, S])
        SC = sbuf(nc, mem, "gla_SC", [P, 2, 2, 2, P])
        ST = sbuf(nc, mem, "gla_ST", [P, 2, P])
        LM = sbuf(nc, mem, "gla_LM", [P, NL * 64], INT32)
        DM = sbuf(nc, mem, "gla_DM", [P, P], INT32)
        with nc.Block() as block:
            @block.gpsimd
            def _(pool):
                for n, p in enumerate((0, 2, 3)):
                    if p:
                        pool.wait_ge(out_done, NT * p)
                    pool.memset(flat[:, 0:NL * S], 0.0).then_inc(cleared, 1)

            @block.vector
            def _(dve):
                own = Own(dve, own_d)
                own(dve.tensor_copy(LM[:, :], level))
                own(dve.tensor_copy(DM[:, :], ident))
                own(dve.memset(SC, 0.0))
                own.wait()
                for p, (first, dk) in enumerate(PASS_ROWS):
                    g = tile_of[p]
                    rows = [slice(first + h * dk, first + (h + 1) * dk) for h in range(2)]
                    new_tile = p == 0 or tile_of[p - 1] != g
                    if p:
                        dve.wait_ge(out_done, NT * p)
                    if new_tile:
                        own.then(dve.tensor_tensor_scan(C, keep, LF[:, g, :], 0.0, ALU.mult, ALU.add))
                        dve.sem_inc(cums, 1)

                    def refer(n):
                        b = LEVELS[n]
                        z = Z[:, n % 2, :].rearrange("p (m w) -> p m w", w=2 * b)
                        c3 = C.rearrange("p (m w) -> p m w", w=2 * b)
                        ref = c3[:, :, b - 1:b].to_broadcast([P, S // (2 * b), 2 * b])
                        if n >= 2 or g >= 1:
                            dve.wait_ge(weights, NL * g + n - 1 if n >= 2 else NL * g)
                        dve.tensor_tensor(z, c3, ref, ALU.subtract).then_inc(refs, 1)

                    if new_tile:
                        refer(0)
                    for n, b in enumerate(LEVELS):
                        if new_tile:
                            if n + 1 < NL:
                                refer(n + 1)
                            dve.wait_ge(weights, NL * g + n + 1)
                        if n == 0:
                            dve.wait_ge(cleared, max(p, 1))
                        w = KW[:, n, :].rearrange("p (c m w) -> p c m w", c=NT, w=2 * b)
                        q4 = Q[:, g, :].rearrange("p (c m w) -> p c m w", c=NT, w=2 * b)
                        for h, r in enumerate(rows):
                            own(dve.tensor_tensor(QW[r, n, :, h, :].rearrange("p c (m w) -> p c m w", w=b),
                                                  w[r, :, :, b:2 * b], q4[r, :, :, b:2 * b], ALU.mult))
                        if new_tile:
                            w3 = KW[:, n, :].rearrange("p (m w) -> p m w", w=2 * b)[:, :, 0:b]
                            k3 = K[:, g, :].rearrange("p (m w) -> p m w", w=2 * b)[:, :, 0:b]
                            own(dve.tensor_tensor(w3, w3, k3, ALU.mult))
                    if new_tile:
                        own(dve.tensor_tensor(QK, Q[:, g, :], K[:, g, :], ALU.mult))
                        z = Z[:, 0, :].rearrange("p (m w) -> p m w", w=P)
                        c3 = C.rearrange("p (m w) -> p m w", w=P)
                        own.then(dve.tensor_tensor(z, c3[:, :, P - 1:P].to_broadcast([P, NT, P]), c3,
                                                   ALU.subtract))
                        dve.sem_inc(state_w, 1)
                        dve.wait_ge(own_a, 3 * (g + 1))
                        own(dve.tensor_tensor(QE, QE, Q[:, g, :], ALU.mult))
                        own(dve.tensor_tensor(KL[:, :], KL[:, :], K[:, g, :], ALU.mult))
                    own(dve.memset(ST, 0.0))
                    own.wait()
                    dve.sem_inc(mixed, 1)
                    for c in range(NT):
                        step = NT * p + c
                        dve.wait_ge(scored, step + 1)
                        if step >= 2:
                            dve.wait_ge(out_done, step - 1)
                        bank = kit.pair(step % 2)
                        moves = [lambda o: dve.copy_predicated(o, DM.unsqueeze(1).to_broadcast([P, 2, P]),
                                                               bank[:, NL * P:NL * P + 2].unsqueeze(2)
                                                               .to_broadcast([P, 2, P])),
                                 lambda o: dve.tensor_copy(o[0:64, :, 64:P],
                                                           bank[0:64, 0:P].rearrange("p (h m) -> p h m", h=2))]
                        moves += [lambda o, n=n, b=b: dve.copy_predicated(
                            o.rearrange("p h (m w) -> p h m w", w=2 * b)[:, :, :, b:2 * b],
                            LM[:, n * 64:(n + 1) * 64].rearrange("p (m w) -> p m w", w=b)
                            .unsqueeze(1).to_broadcast([P, 2, 64 // b, b]),
                            bank[:, n * P:(n + 1) * P].rearrange("p (h m w) -> p h m w", h=2, w=b))
                            for n, b in list(enumerate(LEVELS))[1:]]
                        for n, move in enumerate(moves):
                            if n >= 2:
                                own.wait(own.n - 1)
                            own(move(SC[:, step % 2, n % 2]))
                        own.wait()
                        dve.sem_inc(placed, 1)
                        dve.wait_ge(upd_done, step + 1)
                        if c < NT - 1:
                            if c >= 1:
                                dve.wait_ge(out_done, step)
                            for h, r in enumerate(rows):
                                v = slice(h * 64, (h + 1) * 64)
                                last = dve.scalar_tensor_tensor(
                                    ST[r, (c + 1) % 2, v], ST[r, c % 2, v], EL[r, c:c + 1],
                                    kit.psum[r, 7, v], ALU.mult, ALU.add)
                            last.then_inc(upd_taken, 1)
                            dve.wait_ge(upd_taken, (NT - 1) * p + c + 1)

            @block.scalar
            def _(act):
                own = Own(act, own_a)
                for p in range(NP):
                    g = tile_of[p]
                    if p == 0 or tile_of[p - 1] != g:
                        act.wait_ge(cums, g + 1)
                        for n, b in enumerate(LEVELS):
                            act.wait_ge(refs, NL * g + n + 1)
                            z = Z[:, n % 2, :].rearrange("p (m w) -> p m w", w=2 * b)
                            w = KW[:, n, :].rearrange("p (m w) -> p m w", w=2 * b)
                            act.activation(w[:, :, b:2 * b], z[:, :, b:2 * b], ACT.Exp)
                            act.activation(w[:, :, 0:b], z[:, :, 0:b], ACT.Exp, scale=-1.0).then_inc(weights, 1)
                        act.wait_ge(state_w, g + 1)
                        own(act.activation(QE, C, ACT.Exp))
                        own(act.activation(KL[:, :], Z[:, 0, :], ACT.Exp))
                        own(act.activation(EL[:, :].unsqueeze(2),
                                           C.rearrange("p (m w) -> p m w", w=P)[:, :, P - 1:P], ACT.Exp))
                        for c in range(2):
                            act.wait_ge(kt_done, 2 * g + c + 1)
                            act.activation(KLT[:, c * HALF:(c + 1) * HALF], kit.psum[:, 4 + c, :], ACT.Copy
                                           ).then_inc(kt_taken, 1)
                    for c in range(NT):
                        act.wait_ge(out_done, NT * p + c + 1)
                        act.activation(O[:, c, P * p:P * (p + 1)], kit.psum[:, 6, 0:P], ACT.Copy
                                       ).then_inc(out_taken, 1)

            @block.tensor
            def _(pe):
                def scores(p, c):
                    step = NT * p + c
                    if step >= 2:
                        pe.wait_ge(placed, step - 1)
                    bank = kit.pair(step % 2)
                    at = slice(c * P, (c + 1) * P)
                    for n in range(NL):
                        pe.matmul(bank[:, n * P:(n + 1) * P], KW[:, n, at],
                                  QW[:, n, c, :, :].rearrange("p h m -> p (h m)"), start=True, stop=True)
                    pe.matmul(bank[:, NL * P:NL * P + 2], QK[:, at], heads[:, 2 * p:2 * p + 2],
                              start=True, stop=True).then_inc(scored, 1)

                for p in range(NP):
                    g = tile_of[p]
                    V, v_at = (VA, P * p) if p < 2 else (VC, P * (p - 2))
                    pe.wait_ge(mixed, p + 1)
                    if p == 0 or tile_of[p - 1] != g:
                        for c in range(2):
                            if g:
                                pe.wait_ge(kt_taken, 2 * g + c - 1)
                            for n in range(4):
                                m = 4 * c + n
                                last = pe.transpose(kit.psum[:, 4 + c, n * P:(n + 1) * P],
                                                    KL[:, m * P:(m + 1) * P], ident)
                            last.then_inc(kt_done, 1)
                    scores(p, 0)
                    pe.wait_ge(kt_taken, 2 * g + 2)
                    for c in range(NT):
                        step = NT * p + c
                        if (NT - 1) * p + c:
                            pe.wait_ge(upd_taken, (NT - 1) * p + c)
                        pe.matmul(kit.psum[:, 7, 0:P], KLT[:, c * P:(c + 1) * P], V[:, c, v_at:v_at + P],
                                  start=True, stop=True).then_inc(upd_done, 1)
                        if step:
                            pe.wait_ge(out_taken, step)
                        pe.matmul(kit.psum[:, 6, 0:P], QE[:, c * P:(c + 1) * P], ST[:, c % 2, :],
                                  start=True, stop=False)
                        if c + 1 < NT:
                            scores(p, c + 1)
                        pe.wait_ge(placed, step + 1)
                        for h in range(2):
                            for n in range(2):
                                last = pe.matmul(kit.psum[:, 6, h * 64:(h + 1) * 64], SC[:, step % 2, n, h, :],
                                                 V[:, c, v_at + h * 64:v_at + (h + 1) * 64], start=False,
                                                 stop=h == 1 and n == 1)
                        last.then_inc(out_done, 1)


def head_norm_stage(kit, tag, O, parts, heads, width, gains, eps, copies, ident, scale=None, silu=True, also=()):
    nc = kit.nc
    also_in = kit.sem(f"{tag}_also_in")
    gain_in, sq, root, gated, sums, rows, turned, copied, own_d = (
        kit.sem(f"{tag}_{n}") for n in ("gain_in", "sq", "root", "gated", "sums", "rows", "turned", "copied",
                                        "own_d"))
    W = heads * width
    with ExitStack() as mem:
        G = sbuf(nc, mem, f"{tag}_G", [P, W])
        SQ = sbuf(nc, mem, f"{tag}_SQ", [P, 2, W])
        ss = sbuf(nc, mem, f"{tag}_ss", [P, NT, heads])
        eps_col = sbuf(nc, mem, f"{tag}_eps", [P, 1])
        with nc.Block() as block:
            @block.sync
            def _(sp):
                at = 0
                for g, n in gains:
                    sp.dma_start(G[:, at:at + n], bcast(g)).then_inc(gain_in, 16)
                    at += n
                for dst, src in also:
                    sp.dma_start(dst, src).then_inc(also_in, 16)
                if also:
                    sp.wait_ge(also_in, 16 * len(also))

            @block.scalar
            def _(act):
                for t in range(NT):
                    if t >= 2:
                        act.wait_ge(sums, t - 1)
                    act.activation(SQ[:, t % 2, :], O[:, t, 0:W], ACT.Square).then_inc(sq, 1)
                act.wait_ge(sums, NT)
                act.activation(ss, ss, ACT.Sqrt, scale=1.0 / width, bias=eps_col).then_inc(root, 1)
                if silu:
                    for at, n, gate in parts:
                        act.activation(gate, gate, ACT.Silu).then_inc(gated, 1)
                for t in range(NT):
                    act.wait_ge(turned, t + 1)
                    for n, (_, dst) in enumerate(copies):
                        ins = act.activation(dst[:, t * P:(t + 1) * P],
                                             kit.pair(t % 2)[:, n * P:(n + 1) * P], ACT.Copy)
                    ins.then_inc(copied, 1)

            @block.vector
            def _(dve):
                own = Own(dve, own_d)
                own(dve.memset(eps_col, eps))
                own.wait()
                dve.wait_ge(gain_in, 16 * len(gains))
                if scale is not None:
                    own.then(dve.tensor_scalar(G, G, scale, None, ALU.mult))
                for t in range(NT):
                    dve.wait_ge(sq, t + 1)
                    dve.tensor_reduce(ss[:, t, :], SQ[:, t % 2, :].rearrange("p (h w) -> p h w", h=heads),
                                      AX.X, ALU.add).then_inc(sums, 1)
                dve.wait_ge(root, 1)
                own.then(dve.reciprocal(ss, ss))
                if silu:
                    dve.wait_ge(gated, len(parts))
                for t in range(NT):
                    o = O[:, t, 0:W].rearrange("p (h w) -> p h w", h=heads)
                    own.then(dve.tensor_tensor(o, o, ss[:, t, :].unsqueeze(2).to_broadcast([P, heads, width]),
                                               ALU.mult))
                    own.then(dve.tensor_tensor(O[:, t, 0:W], O[:, t, 0:W], G, ALU.mult))
                    for n, (at, w, gate) in enumerate(parts):
                        ins = dve.tensor_tensor(O[:, t, at:at + w], O[:, t, at:at + w], gate[:, t, :], ALU.mult)
                    ins.then_inc(rows, 1)

            @block.tensor
            def _(pe):
                for t in range(NT):
                    pe.wait_ge(rows, t + 1)
                    if t >= 2:
                        pe.wait_ge(copied, t - 1)
                    for n, (c, _) in enumerate(copies):
                        last = pe.transpose(kit.pair(t % 2)[:, n * P:(n + 1) * P],
                                            O[:, t, c * P:(c + 1) * P], ident)
                    last.then_inc(turned, 1)


def residual_stage(kit, tag, tiles, w_view, X, alpha, chunk):
    nc = kit.nc
    K = len(tiles)
    n_chunks = D // chunk
    w_in = [kit.sem(f"{tag}_w_in{s}") for s in range(2)]
    products, added = kit.sem(f"{tag}_products"), kit.sem(f"{tag}_added")
    with ExitStack() as mem:
        W = sbuf(nc, mem, f"{tag}_W", [P, 2, K, chunk])
        with nc.Block() as block:
            @block.sync
            def _(sp):
                for c in range(n_chunks):
                    if c >= 2:
                        sp.wait_ge(products, NT * (c - 1))
                    sp.dma_start(W[:, c % 2, :, :], w_view[:, :, c * chunk:(c + 1) * chunk]
                                 ).then_inc(w_in[c % 2], 16)

            @block.tensor
            def _(pe):
                for c in range(n_chunks):
                    pe.wait_ge(w_in[c % 2], 16 * (c // 2 + 1))
                    for t in range(NT):
                        n = c * NT + t
                        if n >= 8:
                            pe.wait_ge(added, n - 7)
                        for k in range(K):
                            last = pe.matmul(kit.psum[:, n % 8, 0:chunk], tiles[k][:, t * P:(t + 1) * P],
                                             W[:, c % 2, k, :], start=k == 0, stop=k == K - 1)
                        last.then_inc(products, 1)

            @block.vector
            def _(dve):
                for n in range(n_chunks * NT):
                    c, t = divmod(n, NT)
                    dve.wait_ge(products, n + 1)
                    x = X[:, t, c * chunk:(c + 1) * chunk]
                    dve.scalar_tensor_tensor(x, x, alpha, kit.psum[:, n % 8, 0:chunk], ALU.mult, ALU.add
                                             ).then_inc(added, 1)


def ffn_stage(kit, XT, REST, X, d):
    nc = kit.nc
    GROUP = 7
    GROUPS = FT // GROUP
    RAW, SLOTS = 4, 2
    ITEMS = 4 * GROUP
    w_in = [kit.sem(f"ffn_w_in{s}") for s in range(RAW)]
    begun = kit.sem("ffn_begun")
    params, padded, split, rounded, used, banks, gate_out, conv, gelu, val_out, parts, added, own_d = (
        kit.sem(f"ffn_{n}") for n in ("params", "padded", "split", "rounded", "used", "banks", "gate_out", "conv",
                                      "gelu", "val_out", "parts", "added", "own_d"))
    SPLIT_CREDIT, USED_CREDIT, CONV_CREDIT, PARTS_CREDIT, ADDED_CREDIT = RAW, SLOTS, 2, 2, 1
    BANKS = 2 * (NT - 1)

    def width(i):
        return KT * P if i < 2 * GROUP else HALF

    with ExitStack() as mem:
        W = sbuf(nc, mem, "ffn_W", [P, RAW, KT * P])
        W1 = sbuf(nc, mem, "ffn_W1", [P, SLOTS, KT * P], FP32R)
        W2 = sbuf(nc, mem, "ffn_W2", [P, SLOTS, KT * P], FP32R)
        PR1 = sbuf(nc, mem, "ffn_PR1", [P, GROUP, S], FP32R)
        PR2 = sbuf(nc, mem, "ffn_PR2", [P, GROUP, S], FP32R)
        par = sbuf(nc, mem, "ffn_par", [P, 4, GROUP])
        G = sbuf(nc, mem, "ffn_G", [P, 2, 2 + S])
        Y = sbuf(nc, mem, "ffn_Y", [P, 2, S])
        with nc.Block() as block:
            @block.sync
            def _(sp):
                with sp.Fori(0, GROUPS) as g:
                    sp.wait_ge(conv, GROUP * g + CONV_CREDIT)
                    sp.dma_start(par.rearrange("p n f -> p (n f)"), d["ffn_par"][g]).then_inc(params, 16)
                    for i in range(ITEMS):
                        sp.wait_ge(split, ITEMS * g + (i + 1))
                        if i < 2 * GROUP:
                            src = d["ffn_w_val" if i % 2 else "ffn_w_gate"][GROUP * g + i // 2]
                        else:
                            c, j = divmod(i - 2 * GROUP, GROUP)
                            src = d["ffn_w_down"][GROUP * g + j][:, c * HALF:(c + 1) * HALF]
                        sp.dma_start(W[:, i % RAW, 0:width(i)], src).then_inc(w_in[i % RAW], 16)

            @block.gpsimd
            def _(pool):
                pool.sem_inc(split, SPLIT_CREDIT)
                with pool.Fori(0, GROUPS) as g:
                    for i in range(ITEMS):
                        w, w1, w2 = (a[:, i % n, 0:width(i)] for a, n in ((W, RAW), (W1, SLOTS), (W2, SLOTS)))
                        pool.wait_ge(w_in[i % RAW], 16 * (ITEMS // RAW) * g + 16 * (i // RAW + 1))
                        pool.wait_ge(used, ITEMS * g + (i + 1))
                        pool.sem_inc(begun, 1)
                        pool.tensor_copy(w1, w).then_inc(rounded, 1)
                        pool.wait_ge(rounded, ITEMS * g + (i + 1))
                        pool.tensor_tensor(w2, w, w1.bitcast(FP32), ALU.subtract).then_inc(split, 1)

            @block.tensor
            def _(pe):
                def wait_weights(g, i):
                    pe.wait_ge(split, ITEMS * g + (i + 1 + SPLIT_CREDIT))

                def product(g, i, pair):
                    wait_weights(g, i)
                    w1, w2 = (a[:, i % SLOTS, :].rearrange("p (k m) -> p k m", k=KT) for a in (W1, W2))
                    for c in range(2):
                        for k in range(KT):
                            at = slice(c * HALF, (c + 1) * HALF)
                            last = three_products(pe, kit.pair(pair)[:, at], w1[:, k, :], w2[:, k, :], XT[:, k, at],
                                                  REST[:, k, at], k == 0, k == KT - 1)
                    last.then_inc(used, 1)

                pe.sem_inc(used, USED_CREDIT)
                with pe.Fori(0, GROUPS) as g:
                    for j in range(GROUP):
                        if j < 2:
                            pe.wait_ge(added, 2 * NT * g + ADDED_CREDIT)
                        else:
                            pe.wait_ge(gate_out, GROUP * g + (j - 1))
                        product(g, 2 * j, j % 2)
                        if j >= 2:
                            pe.wait_ge(val_out, GROUP * g + (j - 1))
                        product(g, 2 * j + 1, 2 + j % 2)
                    pe.wait_ge(gate_out, GROUP * g + GROUP)
                    for c in range(2):
                        for j in range(GROUP):
                            i = 2 * GROUP + c * GROUP + j
                            wait_weights(g, i)
                            if c == 0:
                                pe.wait_ge(parts, GROUP * g + (j + 1 + PARTS_CREDIT))
                            for n, t in enumerate((0, 1, 2, 3, 6, 7, 4, 5)):
                                if j == 0 and c == 0 and t in (6, 4):
                                    pe.wait_ge(val_out, GROUP * g + GROUP - (t == 6))
                                if j == 0 and c == 1:
                                    pe.wait_ge(added, 2 * NT * g + (n + 1 + ADDED_CREDIT))
                                at = slice(t * P, (t + 1) * P)
                                last = three_products(pe, kit.psum[:, t, :], PR1[:, j, at], PR2[:, j, at],
                                                      W1[:, i % SLOTS, 0:HALF], W2[:, i % SLOTS, 0:HALF],
                                                      j == 0, j == GROUP - 1)
                                if j == GROUP - 1 and n < NT - 1:
                                    last.then_inc(banks, 1)
                            last.then_inc(used, 1)

            @block.scalar
            def _(act):
                act.wait_ge(padded, 1)

                def bend(g, j):
                    act.wait_ge(conv, GROUP * g + (j + 1 + CONV_CREDIT))
                    act.activation(Y[:, j % 2, :], Y[:, j % 2, :], ACT.Gelu_apprx_tanh).then_inc(gelu, 1)

                with act.Fori(0, GROUPS) as g:
                    for j in range(GROUP):
                        act.wait_ge(used, ITEMS * g + (2 * j + 1 + USED_CREDIT))
                        act.wait_ge(conv, GROUP * g + (j - 1 + CONV_CREDIT + (j == 0)))
                        act.activation(G[:, j % 2, 2:2 + S], kit.pair(j % 2), ACT.Copy).then_inc(gate_out, 1)
                        if j >= 1:
                            bend(g, j - 1)
                    bend(g, GROUP - 1)

            @block.vector
            def _(dve):
                def convolve(g, j, own):
                    x, y = G[:, j % 2, :], Y[:, j % 2, :]
                    dve.wait_ge(gate_out, GROUP * g + (j + 1))
                    dve.wait_ge(parts, GROUP * g + (j - 1 + PARTS_CREDIT + (j == 0)))
                    own.then(dve.tensor_scalar(y, x[:, 2:2 + S], par[:, 2, j:j + 1], par[:, 3, j:j + 1],
                                               ALU.mult, ALU.add))
                    own.then(dve.scalar_tensor_tensor(y, x[:, 0:S], par[:, 0, j:j + 1], y, ALU.mult, ALU.add))
                    dve.scalar_tensor_tensor(y, x[:, 1:1 + S], par[:, 1, j:j + 1], y, ALU.mult, ALU.add
                                             ).then_inc(conv, 1)

                def finish(g, j, own):
                    y = Y[:, j % 2, :]
                    dve.wait_ge(gelu, GROUP * g + (j + 1))
                    dve.wait_ge(used, ITEMS * g + (2 * j + 2 + USED_CREDIT))
                    dve.tensor_tensor(y, y, kit.pair(2 + j % 2), ALU.mult).then_inc(val_out, 1)
                    dve.wait_ge(val_out, GROUP * g + (j + 1))
                    own.then(dve.tensor_copy(PR1[:, j, :], y))
                    dve.tensor_tensor(PR2[:, j, :], y, PR1[:, j, :].bitcast(FP32), ALU.subtract
                                      ).then_inc(parts, 1)

                dve.memset(G[:, :, 0:2], 0.0).then_inc(padded, 1)
                dve.sem_inc(conv, CONV_CREDIT)
                dve.sem_inc(parts, PARTS_CREDIT)
                dve.sem_inc(added, ADDED_CREDIT)
                with dve.Fori(0, GROUPS) as g:
                    own = Own(dve, own_d, 3 * GROUP * g)
                    dve.wait_ge(params, 16 * g + 16)
                    for j in range(GROUP):
                        convolve(g, j, own)
                        if j >= 1:
                            finish(g, j - 1, own)
                    finish(g, GROUP - 1, own)
                    dve.wait_ge(added, 2 * NT * g + ADDED_CREDIT)
                    for c in range(2):
                        for n, t in enumerate((0, 1, 2, 3, 6, 7, 4, 5)):
                            if n < NT - 1:
                                dve.wait_ge(banks, BANKS * g + (c * (NT - 1) + n + 1))
                            else:
                                dve.wait_ge(used, ITEMS * g + ((3 + c) * GROUP + USED_CREDIT))
                            x = X[:, t, c * HALF:(c + 1) * HALF]
                            dve.tensor_tensor(x, x, kit.psum[:, t, :], ALU.add).then_inc(added, 1)


def first_block(kit, ctx, residual, C, d):
    nc = kit.nc
    ident = C("ident")
    parts = ExitStack()
    H1 = sbuf(nc, parts, "M1", [P, KT, S], FP32R, side="right")
    H2 = sbuf(nc, parts, "M2", [P, KT, S], FP32R, side="right")
    with ExitStack() as mem:
        X = sbuf(nc, mem, "X_in", [P, NT, D])
        norm_stage(kit, "mixnorm", X, H1, ident, d["norm_mix"], rest=H2, load=d["x"])
    mix = ExitStack()
    with mix:
        BG = sbuf(nc, mix, "BG", [P, 4, S])
        gla = ExitStack()
        VA = sbuf(nc, gla, "VA", [P, NT, 512])
        VC = sbuf(nc, gla, "VC", [P, NT, 512])
        Q = sbuf(nc, gla, "Q", [P, 3, S])
        K = sbuf(nc, gla, "K", [P, 3, S])
        AF = sbuf(nc, gla, "AF", [P, 2, S])
        CLR = sbuf(nc, gla, "CLR", [16, S])
        lru = ExitStack()
        BX = sbuf(nc, lru, "BX", [P, 4, 3 + S])
        dst = ([Q[:, 0, :], Q[:, 1, :], AF[:, 0, :], AF[:, 1, :]] + [BX[:, j, 3:3 + S] for j in range(4)]
               + [BG[:, j, :] for j in range(4)] + [Q[:, 2, :], K[:, 2, :]])
        items = [(d["w_in_feat"][m], S) for m in range(14)] + [(d["w_in_lr"], KT * 16)]
        items += [(d["w_in_tok"][k * P:(k + 1) * P, c * HALF:(c + 1) * HALF], HALF)
                  for c in range(2) for k in range(KT)]
        units = []
        for m in range(14):
            scale = 32 ** -0.5 if m == 12 else 1.0
            take = copy_into(dst[m], scale=scale) if m % 2 == 0 else copy_into_dve(dst[m])
            units.append(Unit(P, "act" if m % 2 == 0 else "dve", take))
        units.append(Unit(16, "act", copy_into(CLR[:, :], rows=16)))
        wides = [Wide(HALF, lambda act, bank, t, dst=dst: act.activation(dst[:, t, :], bank, ACT.Copy))
                 for dst in (VA, VC)]
        product_stage(kit, "win", H1, H2, items, units, slots=2, wides=wides)
        parts.close()
        X = sbuf(nc, residual, "X", [P, NT, D], side="right")
        mixer = ExitStack()
        XT = sbuf(nc, mixer, "XT_mixer", [P, KT, S], side="right")
        tables = ExitStack()
        FIRST = sbuf(nc, tables, "FIRST", [P, ROPE_AT - FIRST_AT], side="right")
        level, heads, keep = FIRST[:, 0:7 * 64], FIRST[:, 7 * 64:7 * 64 + 8], FIRST[:, 7 * 64 + 8:]
        first_in = kit.sem("first_in")
        pad = kit.sem("pad")
        with nc.Block() as block:
            @block.sync
            def _(sp):
                sp.dma_start(FIRST, d["constants"][:, FIRST_AT:ROPE_AT]).then_inc(first_in, 16)
                sp.wait_ge(first_in, 16)

            @block.gpsimd
            def _(pool):
                pool.memset(BX[:, :, 0:3], 0.0).then_inc(pad, 1)
        rglru_stage(kit, BX, BG, XT, K[:, 0, :], d)
        lru.close()
        OM = sbuf(nc, gla, "OM", [P, NT, 512])
        LF = sbuf(nc, gla, "LF", [P, 3, S])
        gate_prep_stage(kit, AF, K[:, 0:2, :], CLR, LF, XT, d)
        gla_stage(kit, Q, K, LF, VA, VC, OM, XT, X, AF, ident, level, heads, keep)
        OT = XT
        head_norm_stage(kit, "hn", OM, [(0, 256, VA[:, :, 256:512]), (256, 256, VC[:, :, 256:512])], 8, 64,
                        [(d["hgrn_norm"], 256), (d["gla_norm"], 256)], EPS,
                        [(n, OT[:, n, :]) for n in range(4)], ident,
                        also=[(X, d["x"].rearrange("(t p) n -> p t n", p=P))])
        gla.close()
        tiles = [OT[:, 0, :], OT[:, 1, :]] + [BG[:, j, :] for j in range(4)] + [OT[:, 2, :], OT[:, 3, :]]
        residual_stage(kit, "wout", tiles, d["w_out"].rearrange("(k p) n -> p k n", p=P), X, 1.0, 512)
    tables.close()
    mixer.close()
    H1 = sbuf(nc, ctx, "H1", [P, KT, S], FP32R)
    H2 = sbuf(nc, ctx, "H2", [P, KT, S], FP32R)
    norm_stage(kit, "ffnnorm", X, H1, ident, d["norm_ffn"], rest=H2)
    ffn_stage(kit, H1, H2, X, d)
    return X, H1, H2


def keys_at(t):
    return P * t * (t + 1) // 2


KEYS = keys_at(NT)


def index_stage(kit, IQ, IW, IS, AM, causal):
    nc = kit.nc
    scored, bent, added, done, own_d = (kit.sem(f"ix_{n}") for n in ("scored", "bent", "added", "done", "own_d"))
    H = 8
    SLOTS = 4
    with ExitStack() as mem:
        R = sbuf(nc, mem, "ix_R", [P, SLOTS, S])
        with nc.Block() as block:
            @block.tensor
            def _(pe):
                for t in range(NT):
                    n = P * (t + 1)
                    for h in range(H):
                        j = t * H + h
                        if j >= SLOTS:
                            pe.wait_ge(bent, j - SLOTS + 1)
                        for c in range(0, n, HALF):
                            e = min(n, c + HALF)
                            last = pe.matmul(kit.pair(j % SLOTS)[:, c:e], IQ[:, h // 2, t * P:(t + 1) * P],
                                             IQ[:, 4 + h % 2, c:e], start=True, stop=True)
                        last.then_inc(scored, 1)

            @block.scalar
            def _(act):
                for j in range(NT * H):
                    n = P * (j // H + 1)
                    act.wait_ge(scored, j + 1)
                    if j >= SLOTS:
                        act.wait_ge(added, j - SLOTS + 1)
                    act.activation(R[:, j % SLOTS, 0:n], kit.pair(j % SLOTS)[:, 0:n], ACT.Relu).then_inc(bent, 1)

            @block.vector
            def _(dve):
                own = Own(dve, own_d)
                for t in range(NT):
                    n = P * (t + 1)
                    out = IS[:, keys_at(t):keys_at(t) + n]
                    for h in range(H):
                        j = t * H + h
                        dve.wait_ge(bent, j + 1)
                        if h:
                            dve.wait_ge(added, j)
                            ins = dve.scalar_tensor_tensor(out, R[:, j % SLOTS, 0:n], IW[:, t, h:h + 1], out,
                                                           ALU.mult, ALU.add)
                        else:
                            ins = dve.tensor_scalar(out, R[:, j % SLOTS, 0:n], IW[:, t, h:h + 1], None, ALU.mult)
                        ins.then_inc(added, 1)
                    dve.wait_ge(added, (t + 1) * H)
                    own.then(dve.tensor_reduce(AM[:, t:t + 1], out, AX.X, ALU.max, apply_absolute_value=True))
                    dve.tensor_tensor(out[:, t * P:n], out[:, t * P:n], causal, ALU.add).then_inc(done, 1)
                dve.wait_ge(done, NT)


def topk_program(kit, mem, IS, AM, MB, B, R, causal):
    nc = kit.nc
    T0 = TOPK // P
    N = NT - T0
    A = MB[:, keys_at(NT - 1):KEYS]
    own_d = kit.sem("tk_own_d")
    mid, mid_half, cnt, left = (sbuf(nc, mem, f"tk_{n}", [P, N]) for n in ("mid", "mid_half", "cnt", "left"))
    ends = sbuf(nc, mem, "tk_ends", [P, 2, N])
    lo, hi = ends[:, 0, :], ends[:, 1, :]
    ge = sbuf(nc, mem, "tk_ge", [P, 2, N], INT32)
    one = sbuf(nc, mem, "tk_one", [P, 1], BF16)

    def program(dve):
        own = Own(dve, own_d)
        own(dve.memset(one, 1.0))
        own(dve.memset(MB[:, 0:keys_at(T0)], 0.0))
        own.wait()
        for t in range(T0):
            own(dve.tensor_copy(MB[:, keys_at(t) + t * P:keys_at(t) + (t + 1) * P], causal))
        own(dve.tensor_scalar(lo, AM[:, T0:NT], -0.5, None, ALU.mult))
        own(dve.tensor_scalar(hi, AM[:, T0:NT], 0.5 + 2.0 ** -21, 1e-28, ALU.mult, ALU.add))
        own.wait()
        for i in range(BISECTIONS):
            own.then(dve.tensor_tensor(mid, lo, hi, ALU.add))
            for t in range(T0, NT):
                n = P * (t + 1)
                own(dve.tensor_scalar(MB[:, keys_at(t):keys_at(t) + n], IS[:, keys_at(t):keys_at(t) + n],
                                      mid[:, t - T0:t - T0 + 1], 0.0, ALU.is_ge, ALU.add,
                                      accum_out=cnt[:, t - T0:t - T0 + 1]))
            own(dve.tensor_scalar(mid_half, mid, 0.5, None, ALU.mult))
            own.wait()
            own(dve.tensor_scalar(ge[:, 0, :], cnt, float(TOPK), None, ALU.is_ge))
            own(dve.tensor_scalar(ge[:, 1, :], cnt, float(TOPK), None, ALU.is_lt))
            own.wait()
            own.then(dve.copy_predicated(ends, ge, mid_half.unsqueeze(1).to_broadcast([P, 2, N])))
        own.then(dve.tensor_scalar(ends, ends, 2.0, None, ALU.mult))
        for t in range(T0, NT):
            n = P * (t + 1)
            m = t - T0
            s = IS[:, keys_at(t):keys_at(t) + n]
            own(dve.tensor_scalar(A[:, 0:n], s, hi[:, m:m + 1], 0.0, ALU.is_ge, ALU.add,
                                  accum_out=cnt[:, m:m + 1]))
            own.wait()
            own(dve.tensor_scalar(left[:, m:m + 1], cnt[:, m:m + 1], -1.0, float(TOPK), ALU.mult, ALU.add))
            own.then(dve.scalar_tensor_tensor(B[:, 0:n], s, lo[:, m:m + 1], A[:, 0:n], ALU.is_ge, ALU.subtract))
            own.then(dve.tensor_tensor_scan(R[:, 0:n], one.to_broadcast([P, n]), B[:, 0:n], 0.0, ALU.mult, ALU.add))
            own.then(dve.scalar_tensor_tensor(B[:, 0:n], R[:, 0:n], left[:, m:m + 1], B[:, 0:n],
                                              ALU.is_le, ALU.mult))
            own.then(dve.tensor_tensor(A[:, 0:n], A[:, 0:n], B[:, 0:n], ALU.add))
            own.then(dve.tensor_scalar(MB[:, keys_at(t):keys_at(t) + n], A[:, 0:n], 1.0, -NEG,
                                       ALU.subtract, ALU.mult))
    return program


def clear_stage(kit, tag, tiles):
    done = kit.sem(f"{tag}_done")
    with kit.nc.Block() as block:
        @block.gpsimd
        def _(pool):
            for t in tiles:
                pool.memset(t, 0.0).then_inc(done, 1)


def attend_stage(kit, tag, heads, q, k, v, dv, O, out_at, ident, identb, mask, masked_all, decay=None,
                 minus_lam=None, v_at=lambda h: 0):
    nc = kit.nc
    maps = 2 if minus_lam is not None else 1
    jobs = [(t, h) for t in range(NT) for h in range(heads)]
    J = len(jobs)
    RING = 3
    LAG = 2 if maps == 2 else 1
    groups = []
    for j, (t, h) in enumerate(jobs):
        for b in range(0, t + 1, 4):
            groups.append((j, b, min(t + 1, b + 4)))
    scored, greatest, exped, ready, turned, taken_a, taken_v, summed, out, own_d = (
        kit.sem(f"{tag}_{n}") for n in ("scored", "greatest", "exped", "ready", "turned", "taken_a", "taken_v",
                                        "summed", "out", "own_d"))

    def groups_of(j):
        return [g for g, (jj, _, _) in enumerate(groups) if jj == j]

    with ExitStack() as mem:
        PR = sbuf(nc, mem, f"{tag}_PR", [P, RING, maps, S])
        PT = sbuf(nc, mem, f"{tag}_PT", [P, 2, NT, P])
        nmax = sbuf(nc, mem, f"{tag}_nmax", [P, J, maps])
        sums = sbuf(nc, mem, f"{tag}_sums", [P, J, maps])
        inv = sbuf(nc, mem, f"{tag}_inv", [P, J, 2 * maps - 1])
        with nc.Block() as block:
            @block.tensor
            def _(pe):
                def scores(j):
                    t, h = jobs[j]
                    n = P * (t + 1)
                    for m in range(maps):
                        i = j * maps + m
                        if i >= 2:
                            pe.wait_ge(exped, i - 1)
                        for c in range(0, n, HALF):
                            e = min(n, c + HALF)
                            dst = kit.pair(i % 2)
                            more = masked_all or e == n
                            pe.matmul(dst[:, c:e], q(h, m, t), k(h, m, c, e), start=True,
                                      stop=not (more or decay))
                            if decay:
                                lhs, rhs = decay(h, c, e)
                                last = pe.matmul(dst[:, c:e], lhs, rhs, start=False, stop=not more)
                            if more:
                                a = c if masked_all else t * P
                                last = pe.matmul(dst[:, a:e], identb, mask(t, a, e), start=False, stop=True)
                        last.then_inc(scored, 1)

                def turn(j):
                    if maps == 2:
                        pe.wait_ge(ready, j + 1)
                    else:
                        pe.wait_ge(exped, j + 1)
                    for g in groups_of(j):
                        _, b0, b1 = groups[g]
                        if g >= 2:
                            pe.wait_ge(taken_v if g % 2 else taken_a, g // 2)
                        for b in range(b0, b1):
                            last = pe.transpose(kit.psum[:, 4 + g % 2, (b - b0) * P:(b - b0 + 1) * P],
                                                PR[:, j % RING, 0, b * P:(b + 1) * P], ident)
                        last.then_inc(turned, 1)

                def weigh(j):
                    t, h = jobs[j]
                    g = groups_of(j)[-1]
                    pe.wait_ge(taken_a, g // 2 + 1)
                    if g:
                        pe.wait_ge(taken_v, (g + 1) // 2)
                    if j >= 2:
                        pe.wait_ge(out, j - 1)
                    for b in range(t + 1):
                        last = pe.matmul(kit.psum[:, 6 + j % 2, 0:P], PT[:, j % 2, b, :], v(h, b),
                                         start=b == 0, stop=b == t)
                    last.then_inc(summed, 1)

                for j in range(J + LAG + 1):
                    if j < J:
                        scores(j)
                    if 0 <= j - LAG < J:
                        turn(j - LAG)
                    if 0 <= j - LAG - 1 < J:
                        weigh(j - LAG - 1)

            def take_group(eng, g, sem, copy):
                j, b0, b1 = groups[g]
                eng.wait_ge(turned, g + 1)
                if j >= 2:
                    eng.wait_ge(summed, j - 1)
                copy(PT[:, j % 2, b0:b1, :].rearrange("p b n -> p (b n)"),
                     kit.psum[:, 4 + g % 2, 0:(b1 - b0) * P]).then_inc(sem, 1)

            @block.scalar
            def _(act):
                for j in range(J + LAG):
                    if j < J:
                        n = P * (jobs[j][0] + 1)
                        if j >= RING:
                            act.wait_ge(turned, groups_of(j - RING)[-1] + 1)
                        for m in range(maps):
                            i = j * maps + m
                            act.wait_ge(greatest, i + 1)
                            act.activation(PR[:, j % RING, m, 0:n], kit.pair(i % 2)[:, 0:n], ACT.Exp,
                                           bias=nmax[:, j, m:m + 1], accum_out=sums[:, j, m:m + 1]
                                           ).then_inc(exped, 1)
                    if j >= LAG:
                        for g in groups_of(j - LAG):
                            if g % 2 == 0:
                                take_group(act, g, taken_a, lambda o, i: act.activation(o, i, ACT.Copy))

            @block.vector
            def _(dve):
                own = Own(dve, own_d)

                def maxima(j):
                    n = P * (jobs[j][0] + 1)
                    for m in range(maps):
                        i = j * maps + m
                        dve.wait_ge(scored, i + 1)
                        dve.tensor_reduce(nmax[:, j, m:m + 1], kit.pair(i % 2)[:, 0:n], AX.X, ALU.max,
                                          negate=True).then_inc(greatest, 1)

                def norms(j):
                    dve.wait_ge(exped, (j + 1) * maps)
                    own(dve.reciprocal(inv[:, j, 0:maps], sums[:, j, :]))
                    if maps == 2:
                        n = P * (jobs[j][0] + 1)
                        own.wait()
                        own.then(dve.scalar_tensor_tensor(inv[:, j, 2:3], sums[:, j, 0:1], inv[:, j, 1:2],
                                                          minus_lam, ALU.mult, ALU.mult))
                        dve.scalar_tensor_tensor(PR[:, j % RING, 0, 0:n], PR[:, j % RING, 1, 0:n],
                                                 inv[:, j, 2:3], PR[:, j % RING, 0, 0:n],
                                                 ALU.mult, ALU.add).then_inc(ready, 1)

                def result(j):
                    t, h = jobs[j]
                    at = out_at + h * dv
                    dve.wait_ge(summed, j + 1)
                    a = v_at(h)
                    dve.tensor_scalar(O[:, t, at:at + dv], kit.psum[:, 6 + j % 2, a:a + dv], inv[:, j, 0:1], None,
                                      ALU.mult).then_inc(out, 1)

                for j in range(J + LAG + 1):
                    if j < J:
                        maxima(j)
                    if 0 <= j - 1 < J:
                        norms(j - 1)
                    if 0 <= j - LAG < J:
                        for g in groups_of(j - LAG):
                            if g % 2:
                                take_group(dve, g, taken_v, lambda o, i: dve.tensor_copy(o, i))
                    if 0 <= j - LAG - 1 < J:
                        own.wait()
                        result(j - LAG - 1)


def prepare_stage(kit, l, LAM, IW, VS, FF, FB, pick, pickb, identb, causalb, ident, causal, d):
    nc = kit.nc
    params, ff, exps, own_d, own_a = (kit.sem(f"pr_{n}") for n in ("params", "ff", "exps", "own_d", "own_a"))
    with ExitStack() as mem:
        LV = sbuf(nc, mem, "pr_LV", [P, 4, 64])
        dots = sbuf(nc, mem, "pr_dots", [P, 2])
        init = sbuf(nc, mem, "pr_init", [P, 2])
        bf = sbuf(nc, mem, "pr_bf", [4, 1])
        E = sbuf(nc, mem, "pr_E", [4, S])
        ones = sbuf(nc, mem, "pr_ones", [4, 1])
        part = sbuf(nc, mem, "pr_part", [4, S], BF16)
        with nc.Block() as block:
            @block.sync
            def _(sp):
                for n, name in enumerate(("lam_q1_2", "lam_q2_2", "lam_k1_2", "lam_k2_2")):
                    sp.dma_start(LV[:, n, :], bcast(d[name][l])).then_inc(params, 16)
                sp.dma_start(init, bcast(d["lam_init"][l])).then_inc(params, 16)
                with nc.allow_non_contiguous_dma(reason="four gate biases"):
                    sp.dma_start(bf, d["b_f_2"][l].rearrange("(p o) -> p o", o=1)).then_inc(params, 16)

            @block.scalar
            def _(act):
                act.wait_ge(params, 96)
                act.activation(E, FF, ACT.Abs, bias=bf).then_inc(own_a, 1)
                act.wait_ge(own_a, 1)
                act.activation(E, E, ACT.Exp, scale=-1.0).then_inc(own_a, 1)
                act.wait_ge(own_a, 2)
                act.activation(E, E, ACT.Ln, bias=1.0).then_inc(exps, 1)
                act.wait_ge(ff, 1)
                act.activation(dots, dots, ACT.Exp).then_inc(exps, 1)

            @block.vector
            def _(dve):
                own = Own(dve, own_d)
                own(dve.memset(ones, 1.0))
                own(dve.memset(FB, 0.0))
                own(dve.tensor_copy(pickb, pick))
                own(dve.tensor_copy(identb, ident))
                own(dve.tensor_copy(causalb, causal))
                own(dve.tensor_scalar(IW, VS[:, :, 64:72], IDX_SCALE, None, ALU.mult))
                dve.wait_ge(params, 96)
                own.then(dve.tensor_tensor(LV[:, 0:2, :], LV[:, 0:2, :], LV[:, 2:4, :], ALU.mult))
                dve.tensor_reduce(dots, LV[:, 0:2, :], AX.X, ALU.add).then_inc(ff, 1)
                dve.wait_ge(exps, 1)
                own.then(dve.tensor_scalar(FF, FF, bf, 0.0, ALU.add, ALU.min))
                own.then(dve.tensor_tensor(FF, FF, E, ALU.subtract))
                own(dve.tensor_tensor_scan(FF, ones.to_broadcast([4, S]), FF, 0.0, ALU.mult, ALU.subtract))
                own.wait()
                for n in range(3):
                    own.then(dve.tensor_copy(part, FF))
                    own(dve.tensor_copy(FB[32 * n:32 * n + 4, :], part))
                    if n < 2:
                        own.then(dve.tensor_tensor(FF, FF, part, ALU.subtract))
                dve.wait_ge(exps, 2)
                own.then(dve.tensor_tensor(LAM[:, 0:1], dots[:, 1:2], dots[:, 0:1], ALU.subtract))
                own(dve.tensor_tensor(LAM[:, 0:1], LAM[:, 0:1], init[:, 0:1], ALU.subtract))
                own(dve.tensor_copy(LAM[:, 1:2], init[:, 1:2]))
                own.wait()


def finish_stage(kit, tag, OD, OS, GATE, w_out, XD, XT, REST, g_subln, keep_scale, ln_g, ln_b, ident):
    nc = kit.nc
    H = 4
    XS = 3
    gate_in = [kit.sem(f"{tag}_gate_in{s}") for s in range(2)]
    w_in = [kit.sem(f"{tag}_w_in{s}") for s in range(2)]
    x_in = [kit.sem(f"{tag}_x_in{s}") for s in range(XS)]
    stored = [kit.sem(f"{tag}_stored{s}") for s in range(XS)]
    parted = kit.sem(f"{tag}_parted")
    (gains, sq, summed, root, inverse, scaled, turned, mixed, products, stats, ln_root, rows, ln_turned,
     copied, own_d) = (kit.sem(f"{tag}_{n}") for n in (
         "gains", "sq", "summed", "root", "inverse", "scaled", "turned", "mixed", "products", "stats",
         "ln_root", "rows", "ln_turned", "copied", "own_d"))
    with ExitStack() as mem:
        W = sbuf(nc, mem, f"{tag}_W", [P, KT, D])
        X = sbuf(nc, mem, f"{tag}_X", [P, XS, D])
        XM = sbuf(nc, mem, f"{tag}_XM", [P, 2, KT, P])
        GT = sbuf(nc, mem, f"{tag}_GT", [P, 2, KT, P])
        SQ = sbuf(nc, mem, f"{tag}_SQ", [P, 2, H * P])
        ss = sbuf(nc, mem, f"{tag}_ss", [P, NT, H])
        G = sbuf(nc, mem, f"{tag}_G", [P, D])
        B = sbuf(nc, mem, f"{tag}_B", [P, D])
        gain = sbuf(nc, mem, f"{tag}_gain", [P, 1])
        eps = sbuf(nc, mem, f"{tag}_eps", [P, 2])
        bn = sbuf(nc, mem, f"{tag}_bn", [P, 2, 6])
        mv = sbuf(nc, mem, f"{tag}_mv", [P, NT, 2])
        dev = sbuf(nc, mem, f"{tag}_dev", [P, NT])
        inv = sbuf(nc, mem, f"{tag}_inv", [P, NT])
        with nc.Block() as block:
            @block.sync
            def _(sp):
                def gates(t):
                    sp.dma_start(GT[:, t % 2], GATE[:, :, t * P:(t + 1) * P]).then_inc(gate_in[t % 2], 16)

                def store(t):
                    sp.wait_ge(rows, t + 1)
                    sp.dma_start(XD[t * P:(t + 1) * P, :], X[:, t % XS, :]).then_inc(stored[t % XS], 16)

                with nc.allow_non_contiguous_dma(reason="one gain per partition"):
                    sp.dma_start(gain, g_subln.rearrange("(p o) -> p o", o=1)).then_inc(gains, 16)
                gates(0)
                for c in range(2):
                    sp.dma_start(W[:, :, c * HALF:(c + 1) * HALF], w_out[:, :, c * HALF:(c + 1) * HALF]
                                 ).then_inc(w_in[c], 16)
                sp.dma_start(G, bcast(ln_g)).then_inc(gains, 16)
                sp.dma_start(B, bcast(ln_b)).then_inc(gains, 16)
                gates(1)
                for t in range(XS):
                    sp.dma_start(X[:, t, :], XD[t * P:(t + 1) * P, :]).then_inc(x_in[t], 16)
                for t in range(NT):
                    if t >= 2:
                        sp.wait_ge(mixed, t - 1)
                        gates(t)
                    if t >= 2:
                        store(t - 2)
                    if t >= 2 and t + 1 < NT:
                        sp.wait_ge(stored[(t - 2) % XS], 16 * ((t - 2) // XS + 1))
                        sp.wait_ge(ln_turned, t - 1)
                        sp.dma_start(X[:, (t + 1) % XS, :], XD[(t + 1) * P:(t + 2) * P, :]
                                     ).then_inc(x_in[(t + 1) % XS], 16)
                store(NT - 2)
                store(NT - 1)
                for n, sem in enumerate(stored):
                    sp.wait_ge(sem, 16 * len(range(n, NT, XS)))

            @block.scalar
            def _(act):
                for t in range(NT):
                    if t >= 2:
                        act.wait_ge(summed, t - 1)
                    act.activation(SQ[:, t % 2, :], OD[:, t, :], ACT.Square).then_inc(sq, 1)
                act.wait_ge(summed, NT + 1)
                act.activation(ss, ss, ACT.Sqrt, scale=1.0 / P, bias=eps[:, 0:1]).then_inc(root, 1)
                act.wait_ge(inverse, 1)
                for t in range(NT):
                    for h in range(H):
                        o = OD[:, t, h * P:(h + 1) * P]
                        ins = act.activation(o, o, ACT.Copy, scale=ss[:, t, h:h + 1])
                    ins.then_inc(scaled, 1)
                for t in range(NT):
                    act.wait_ge(stats, t + 1)
                    act.activation(dev[:, t:t + 1], mv[:, t, 1:2], ACT.Sqrt, bias=eps[:, 1:2]).then_inc(ln_root, 1)
                    act.wait_ge(ln_turned, t + 1)
                    act.activation(XT[:, :, t * P:(t + 1) * P],
                                   kit.pair(1).rearrange("p (k n) -> p k n", k=KT), ACT.Copy).then_inc(copied, 1)

            @block.vector
            def _(dve):
                own = Own(dve, own_d)
                own(dve.memset(eps[:, 0:1], SUBLN_EPS))
                own.then(dve.memset(eps[:, 1:2], LN_EPS))
                for t in range(NT):
                    dve.wait_ge(sq, t + 1)
                    dve.tensor_reduce(ss[:, t, :], SQ[:, t % 2, :].rearrange("p (h w) -> p h w", h=H),
                                      AX.X, ALU.add).then_inc(summed, 1)
                dve.sem_inc(summed, 1)
                dve.wait_ge(gains, 48)
                own.then(dve.tensor_scalar(gain, gain, keep_scale, None, ALU.mult))
                dve.wait_ge(root, 1)
                dve.reciprocal(ss, ss).then_inc(inverse, 1)

                def gate(t):
                    dve.wait_ge(gate_in[t % 2], 16 * (t // 2 + 1))
                    dve.wait_ge(turned, t + 1)
                    psum = kit.pair(0).rearrange("p (k n) -> p k n", k=KT)
                    if t >= 2:
                        dve.wait_ge(products, t - 1)
                    dve.scalar_tensor_tensor(XM[:, t % 2, 0:H, :], psum[:, 0:H, :], gain, GT[:, t % 2, 0:H, :],
                                             ALU.mult, ALU.mult)
                    dve.tensor_tensor(XM[:, t % 2, H:, :], psum[:, H:, :], GT[:, t % 2, H:, :], ALU.mult
                                      ).then_inc(mixed, 1)

                gate(0)
                def part(t):
                    at = slice(t * P, (t + 1) * P)
                    dve.wait_ge(copied, t + 1)
                    dve.tensor_tensor(REST[:, :, at], kit.pair(1).rearrange("p (k n) -> p k n", k=KT),
                                      XT[:, :, at].bitcast(FP32), ALU.subtract).then_inc(parted, 1)

                for t in range(NT):
                    if t + 1 < NT:
                        gate(t + 1)
                    if t >= 2:
                        part(t - 2)
                    x = X[:, t % XS, :]
                    dve.wait_ge(x_in[t % XS], 16 * (t // XS + 1))
                    dve.wait_ge(products, t + 1)
                    own.then(dve.scalar_tensor_tensor(x, x, ALPHA, kit.pair(2 + t % 2), ALU.mult, ALU.add))
                    for n in range(2):
                        own(dve.bn_stats(bn[:, n, :], x[:, n * HALF:(n + 1) * HALF]))
                    own.wait()
                    dve.bn_aggr(mv[:, t, :], bn).then_inc(stats, 1)
                    dve.wait_ge(ln_root, t + 1)
                    own.then(dve.reciprocal(inv[:, t:t + 1], dev[:, t:t + 1]))
                    own.then(dve.tensor_scalar(x, x, mv[:, t, 0:1], inv[:, t:t + 1], ALU.subtract, ALU.mult))
                    own.then(dve.tensor_tensor(x, x, G, ALU.mult))
                    dve.tensor_tensor(x, x, B, ALU.add).then_inc(rows, 1)
                part(NT - 2)
                part(NT - 1)

            @block.tensor
            def _(pe):
                def turn(t):
                    pe.wait_ge(scaled, t + 1)
                    if t:
                        pe.wait_ge(mixed, t)
                    for k in range(KT):
                        O = OD if k < H else OS
                        last = pe.transpose(kit.pair(0)[:, k * P:(k + 1) * P],
                                            O[:, t, k % H * P:(k % H + 1) * P], ident)
                    last.then_inc(turned, 1)

                def turn_norm(t):
                    pe.wait_ge(rows, t + 1)
                    if t:
                        pe.wait_ge(parted, t)
                    for k in range(KT):
                        last = pe.transpose(kit.pair(1)[:, k * P:(k + 1) * P], X[:, t % XS, k * P:(k + 1) * P], ident)
                    last.then_inc(ln_turned, 1)

                turn(0)
                for t in range(NT):
                    if t + 1 < NT:
                        turn(t + 1)
                    else:
                        pe.wait_ge(mixed, NT)
                    if t >= 2:
                        pe.wait_ge(rows, t - 1)
                    for c in range(2):
                        if t == 0:
                            pe.wait_ge(w_in[c], 16)
                        for k in range(KT):
                            last = pe.matmul(kit.pair(2 + t % 2)[:, c * HALF:(c + 1) * HALF],
                                             XM[:, t % 2, k, :], W[:, k, c * HALF:(c + 1) * HALF],
                                             start=k == 0, stop=k == KT - 1)
                    last.then_inc(products, 1)
                    if t:
                        turn_norm(t - 1)
                turn_norm(NT - 1)


def rows_of(w, c, e):
    return [(w[k * P:(k + 1) * P, c:e], e - c) for k in range(KT)]


def layer(kit, l, XD, XT, REST, C, cos, sin, LAM, OM, GATE, d):
    nc = kit.nc
    ident, causal, swap = C("ident"), C("causal"), C("swap")
    pick = C("pick").rearrange("p (h n) -> p h n", h=4)
    w_feat, w_tok = d["w2_feat"][l], d["w2_tok"][l]
    attn, ends = ExitStack(), ExitStack()
    flat = OM.rearrange("p h n -> p (h n)")
    OD, OS = (OM[:, n, :].rearrange("p (t n) -> p t n", t=NT) for n in range(2))
    with attn:
        identb = sbuf(nc, attn, "identb", [P, P], BF16)
        causalb = sbuf(nc, attn, "causalb", [P, P], BF16)
        early = ExitStack()
        SQ = sbuf(nc, early, "SQ", [P, 4, S])
        VS = sbuf(nc, early, "VS", [P, NT, 328])
        FB = sbuf(nc, early, "FB", [P, S], BF16)
        pickb = sbuf(nc, early, "pickb", [P, 4, P], BF16)
        AM = sbuf(nc, early, "AM", [P, NT])
        MB = sbuf(nc, early, "MB", [P, KEYS], BF16)
        index = ExitStack()
        IW = sbuf(nc, index, "IW", [P, NT, 8])
        FF = sbuf(nc, index, "FF", [4, S])
        IQ = sbuf(nc, index, "IQ", [P, 6, S])
        items = [(w_feat[m], S) for m in range(8)] + [(d["w2_ff"][l], KT * 4)]
        items += rows_of(w_tok, 0, 328)
        dst = [SQ[:, 0, :], SQ[:, 1, :], None] + [IQ[:, j, :] for j in range(4)] + [None]
        split = {2: (SQ[:, 2, :], SQ[:, 3, :]), 7: (IQ[:, 4, :], IQ[:, 5, :])}
        units = []

        def take_keys(pair):
            def take(act, psum, own):
                act.activation(FQ[0:64, 2 + 2 * pair, :], psum[0:64, :], ACT.Copy)
                return act.activation(FQ[64:P, 3 + 2 * pair, :], psum[64:P, :], ACT.Copy)
            return take

        for m in range(8):
            units.append(Unit(P, "rope", (dst[m], QK_SCALE if m < 2 else 1.0, split.get(m))))
        units.append(Unit(4, "act", copy_into(FF, rows=4)))
        wides = [Wide(328, lambda act, bank, t: act.activation(VS[:, t, :], bank, ACT.Copy))]
        clear_stage(kit, "za", [t[64 * (1 - i % 2):64 * (2 - i % 2), :] for i, t in enumerate(
            [SQ[:, 2, :], SQ[:, 3, :], IQ[:, 4, :], IQ[:, 5, :]])])
        product_stage(kit, "pa", XT, REST, items, units, rope=(cos, sin, swap), wides=wides,
                      place=flat.rearrange("p (s n) -> p s n", n=S),
                      rot_place=MB[:, 0:4 * S].bitcast(FP32).rearrange("p (a n) -> p a n", a=2))
        prepare_stage(kit, l, LAM, IW, VS, FF, FB, pick, pickb, identb, causalb, ident, causal, d)
        IS = flat[:, 0:KEYS]
        index_stage(kit, IQ, IW, IS, AM, causal)
        index.close()
        FQ = sbuf(nc, early, "FQ", [P, 6, S])
        clear_stage(kit, "zf", [FQ[64 * (1 - j % 2):64 * (2 - j % 2), 2 + j, :] for j in range(4)])
        late = ExitStack()
        DV = ends.enter_context(nc.sbuf_tensor("DV", [P, NT, 512], FP32, side="right"))[:, :, :]
        with ExitStack() as mem:
            room = flat[:, KEYS:]
            staged = [room[:, n * S:(n + 1) * S] for n in range(2)]
            topk = topk_program(kit, mem, IS, AM, MB, room[:, 3 * S:3 * S + S // 2].bitcast(BF16),
                                room[:, 2 * S:3 * S], causal)
            items = [(w_feat[8 + m], S) for m in range(12)] + rows_of(w_tok, 328, 840)
            units = [Unit(P, "act", copy_into(FQ[:, m, :], scale=QK_SCALE)) for m in range(2)]
            units += [Unit(P, "act", take_keys(m)) for m in range(2)]
            units += [Unit(P, "act",
                           lambda act, psum, own, m=m: act.activation(staged[m % 2], psum, ACT.Silu),
                           store=(GATE[:, m, :], staged[m % 2])) for m in range(KT)]
            wides = [Wide(HALF, lambda act, bank, t: act.activation(DV[:, t, :], bank, ACT.Copy))]
            product_stage(kit, "tk", XT, REST, items, units, slots=1, beside=topk, wides=wides)

        attend_stage(kit, "sp", 4, lambda h, m, t: SQ[:, h // 2, t * P:(t + 1) * P],
                     lambda h, m, c, e: SQ[:, 2 + h % 2, c:e], lambda h, b: VS[:, b, 0:P], 64, OS, 0,
                     ident, identb, lambda t, c, e: MB[:, keys_at(t) + c:keys_at(t) + e], True)
        attend_stage(kit, "fg", 4, lambda h, m, t: FQ[:, h // 2, t * P:(t + 1) * P],
                     lambda h, m, c, e: FQ[:, 2 + h, c:e],
                     lambda h, b: VS[:, b, 72 + P * (h // 2):200 + P * (h // 2)], 64, OS, 256, ident, identb,
                     lambda t, c, e: causalb, False,
                     v_at=lambda h: 64 * (h % 2),
                     decay=lambda h, c, e: (pickb[:, h, :], FB[:, c:e]))
        early.close()
        DQ = sbuf(nc, late, "DQ", [P, 12, S])
        items = [(w_feat[20 + m], S) for m in range(8)]
        units = [Unit(P, "rope", (DQ[:, m, :], QK_SCALE, None)) for m in range(4)]
        units += [Unit(P, "rope", (None, 1.0, (DQ[:, 2 * m - 4, :], DQ[:, 2 * m - 3, :])))
                  for m in range(4, 8)]
        clear_stage(kit, "zd", [DQ[64 * (1 - m % 2):64 * (2 - m % 2), 4 + m, :] for m in range(8)])
        lent = flat[:, 0:4 * S].rearrange("p (s n) -> p s n", n=S)
        product_stage(kit, "pd", XT, REST, items, units, slots=2, rope=(cos, sin, swap),
                      place=lent[:, 0:2, :], rot_place=lent[:, 2:4, :])
        attend_stage(kit, "df", 4, lambda h, m, t: DQ[:, h, t * P:(t + 1) * P],
                     lambda h, m, c, e: DQ[:, 4 + 2 * h + m, c:e],
                     lambda h, b: DV[:, b, 128 * h:128 * h + 128], 128, OD, 0, ident, identb,
                     lambda t, c, e: causalb, False, minus_lam=LAM[:, 0:1])
        late.close()
    ends.close()
    finish_stage(kit, "fin", OD, OS, GATE, d["w_out_2"][l].rearrange("(k p) n -> p k n", p=P), XD, XT, REST,
                 d["g_subln_2"][l], LAM[:, 1:2], d["ln_g_2"][l], d["ln_b_2"][l], ident)


def second_block(kit, X, residual, XD, XT, REST, C, d):
    nc = kit.nc
    with ExitStack() as mem:
        ROPE = sbuf(nc, mem, "ROPE", [P, 2 * S])
        LAM = sbuf(nc, mem, "LAM", [P, 2])
        OM = sbuf(nc, mem, "OM2", [P, 2, NT * HALF])
        GATE = nc.dram_tensor("GATE", (P, KT, S), FP32).ap()
        norm_stage(kit, "finalnorm", X, XT, C("ident"), d["norm_final"], keep=True, rest=REST, store=XD,
                   also=[(ROPE, d["constants"][:, ROPE_AT:ROPE_AT + 2 * S])])
        residual.close()
        kit.clear_semaphores()
        with nc.Fori(0, DEPTH_2) as l:
            layer(kit, l, XD, XT, REST, C, ROPE[:, 0:S], ROPE[:, S:2 * S], LAM, OM, GATE, d)
            kit.clear_semaphores()


def build(nc, d, out):
    ctx = ExitStack()
    with ctx:
        kit = Kit(nc, ctx)
        CONST = sbuf(nc, ctx, "CONST", [P, FIRST_AT])

        def C(name):
            at, width = CONST_AT[name]
            return CONST[:, at:at + width]

        loaded = kit.sem("loaded")
        with nc.Block() as block:
            @block.sync
            def _(sp):
                sp.dma_start(CONST[:, :], d["constants"][:, 0:FIRST_AT]).then_inc(loaded, 16)
                sp.wait_ge(loaded, 16)
        residual = ExitStack()
        X, H1, H2 = first_block(kit, ctx, residual, C, d)
        second_block(kit, X, residual, out, H1, H2, C, d)


def _feature_tiles(w):
    k, n = w.shape
    return np.ascontiguousarray(w.reshape(k // P, P, n // P, P).transpose(2, 1, 0, 3)).reshape(n // P, P, k)


def _narrow_tile(w):
    k, m = w.shape
    return np.ascontiguousarray(w.reshape(k // P, P, m).transpose(1, 0, 2)).reshape(P, -1)


def layout(inputs):
    a = {n: np.asarray(v) for n, v in inputs.items()}
    d = {"x": a["x"][0], "constants": constants()}
    for n in ("norm_mix", "hgrn_lower_bounds", "hgrn_norm", "rg_conv_w", "rg_conv_b", "rg_w_a", "rg_b_a",
              "rg_w_x", "rg_b_x", "rg_lambda", "gla_w_gate_up", "gla_b_gate", "gla_norm", "w_out", "norm_ffn"):
        d[n] = a[n][0]
    d["norm_final"] = a["norm_final"]
    at = np.cumsum([0, 256, 256, 256, 256, 512, 512, 128, 128, 256, 256, 16])
    aq, af, ai, ag, bx, bg, cq, ck, cv, cg, lr = [a["w_in"][0][:, at[n]:at[n + 1]] for n in range(11)]
    d["w_in_feat"] = _feature_tiles(np.concatenate([aq, af, bx, bg, cq, ck], 1))
    d["w_in_lr"] = _narrow_tile(lr)
    d["w_in_tok"] = np.concatenate([ai, ag, cv, cg], 1)
    d["ffn_w_gate"] = _feature_tiles(a["ffn_w_gate"][0])
    d["ffn_w_val"] = _feature_tiles(a["ffn_w_val"][0])
    d["ffn_w_down"] = a["ffn_w_down"][0].reshape(FT, P, D)
    d["ffn_par"] = np.concatenate([a["ffn_conv_w"][0], a["ffn_conv_b"]], 0).reshape(
        4, FT // 7, 7, P).transpose(1, 3, 0, 2).reshape(FT // 7, P, 28)
    at = np.cumsum([0, 512, 512, 512, 256, 64, 64, 512, 64, 8, 256, 256, 256, 4, 1024])
    feats, toks, narrow = [], [], []
    for l in range(DEPTH_2):
        dq, dk, dv, sq, sk, sv, iq, ik, iw, fq, fk, fv, ff, gate = [
            a["w_in_2"][l][:, at[n]:at[n + 1]] for n in range(14)]
        feats.append(_feature_tiles(np.concatenate([sq, sk, sk, iq, ik, ik, fq, fk,
                                                      gate, dq, dk], 1)))
        toks.append(np.concatenate([sv, iw, fv, dv], 1))
        narrow.append(_narrow_tile(ff))
    d["w2_feat"], d["w2_tok"], d["w2_ff"] = np.stack(feats), np.stack(toks), np.stack(narrow)
    for n in ("b_f", "lam_q1", "lam_k1", "lam_q2", "lam_k2", "g_subln", "w_out", "ln_g", "ln_b"):
        d[n + "_2"] = a[n + "_2"]
    init = [0.8 - 0.6 * math.exp(-0.3 * l) for l in range(DEPTH_2)]
    d["lam_init"] = np.array([[i, 1.0 - i] for i in init], np.float32)
    return {n: np.ascontiguousarray(v) for n, v in d.items()}


def kernel(**inputs):
    import concourse.bacc as _bacc
    from concourse.bass_utils import run_bass_kernel_spmd as _run

    nc = _bacc.Bacc("TRN2", target_bir_lowering=False, num_devices=1)
    arrays = {f"in_{n}": v for n, v in layout(inputs).items()}
    d = {n[3:]: nc.dram_tensor(n, v.shape, mybir.dt.from_np(v.dtype), kind="ExternalInput").ap()
         for n, v in arrays.items()}
    out = nc.dram_tensor("out_x", (S, D), FP32, kind="ExternalOutput").ap()
    build(nc, d, out)
    r = _run(nc, [arrays], core_ids=[0])
    return r.results[0]["out_x"].reshape(1, S, D)
```
